# Optimizing a Trainium2 kernel written in Bass

```python
import math
import jax, jax.numpy as jnp
from jax import lax
import numpy as np

D_MODEL = 1024
BATCH = 1
SEQ = 256
DEPTH = 1

HEAD_DIM = 128
N_HEADS = D_MODEL // HEAD_DIM
GDN_HEADS = N_HEADS // 2
NSA_HEADS = N_HEADS - GDN_HEADS
GDN_WIDTH = GDN_HEADS * HEAD_DIM
NSA_WIDTH = NSA_HEADS * HEAD_DIM
GDN_CONV = 4
GDN_CHUNK = 64
CMP_BLOCK = 32
CMP_STRIDE = 16
SEL_BLOCK = 64
N_SELECT = 16
WINDOW = 512
Q_BLOCK = 128
D_FF = 2816
FFN_CONV = 3
N_GATES = 3
IN_SPLITS = (GDN_WIDTH, GDN_WIDTH, GDN_WIDTH, GDN_WIDTH, GDN_HEADS, GDN_HEADS,
             NSA_WIDTH, HEAD_DIM, HEAD_DIM, HEAD_DIM, HEAD_DIM, HEAD_DIM, HEAD_DIM,
             N_GATES * NSA_HEADS)
N_IN = 4 * GDN_WIDTH + 2 * GDN_HEADS + NSA_WIDTH + 6 * HEAD_DIM + N_GATES * NSA_HEADS
EPS = 1e-6
NEG_INF = -1e30
FORCE_BONUS = 1e4


def rmsnorm(x, w):
    xf = x.astype(jnp.float32)
    y = xf * lax.rsqrt(jnp.mean(xf * xf, axis=-1, keepdims=True) + EPS)
    return (y * w.astype(jnp.float32)).astype(x.dtype)

def l2norm(x):
    xf = x.astype(jnp.float32)
    return xf * lax.rsqrt(jnp.sum(xf * xf, axis=-1, keepdims=True) + EPS)

def causal_dwconv(x, w, b=None):
    k = w.shape[0]
    y = lax.conv_general_dilated(x, w[:, None, :].astype(x.dtype), window_strides=(1,),
                                 padding=[(k - 1, 0)], dimension_numbers=('NWC', 'WIO', 'NWC'),
                                 feature_group_count=x.shape[-1])
    if b is not None:
        y = y + b
    return y

def masked_softmax(s, mask):
    p = jax.nn.softmax(jnp.where(mask, s, NEG_INF), axis=-1)
    return jnp.where(mask, p, 0.0)

def gated_delta_chunked(q, k, v, g, beta):
    B, S, H, dk = q.shape
    dv = v.shape[-1]
    n = S // GDN_CHUNK
    f32 = jnp.float32

    def to_chunks(t):
        t = t.astype(f32).reshape((B, n, GDN_CHUNK) + t.shape[2:])
        return jnp.moveaxis(t, 3, 1)

    q, k, v, g, beta = (to_chunks(t) for t in (q, k, v, g, beta))
    q = q * (dk ** -0.5)
    gc = jnp.cumsum(g, axis=-1)
    idx = jnp.arange(GDN_CHUNK)
    incl = idx[:, None] >= idx[None, :]
    strict = idx[:, None] > idx[None, :]
    decay = jnp.exp(jnp.where(incl, gc[..., :, None] - gc[..., None, :], NEG_INF))
    k_beta = k * beta[..., None]
    a_mat = jnp.where(strict, jnp.einsum('bhncd,bhnsd->bhncs', k_beta, k) * decay, 0.0)
    eye = jnp.eye(GDN_CHUNK, dtype=f32)
    t_mat = lax.linalg.triangular_solve(eye + a_mat, jnp.broadcast_to(eye, a_mat.shape),
                                        left_side=True, lower=True, unit_diagonal=True)
    u = t_mat @ (v * beta[..., None])
    w = t_mat @ (k_beta * jnp.exp(gc)[..., None])
    attn_intra = jnp.where(incl, jnp.einsum('bhncd,bhnsd->bhncs', q, k) * decay, 0.0)
    q_dec = q * jnp.exp(gc)[..., None]
    k_dec = k * jnp.exp(gc[..., -1:] - gc)[..., None]
    g_last = jnp.exp(gc[..., -1])

    def step(state, inp):
        u_i, w_i, qd_i, kd_i, a_i, gl_i = inp
        v_new = u_i - w_i @ state
        o_i = qd_i @ state + a_i @ v_new
        state = state * gl_i[..., None, None] + jnp.swapaxes(kd_i, -1, -2) @ v_new
        return state, o_i

    xs = tuple(jnp.moveaxis(t, 2, 0) for t in (u, w, q_dec, k_dec, attn_intra, g_last))
    state0 = jnp.zeros((B, H, dk, dv), f32)
    _, o = lax.scan(step, state0, xs)
    return jnp.transpose(o, (1, 0, 3, 2, 4)).reshape(B, S, H, dv)

def nsa_compress(kv, pos, w1, w2):
    B, S, D = kv.shape
    n_cmp = (S - CMP_BLOCK) // CMP_STRIDE + 1
    idx = jnp.arange(n_cmp)[:, None] * CMP_STRIDE + jnp.arange(CMP_BLOCK)[None, :]
    blocks = kv[:, idx] + pos
    hid = jax.nn.silu(blocks.reshape(B, n_cmp, CMP_BLOCK * D) @ w1)
    return hid @ w2

def nsa_attention(q, k_cmp, v_cmp, k_slc, v_slc, k_win, v_win, gates):
    f32 = jnp.float32
    q, k_cmp, v_cmp, k_slc, v_slc, k_win, v_win, gates = (
        t.astype(f32) for t in (q, k_cmp, v_cmp, k_slc, v_slc, k_win, v_win, gates))
    B, S, H, D = q.shape
    scale = D ** -0.5
    n_cmp = k_cmp.shape[1]
    n_sel = S // SEL_BLOCK
    n_pick = min(N_SELECT, n_sel)
    cs = jnp.arange(n_cmp) * CMP_STRIDE
    ss = jnp.arange(n_sel) * SEL_BLOCK
    ov = jnp.minimum(cs[:, None] + CMP_BLOCK, ss[None, :] + SEL_BLOCK) - jnp.maximum(cs[:, None], ss[None, :])
    overlap = jnp.clip(ov, 0, None).astype(f32) / CMP_BLOCK
    cmp_end = cs + CMP_BLOCK - 1
    k_blocks = k_slc.reshape(B, n_sel, SEL_BLOCK, D)
    v_blocks = v_slc.reshape(B, n_sel, SEL_BLOCK, D)
    k_win_pad = jnp.pad(k_win, ((0, 0), (WINDOW, 0), (0, 0)))
    v_win_pad = jnp.pad(v_win, ((0, 0), (WINDOW, 0), (0, 0)))
    blk = jnp.arange(n_sel)
    gather = jax.vmap(lambda kb, ib: kb[ib])

    def block(qi):
        t0 = qi * Q_BLOCK
        qb = lax.dynamic_slice_in_dim(q, t0, Q_BLOCK, axis=1)
        gb = lax.dynamic_slice_in_dim(gates, t0, Q_BLOCK, axis=1)
        t = t0 + jnp.arange(Q_BLOCK)
        mask_c = cmp_end[None, :] <= t[:, None]
        s_c = jnp.einsum('bqhd,bkd->bqhk', qb, k_cmp) * scale
        p_c = masked_softmax(s_c, mask_c[None, :, None, :])
        o_c = jnp.einsum('bqhk,bkd->bqhd', p_c, v_cmp)
        imp = jnp.einsum('bqhk,kj->bqj', p_c, overlap)
        cur = t // SEL_BLOCK
        valid = blk[None, :] <= cur[:, None]
        forced = (blk[None, :] == 0) | (blk[None, :] == cur[:, None]) | (blk[None, :] == cur[:, None] - 1)
        imp = jnp.where(valid[None], imp + jnp.where(forced, FORCE_BONUS, 0.0)[None], NEG_INF)
        _, sel = lax.top_k(imp, n_pick)
        ks = gather(k_blocks, sel).reshape(B, Q_BLOCK, n_pick * SEL_BLOCK, D)
        vs = gather(v_blocks, sel).reshape(B, Q_BLOCK, n_pick * SEL_BLOCK, D)
        pos_s = (sel[..., None] * SEL_BLOCK + jnp.arange(SEL_BLOCK)).reshape(B, Q_BLOCK, n_pick * SEL_BLOCK)
        mask_s = pos_s <= t[None, :, None]
        s_s = jnp.einsum('bqhd,bqkd->bqhk', qb, ks) * scale
        p_s = masked_softmax(s_s, mask_s[:, :, None, :])
        o_s = jnp.einsum('bqhk,bqkd->bqhd', p_s, vs)
        kw = lax.dynamic_slice_in_dim(k_win_pad, t0, Q_BLOCK + WINDOW, axis=1)
        vw = lax.dynamic_slice_in_dim(v_win_pad, t0, Q_BLOCK + WINDOW, axis=1)
        pos_w = t0 - WINDOW + jnp.arange(Q_BLOCK + WINDOW)
        mask_w = (pos_w[None, :] <= t[:, None]) & (pos_w[None, :] > t[:, None] - WINDOW) & (pos_w[None, :] >= 0)
        s_w = jnp.einsum('bqhd,bkd->bqhk', qb, kw) * scale
        p_w = masked_softmax(s_w, mask_w[None, :, None, :])
        o_w = jnp.einsum('bqhk,bkd->bqhd', p_w, vw)
        return gb[..., 0:1] * o_c + gb[..., 1:2] * o_s + gb[..., 2:3] * o_w

    out = lax.map(block, jnp.arange(S // Q_BLOCK))
    return jnp.moveaxis(out, 0, 1).reshape(B, S, H, D)

def hybrid_layer(x, c, ada_w, ada_b, norm1_w, w_in, gdn_conv_w, gdn_A_log, gdn_dt_bias,
                 gdn_out_norm_w, nsa_q_norm_w, nsa_k_norm_cmp, nsa_k_norm_slc, nsa_k_norm_win,
                 cmp_k_pos, cmp_k_w1, cmp_k_w2, cmp_v_pos, cmp_v_w1, cmp_v_w2, w_out,
                 norm2_w, ffn_w_up, ffn_conv_w, ffn_conv_b, ffn_w_down):
    f32 = jnp.float32
    B, S, _ = x.shape
    mod = jax.nn.silu(c) @ ada_w + ada_b
    shift1, scale1, gate1, shift2, scale2, gate2 = jnp.split(mod[:, None, :], 6, axis=-1)

    h = rmsnorm(x, norm1_w) * (1 + scale1) + shift1
    proj = h @ w_in
    offsets = np.cumsum(IN_SPLITS)[:-1].tolist()
    (gq, gk, gv, gz, ga, gbeta, nq, kc, vc, ksl, vsl, kwn, vwn, ng) = jnp.split(proj, offsets, axis=-1)

    qkv = jax.nn.silu(causal_dwconv(jnp.concatenate([gq, gk, gv], axis=-1), gdn_conv_w))
    gq, gk, gv = jnp.split(qkv, 3, axis=-1)
    hd = (B, S, GDN_HEADS, HEAD_DIM)
    q_g = l2norm(gq.reshape(hd))
    k_g = l2norm(gk.reshape(hd))
    v_g = gv.reshape(hd)
    beta = jax.nn.sigmoid(gbeta.astype(f32))
    log_decay = -jnp.exp(gdn_A_log.astype(f32)) * jax.nn.softplus(ga.astype(f32) + gdn_dt_bias.astype(f32))
    o_g = gated_delta_chunked(q_g, k_g, v_g, log_decay, beta)
    o_g = rmsnorm(o_g, gdn_out_norm_w) * jax.nn.silu(gz.reshape(hd).astype(f32))

    q_n = rmsnorm(nq.reshape(B, S, NSA_HEADS, HEAD_DIM), nsa_q_norm_w)
    k_cmp = rmsnorm(nsa_compress(kc, cmp_k_pos, cmp_k_w1, cmp_k_w2), nsa_k_norm_cmp)
    v_cmp = nsa_compress(vc, cmp_v_pos, cmp_v_w1, cmp_v_w2)
    k_slc = rmsnorm(ksl, nsa_k_norm_slc)
    k_win = rmsnorm(kwn, nsa_k_norm_win)
    gates = jax.nn.sigmoid(ng.reshape(B, S, NSA_HEADS, N_GATES))
    o_n = nsa_attention(q_n, k_cmp, v_cmp, k_slc, vsl, k_win, vwn, gates)

    mixed = jnp.concatenate([o_g.reshape(B, S, GDN_WIDTH), o_n.reshape(B, S, NSA_WIDTH)], axis=-1)
    x = x + gate1 * (mixed.astype(x.dtype) @ w_out)

    h2 = rmsnorm(x, norm2_w) * (1 + scale2) + shift2
    up = causal_dwconv(h2 @ ffn_w_up, ffn_conv_w, ffn_conv_b)
    a, b = jnp.split(up, 2, axis=-1)
    x = x + gate2 * ((jax.nn.silu(a) * b) @ ffn_w_down)
    return x

def first_inputs(seed: int = 0) -> dict:
    key = jax.random.key(seed)
    ks = jax.random.split(key, 32)
    f32 = jnp.float32
    L = DEPTH

    def nrm(k, shape, s):
        return jax.random.normal(k, shape, f32) * s

    def gain(k, n):
        return 1.0 + 0.02 * jax.random.normal(k, (L, n), f32)

    dt = jnp.exp(jax.random.uniform(ks[8], (L, GDN_HEADS), f32, math.log(1e-3), math.log(1e-1)))
    return {
        'x': nrm(ks[0], (BATCH, SEQ, D_MODEL), 1.0),
        'c': nrm(ks[1], (BATCH, D_MODEL), 1.0),
        'ada_w': nrm(ks[2], (L, D_MODEL, 6 * D_MODEL), 0.5 * D_MODEL ** -0.5),
        'ada_b': nrm(ks[3], (L, 6 * D_MODEL), 0.02),
        'norm1_w': gain(ks[4], D_MODEL),
        'w_in': nrm(ks[5], (L, D_MODEL, N_IN), D_MODEL ** -0.5),
        'gdn_conv_w': nrm(ks[6], (L, GDN_CONV, 3 * GDN_WIDTH), GDN_CONV ** -0.5),
        'gdn_A_log': jnp.log(jax.random.uniform(ks[7], (L, GDN_HEADS), f32, 1.0, 16.0)),
        'gdn_dt_bias': dt + jnp.log(-jnp.expm1(-dt)),
        'gdn_out_norm_w': gain(ks[9], HEAD_DIM),
        'nsa_q_norm_w': gain(ks[10], HEAD_DIM),
        'nsa_k_norm_cmp': gain(ks[11], HEAD_DIM),
        'nsa_k_norm_slc': gain(ks[12], HEAD_DIM),
        'nsa_k_norm_win': gain(ks[13], HEAD_DIM),
        'cmp_k_pos': nrm(ks[14], (L, CMP_BLOCK, HEAD_DIM), 0.02),
        'cmp_k_w1': nrm(ks[15], (L, CMP_BLOCK * HEAD_DIM, HEAD_DIM), (CMP_BLOCK * HEAD_DIM) ** -0.5),
        'cmp_k_w2': nrm(ks[16], (L, HEAD_DIM, HEAD_DIM), HEAD_DIM ** -0.5),
        'cmp_v_pos': nrm(ks[17], (L, CMP_BLOCK, HEAD_DIM), 0.02),
        'cmp_v_w1': nrm(ks[18], (L, CMP_BLOCK * HEAD_DIM, HEAD_DIM), (CMP_BLOCK * HEAD_DIM) ** -0.5),
        'cmp_v_w2': nrm(ks[19], (L, HEAD_DIM, HEAD_DIM), HEAD_DIM ** -0.5),
        'w_out': nrm(ks[20], (L, D_MODEL, D_MODEL), D_MODEL ** -0.5),
        'norm2_w': gain(ks[21], D_MODEL),
        'ffn_w_up': nrm(ks[22], (L, D_MODEL, 2 * D_FF), D_MODEL ** -0.5),
        'ffn_conv_w': nrm(ks[23], (L, FFN_CONV, 2 * D_FF), FFN_CONV ** -0.5),
        'ffn_conv_b': nrm(ks[24], (L, 2 * D_FF), 0.02),
        'ffn_w_down': nrm(ks[25], (L, D_FF, D_MODEL), D_FF ** -0.5),
    }

def first_block(x, c, ada_w, ada_b, norm1_w, w_in, gdn_conv_w, gdn_A_log, gdn_dt_bias,
              gdn_out_norm_w, nsa_q_norm_w, nsa_k_norm_cmp, nsa_k_norm_slc, nsa_k_norm_win,
              cmp_k_pos, cmp_k_w1, cmp_k_w2, cmp_v_pos, cmp_v_w1, cmp_v_w2, w_out,
              norm2_w, ffn_w_up, ffn_conv_w, ffn_conv_b, ffn_w_down):
    for l in range(DEPTH):
        x = hybrid_layer(x, c, ada_w[l], ada_b[l], norm1_w[l], w_in[l], gdn_conv_w[l], gdn_A_log[l],
                         gdn_dt_bias[l], gdn_out_norm_w[l], nsa_q_norm_w[l], nsa_k_norm_cmp[l],
                         nsa_k_norm_slc[l], nsa_k_norm_win[l], cmp_k_pos[l], cmp_k_w1[l], cmp_k_w2[l],
                         cmp_v_pos[l], cmp_v_w1[l], cmp_v_w2[l], w_out[l], norm2_w[l], ffn_w_up[l],
                         ffn_conv_w[l], ffn_conv_b[l], ffn_w_down[l])
    return x


RET_HEADS = 8
RET_QK_DIM = 64
RET_V_DIM = 128
RET_CHUNK = 128
ROPE_BASE = 10000.0

MOBA_HEADS = 8
MOBA_HEAD_DIM = 64
MOBA_BLOCK = 256
MOBA_TOPK = 3
MOBA_Q_CHUNK = 32

REL_BUCKETS = 32
REL_MAX_DIST = 2048

PEER_HEADS = 8
PEER_N_KEYS = 128
PEER_N_EXPERTS = PEER_N_KEYS * PEER_N_KEYS
PEER_QUERY_DIM = 256
PEER_TOPK = 16
PEER_TOKEN_CHUNK = 128

NORM_EPS = 1e-6
NEG_INF_2 = -1e30

RET_QK_W = RET_HEADS * RET_QK_DIM
RET_V_W = RET_HEADS * RET_V_DIM
MOBA_W = MOBA_HEADS * MOBA_HEAD_DIM
IN_SIZES = (RET_QK_W, RET_QK_W, RET_V_W, RET_V_W, MOBA_W, MOBA_W, MOBA_W, D_MODEL, D_MODEL)
IN_WIDTH = sum(IN_SIZES)


def rmsnorm_2(x, g):
    xf = x.astype(jnp.float32)
    y = xf * lax.rsqrt(jnp.mean(xf * xf, axis=-1, keepdims=True) + NORM_EPS)
    return (y * g.astype(jnp.float32)).astype(x.dtype)

def to_heads(t, n_heads):
    b, s, _ = t.shape
    return t.reshape(b, s, n_heads, -1).transpose(0, 2, 1, 3)

def from_heads(t):
    b, h, s, d = t.shape
    return t.transpose(0, 2, 1, 3).reshape(b, s, h * d)

def rotary(x, pos):
    half = x.shape[-1] // 2
    inv = ROPE_BASE ** (-jnp.arange(half, dtype=jnp.float32) / half)
    ang = pos.astype(jnp.float32)[:, None] * inv[None, :]
    cos, sin = jnp.cos(ang), jnp.sin(ang)
    x1, x2 = x[..., :half], x[..., half:]
    return jnp.concatenate([x1 * cos - x2 * sin, x1 * sin + x2 * cos], axis=-1).astype(x.dtype)

def retention(q, k, v):
    B, H, S, dk = q.shape
    dv = v.shape[-1]
    C = RET_CHUNK
    n = S // C
    log_g = jnp.log1p(-jnp.exp2(-5.0 - jnp.arange(H, dtype=jnp.float32)))
    idx = jnp.arange(C, dtype=jnp.float32)
    rel = idx[:, None] - idx[None, :]
    decay_in = jnp.where(rel[None] >= 0, jnp.exp(jnp.maximum(rel, 0.0)[None] * log_g[:, None, None]), 0.0)
    qc = q.reshape(B, H, n, C, dk)
    kc = k.reshape(B, H, n, C, dk)
    vc = v.reshape(B, H, n, C, dv)
    scores = jnp.einsum('bhnid,bhnjd->bhnij', qc, kc) * decay_in[None, :, None]
    o_in = jnp.einsum('bhnij,bhnje->bhnie', scores, vc)
    k_dec = kc * jnp.exp((C - 1 - idx)[None, :] * log_g[:, None])[None, :, None, :, None]
    kv = jnp.einsum('bhncd,bhnce->bhnde', k_dec, vc)
    chunk_decay = jnp.exp(C * log_g)[None, :, None, None]

    def step(state, kv_n):
        return state * chunk_decay + kv_n, state

    state0 = jnp.zeros((B, H, dk, dv), kv.dtype)
    _, prev = lax.scan(step, state0, jnp.moveaxis(kv, 2, 0))
    prev = jnp.moveaxis(prev, 0, 2)
    q_dec = jnp.exp((idx + 1.0)[None, :] * log_g[:, None])
    o_cross = jnp.einsum('bhncd,bhnde->bhnce', qc, prev) * q_dec[None, :, None, :, None]
    o = (o_in + o_cross).reshape(B, H, S, dv).astype(jnp.float32)
    mu = jnp.mean(o, axis=-1, keepdims=True)
    var = jnp.mean(jnp.square(o - mu), axis=-1, keepdims=True)
    return ((o - mu) * lax.rsqrt(var + NORM_EPS)).astype(q.dtype)

def head_rmsnorm(t, g):
    tf = t.astype(jnp.float32)
    y = tf * lax.rsqrt(jnp.mean(tf * tf, axis=-1, keepdims=True) + NORM_EPS)
    return (y * g.astype(jnp.float32)).astype(t.dtype)

def rel_bucket(dist):
    max_exact = REL_BUCKETS // 2
    n = jnp.maximum(dist, 0)
    nf = jnp.maximum(n, 1).astype(jnp.float32)
    large = max_exact + (jnp.log(nf / max_exact) / math.log(REL_MAX_DIST / max_exact)
                         * (REL_BUCKETS - max_exact)).astype(jnp.int32)
    large = jnp.minimum(large, REL_BUCKETS - 1)
    return jnp.where(n < max_exact, n, large)

def moba_attention(q, k, v, rel_bias):
    B, H, S, dh = q.shape
    L = MOBA_BLOCK
    n_blk = -(-S // L)
    s_pad = n_blk * L
    pad = ((0, 0), (0, 0), (0, s_pad - S), (0, 0))
    k_pad = jnp.pad(k, pad)
    v_pad = jnp.pad(v, pad)
    k_blocks = k_pad.reshape(B, H, n_blk, L, dh)
    v_blocks = v_pad.reshape(B, H, n_blk, L, dh)
    k_mean = jnp.mean(k_blocks.astype(jnp.float32), axis=3)
    n_sel = min(MOBA_TOPK, n_blk)
    Qc = MOBA_Q_CHUNK
    n_qc = S // Qc
    q_chunks = jnp.moveaxis(q.reshape(B, H, n_qc, Qc, dh), 2, 0)
    bias_hb = rel_bias.T.astype(jnp.float32)
    b_idx = jnp.arange(B)[:, None, None, None]
    h_idx = jnp.arange(H)[None, :, None, None]
    h_idx5 = jnp.arange(H)[None, :, None, None, None]
    offs = jnp.arange(L)
    blk_ids = jnp.arange(n_blk)

    def one_chunk(args):
        qc, c = args
        q_start = c * Qc
        blk = q_start // L
        qpos = q_start + jnp.arange(Qc)
        gate = jnp.einsum('bhqd,bhnd->bhqn', qc.astype(jnp.float32), k_mean)
        gate = jnp.where(blk_ids < blk, gate, NEG_INF_2)
        _, sel = lax.top_k(gate, n_sel)
        valid = sel < blk
        k_sel = k_blocks[b_idx, h_idx, sel]
        v_sel = v_blocks[b_idx, h_idx, sel]
        kpos_sel = sel[..., None] * L + offs
        bias_sel = bias_hb[h_idx5, rel_bucket(qpos[None, None, :, None, None] - kpos_sel)]
        logit_sel = jnp.einsum('bhqd,bhqnkd->bhqnk', qc, k_sel).astype(jnp.float32) + bias_sel
        logit_sel = jnp.where(valid[..., None], logit_sel, NEG_INF_2).reshape(B, H, Qc, n_sel * L)
        k_own = lax.dynamic_slice_in_dim(k_pad, blk * L, L, axis=2)
        v_own = lax.dynamic_slice_in_dim(v_pad, blk * L, L, axis=2)
        dist_own = qpos[:, None] - (blk * L + offs)[None, :]
        bias_own = bias_hb[:, rel_bucket(dist_own)]
        logit_own = jnp.einsum('bhqd,bhkd->bhqk', qc, k_own).astype(jnp.float32) + bias_own[None]
        logit_own = jnp.where(dist_own >= 0, logit_own, NEG_INF_2)
        p = jax.nn.softmax(jnp.concatenate([logit_sel, logit_own], axis=-1), axis=-1)
        p_sel = p[..., :n_sel * L].reshape(B, H, Qc, n_sel, L).astype(v.dtype)
        p_own = p[..., n_sel * L:].astype(v.dtype)
        return (jnp.einsum('bhqnk,bhqnkd->bhqd', p_sel, v_sel)
                + jnp.einsum('bhqk,bhkd->bhqd', p_own, v_own))

    out = lax.map(one_chunk, (q_chunks, jnp.arange(n_qc)))
    return jnp.moveaxis(out, 0, 2).reshape(B, H, S, dh)

def peer(h, w_q, sub_keys, u_tab, v_tab):
    B, S, D = h.shape
    T = B * S
    ht = h.reshape(T, D)
    half = PEER_QUERY_DIM // 2
    q = (ht @ w_q).reshape(T, PEER_HEADS, 2, half)
    s = jnp.einsum('thcd,hcnd->thcn', q, sub_keys).astype(jnp.float32)
    s1, i1 = lax.top_k(s[:, :, 0], PEER_TOPK)
    s2, i2 = lax.top_k(s[:, :, 1], PEER_TOPK)
    cand_s = (s1[..., :, None] + s2[..., None, :]).reshape(T, PEER_HEADS, PEER_TOPK * PEER_TOPK)
    cand_i = (i1[..., :, None] * PEER_N_KEYS + i2[..., None, :]).reshape(T, PEER_HEADS, PEER_TOPK * PEER_TOPK)
    top_s, pos = lax.top_k(cand_s, PEER_TOPK)
    experts = jnp.take_along_axis(cand_i, pos, axis=-1)
    gates = jax.nn.softmax(top_s, axis=-1).astype(h.dtype)
    Pc = PEER_TOKEN_CHUNK
    n_c = T // Pc

    def one_chunk(args):
        hc, ec, gc = args
        u = u_tab[ec]
        a = jax.nn.gelu(jnp.einsum('td,thkd->thk', hc, u), approximate=False)
        return jnp.einsum('thk,thkd->td', gc * a, v_tab[ec])

    out = lax.map(one_chunk, (ht.reshape(n_c, Pc, D),
                              experts.reshape(n_c, Pc, PEER_HEADS, PEER_TOPK),
                              gates.reshape(n_c, Pc, PEER_HEADS, PEER_TOPK)))
    return out.reshape(B, S, D)

def second_inputs(seed: int = 0) -> dict:
    key = jax.random.key(seed)
    ks = jax.random.split(key, 14)
    f32 = jnp.float32
    nrm = lambda k, shape, scale: jax.random.normal(k, shape, f32) * scale
    return {
        "x": nrm(ks[0], (BATCH, SEQ, D_MODEL), 1.0),
        "mix_norm_g": 1.0 + nrm(ks[1], (DEPTH, D_MODEL), 0.1),
        "w_in": nrm(ks[2], (DEPTH, D_MODEL, IN_WIDTH), D_MODEL ** -0.5),
        "ret_w_branch": nrm(ks[3], (DEPTH, RET_V_W, D_MODEL), RET_V_W ** -0.5),
        "moba_q_gain": 1.0 + nrm(ks[4], (DEPTH, MOBA_HEAD_DIM), 0.1),
        "moba_k_gain": 1.0 + nrm(ks[5], (DEPTH, MOBA_HEAD_DIM), 0.1),
        "moba_w_branch": nrm(ks[6], (DEPTH, MOBA_W, D_MODEL), MOBA_W ** -0.5),
        "rel_bias": nrm(ks[7], (REL_BUCKETS, MOBA_HEADS), 0.5),
        "w_out": nrm(ks[8], (DEPTH, D_MODEL, D_MODEL), D_MODEL ** -0.5),
        "ffn_norm_g": 1.0 + nrm(ks[9], (DEPTH, D_MODEL), 0.1),
        "peer_w_q": nrm(ks[10], (DEPTH, D_MODEL, PEER_HEADS * PEER_QUERY_DIM), D_MODEL ** -0.5),
        "peer_sub_keys": nrm(ks[11], (DEPTH, PEER_HEADS, 2, PEER_N_KEYS, PEER_QUERY_DIM // 2), (PEER_QUERY_DIM // 2) ** -0.5),
        "peer_u": nrm(ks[12], (DEPTH, PEER_N_EXPERTS, D_MODEL), D_MODEL ** -0.5),
        "peer_v": nrm(ks[13], (DEPTH, PEER_N_EXPERTS, D_MODEL), D_MODEL ** -0.5),
    }

def second_block(x, mix_norm_g, w_in, ret_w_branch, moba_q_gain, moba_k_gain, moba_w_branch,
              rel_bias, w_out, ffn_norm_g, peer_w_q, peer_sub_keys, peer_u, peer_v):
    B, S, D = x.shape
    pos = jnp.arange(S)
    offsets = tuple(int(o) for o in np.cumsum(IN_SIZES)[:-1])
    for l in range(DEPTH):
        h = rmsnorm_2(x, mix_norm_g[l])
        proj = h @ w_in[l]
        rq, rk, rv, rg, mq, mk, mv, ga, gb = jnp.split(proj, offsets, axis=-1)
        rq = rotary(to_heads(rq, RET_HEADS), pos)
        rk = rotary(to_heads(rk, RET_HEADS), pos) * (RET_QK_DIM ** -0.5)
        ret = retention(rq, rk, to_heads(rv, RET_HEADS))
        y_a = (from_heads(ret) * jax.nn.silu(rg)) @ ret_w_branch[l]
        mq = head_rmsnorm(to_heads(mq, MOBA_HEADS), moba_q_gain[l]) * (MOBA_HEAD_DIM ** -0.5)
        mk = head_rmsnorm(to_heads(mk, MOBA_HEADS), moba_k_gain[l])
        att = moba_attention(mq, mk, to_heads(mv, MOBA_HEADS), rel_bias)
        y_b = from_heads(att) @ moba_w_branch[l]
        merged = jax.nn.sigmoid(ga) * y_a + jax.nn.sigmoid(gb) * y_b
        x = x + merged @ w_out[l]
        h2 = rmsnorm_2(x, ffn_norm_g[l])
        x = x + peer(h2, peer_w_q[l], peer_sub_keys[l], peer_u[l], peer_v[l])
    return x


def setup_inputs(seed=0):
    out = dict(first_inputs(seed))
    for name, value in second_inputs(seed + 1).items():
        if name != "x":
            out[name + "_2"] = value
    return out


def reference(
    x, c, ada_w, ada_b, norm1_w, w_in, gdn_conv_w, gdn_A_log, gdn_dt_bias, gdn_out_norm_w,
    nsa_q_norm_w, nsa_k_norm_cmp, nsa_k_norm_slc, nsa_k_norm_win, cmp_k_pos, cmp_k_w1, cmp_k_w2,
    cmp_v_pos, cmp_v_w1, cmp_v_w2, w_out, norm2_w, ffn_w_up, ffn_conv_w, ffn_conv_b, ffn_w_down,
    mix_norm_g_2, w_in_2, ret_w_branch_2, moba_q_gain_2, moba_k_gain_2, moba_w_branch_2,
    rel_bias_2, w_out_2, ffn_norm_g_2, peer_w_q_2, peer_sub_keys_2, peer_u_2, peer_v_2,
):
    x = first_block(
        x, c, ada_w, ada_b, norm1_w, w_in, gdn_conv_w, gdn_A_log, gdn_dt_bias, gdn_out_norm_w,
        nsa_q_norm_w, nsa_k_norm_cmp, nsa_k_norm_slc, nsa_k_norm_win, cmp_k_pos, cmp_k_w1,
        cmp_k_w2, cmp_v_pos, cmp_v_w1, cmp_v_w2, w_out, norm2_w, ffn_w_up, ffn_conv_w,
        ffn_conv_b, ffn_w_down,
    )
    return second_block(
        x, mix_norm_g_2, w_in_2, ret_w_branch_2, moba_q_gain_2, moba_k_gain_2, moba_w_branch_2,
        rel_bias_2, w_out_2, ffn_norm_g_2, peer_w_q_2, peer_sub_keys_2, peer_u_2, peer_v_2,
    )


_drawn_inputs = setup_inputs


def setup_inputs(seed=0):
    import zlib

    import numpy as np

    out = dict(_drawn_inputs(seed))
    spreads = {}
    factors = {'norm1_w': 8.0,
     'gdn_out_norm_w': 8.0,
     'nsa_q_norm_w': 8.0,
     'nsa_k_norm_cmp': 8.0,
     'nsa_k_norm_slc': 8.0,
     'nsa_k_norm_win': 8.0,
     'cmp_k_pos': 8.0,
     'cmp_v_pos': 32.239,
     'norm2_w': 7.952,
     'ffn_conv_b': 8.0,
     'moba_q_gain_2': 6.047,
     'moba_k_gain_2': 4.644,
     'ffn_norm_g_2': 8.0,
     'peer_w_q_2': 4.085,
     'peer_sub_keys_2': 4.078,
     'peer_u_2': 4.521,
     'peer_v_2': 4.077,
     'rel_bias_2': 4.171}
    for name, (base, spread) in spreads.items():
        noise = np.random.default_rng([zlib.crc32(name.encode()), seed]).standard_normal(out[name].shape)
        drawn = base * np.exp(spread * noise) if base else spread * noise
        out[name] = __import__('jax').numpy.asarray(drawn.astype(out[name].dtype))
    for name, factor in factors.items():
        out[name] = (out[name] * factor).astype(out[name].dtype)
    return out
```

```python
import math
import numpy as np
import concourse.bass as bass
from concourse import mybir
from contextlib import ExitStack

P = 128
SEQ, D = 256, 1024
KC = D // P
TT = SEQ // P
HEAD = 128
EPS = 1e-6
NEG = -1e30
TILE = 1024
RING = 4
LEAD = 2

FF = 2816
FC = FF // P
GH = 4
NH = 4
CMP_BLOCK, CMP_STRIDE = 32, 16
N_CMP = (SEQ - CMP_BLOCK) // CMP_STRIDE + 1
CPAD = 16
LEVELS = 7

RH, RQK, RV = 8, 64, 128
MH, MD = 8, 64
BUCKETS, MAXDIST = 32, 2048
PH, NKEY, TOPK = 8, 128, 16
NPAIR = PH * TOPK
NEXP = NKEY * NKEY

C_GQ, C_GK, C_NQ, C_KS, C_KW, C_GV, C_GZ, C_KC, C_VC = 0, 4, 8, 12, 13, 14, 18, 22, 23
C_RQ, C_RK, C_RG, C_MQ, C_MK, C_GA, C_GB = 0, 4, 8, 16, 20, 24, 32

SEGMENTS = [("ada", 48), ("win", 24), ("tok", 2), ("cmp", 8), ("wout", 8), ("up", 2 * FC), ("down", FC),
            ("in2", 40), ("tok2", 12), ("retw", 8), ("mobw", 4), ("out2", 8), ("pq", 16), ("subk", 2),
            ("u", NKEY), ("v", NKEY)]
BASE, _at = {}, 0
for _name, _n in SEGMENTS:
    BASE[_name] = _at
    _at += _n
COUNT = dict(SEGMENTS)
TOTAL = _at


def build_program(nc, A, out):
    f32, f32r = mybir.dt.float32, mybir.dt.float32r
    u32 = mybir.dt.uint32
    ALU, ACT = mybir.AluOpType, mybir.ActivationFunctionType
    X = mybir.AxisListType.X
    add, sub, mul = ALU.add, ALU.subtract, ALU.mult

    ctx = ExitStack()
    with ctx:
        sems = {}

        def S(name):
            if name not in sems:
                sems[name] = ctx.enter_context(nc.semaphore(name))
            return sems[name]

        top = [-(-nc.sbuf_base // 32) * 32]

        def span(shape):
            return -(-4 * int(np.prod(shape[1:])) // 32) * 32

        def at(name, shape, dt, offset=None):
            size = span(shape)
            if offset is None:
                offset = top[0]
                top[0] = offset + size
            assert offset + size <= nc.sbuf_usable_end, (name, offset, size)
            return nc.alloc_sbuf_tensor_at(name, list(shape), dt, offset=offset)

        raw = at("raw", [P, RING, TILE], f32)
        whi = at("whi", [P, RING, TILE], f32r)
        wlo = at("wlo", [P, RING, TILE], f32r)
        raw_end = top[0]
        x = at("x", [P, KC, SEQ], f32)
        hhi = at("hhi", [P, KC, SEQ], f32r)
        hlo = at("hlo", [P, KC, SEQ], f32r)
        cst = at("cst", [P, 4 * P], f32)
        ident, ones, tri, iota = (cst[:, i * P:(i + 1) * P] for i in range(4))
        gains = at("gains", [P, 4, KC], f32)
        shifts = at("shifts", [P, 4, KC], f32)
        mod = at("mod", [P, 48], f32)
        PAIR0 = top[0]
        G0 = PAIR0 + 3 * SEQ * 4
        up_at = [G0]

        def big(name, shape, dt=f32, offset=None):
            if offset is None:
                offset = up_at[0]
                up_at[0] += span(shape)
            return at(name, shape, dt, offset)

        tmp = big("tmp", [P, KC, SEQ])
        rs = big("rs", [P, 14, SEQ])
        R1 = up_at[0]
        prm = big("prm", [P, 256])
        proj = big("proj", [P, 24, SEQ])
        vtok = big("vtok", [P, TT, 256])
        small = big("small", [P, TT, 20])
        wsm = big("wsm", [P, KC, 20])
        w2 = big("w2", [P, 2, P])
        lvl = big("lvl", [P, LEVELS, P])
        nmask = big("nmask", [P, P])
        cmask = big("cmask", [P, TT, CPAD + 1])
        chi = big("chi", [P, KC, 2], f32r)
        clo = big("clo", [P, KC, 2], f32r)
        csl = big("csl", [P, KC, 2])
        hid = big("hid", [P, 2, CPAD])
        kc = big("kc", [P, CPAD])
        sqc = big("sqc", [P, CPAD])
        rsc = big("rsc", [P, CPAD])
        vc = big("vc", [P, P])
        blk = big("blk", [P, 2, CMP_BLOCK, CPAD])
        B0 = up_at[0]
        bhi = big("bhi", [P, 2, CMP_BLOCK, CPAD], f32r)
        blo = big("blo", [P, 2, CMP_BLOCK, CPAD], f32r)
        gsm = big("gsm", [P, 96])
        gcB = big("gcB", [P, 8, P])
        Xs = big("Xs", [P, 8, P], offset=B0)
        wT = big("wT", [P, GH, P], offset=B0 + 4096)
        St = big("St", [P, GH, P], offset=B0 + 6144)
        kbT = big("kbT", [P, GH, SEQ])
        R2 = up_at[0]
        DT = big("DT", [P, 8, P])
        AT = big("AT", [P, 8, P])
        QT = big("QT", [P, 8, P])
        BT = big("BT", [P, 8, P])
        Tm = big("Tm", [P, 8, P])
        TTm = big("TTm", [P, 8, P])
        vb = big("vb", [P, 8, P])
        kw = big("kw", [P, 8, P])
        U = big("U", [P, 8, P])
        qd = big("qd", [P, GH, P])
        eg = big("eg", [P, GH, P])
        og = big("og", [P, GH, SEQ])
        ogsq = big("ogsq", [P, 1024])
        cv = big("cv", [P, 12, SEQ], offset=R2)
        sq = big("sq", [P, 14 * SEQ], offset=R2)
        sp_ = big("sp_", [P, NH, 512], offset=R2)
        spc = big("spc", [P, NH, CPAD], offset=R2 + 8192)
        nst = big("nst", [P, 48], offset=R2 + 8448)
        pt = big("pt", [P, 2, 512], offset=R2 + 8704)
        ptc = big("ptc", [P, 2, P], offset=R2 + 12800)
        ahi = big("ahi", [P, FC, SEQ], f32r, offset=R1)
        alo = big("alo", [P, FC, SEQ], f32r, offset=R1 + FC * 1024)
        o_ = R1 + 2 * FC * 1024
        upc = big("upc", [P, 2 * FC, 4], offset=o_)
        uc = big("uc", [P, 4, SEQ], offset=o_ + 1024)
        upp = big("upp", [P, 2, SEQ], offset=o_ + 5120)
        zz = big("zz", [P, 512], f32r, offset=o_ + 7168)
        zf = big("zf", [P, 512], offset=o_ + 9216)
        up_at[0] = R1
        proj2 = big("proj2", [P, 40, SEQ])
        vtok2 = big("vtok2", [P, TT, 1536])
        bias = big("bias", [P, TT, MH, SEQ])
        dec = big("dec", [P, RH, SEQ])
        rot = big("rot", [P, 3 * P + 2 * SEQ])
        relhot = big("relhot", [BUCKETS, 2 * SEQ])
        relb = big("relb", [BUCKETS, MH])
        line = big("line", [MH, 2 * SEQ])
        prm2 = big("prm2", [P, 16])
        ro = big("ro", [P, RH, SEQ])
        ya = big("ya", [P, KC, SEQ])
        mbhi = big("mbhi", [P, 4, SEQ], f32r)
        mblo = big("mblo", [P, 4, SEQ], f32r)
        mst = big("mst", [P, 32])
        vmean = big("vmean", [P, 16])
        RS = 8192 + G0
        pr = big("pr", [P, 2, 384], offset=RS + 2048)
        sp2 = big("sp2", [P, 4, SEQ], offset=RS + 1024 * 6)
        pt2 = big("pt2", [P, 2, SEQ], offset=RS + 1024 * 11)
        pair = at("pair", [P, 3, SEQ], f32, PAIR0)
        G = at("G", [P, NKEY, SEQ], f32, G0)
        qhi = at("qhi", [P, 16, SEQ], f32r, G0 + 48 * 1024)
        qlo = at("qlo", [P, 16, SEQ], f32r, G0 + 64 * 1024)
        sc = at("sc", [P, TT * PH * 2, NKEY], f32, G0 + 96 * 1024)
        o_ = G0 + 112 * 1024
        top8 = at("top8", [P, 2, TOPK], f32, o_)
        tix = at("tix", [P, 2, TOPK], u32, o_ + 128)
        tixf = at("tixf", [P, 2, TOPK], f32, o_ + 256)
        cand = at("cand", [P, TOPK, TOPK], f32, o_ + 512)
        ctop = at("ctop", [P, TT, PH, TOPK], f32, o_ + 1536)
        cix = at("cix", [P, TOPK], u32, o_ + 2560)
        cab = at("cab", [P, 2, TOPK], f32, o_ + 2624)
        cau = at("cau", [P, 2, TOPK], u32, o_ + 2752)
        eq = at("eq", [P, TOPK, TOPK], f32, o_ + 3072)
        pidx = at("pidx", [P, 2, TT, PH, TOPK], f32, o_ + 4096)
        gden = at("gden", [P, 2, TT * PH], f32, o_ + 6144)
        cand2 = at("cand2", [P, TOPK * TOPK], f32, o_ + 7168)
        scu = at("scu", [P, 2, NKEY], f32, o_ + 8704)
        cbu = at("cbu", [P, TOPK], f32, o_ + 9728)
        scr = at("scr", [P, NKEY], f32, o_ + 8192)
        hh0 = raw_end + KC * SEQ * 4
        e1 = at("e1", [P, 2, 4, P], f32, hh0)
        e2 = at("e2", [P, 2, 4, P], f32, hh0 + 4096)
        mhi = at("mhi", [P, RING, SEQ], f32r, hh0 + 8192)
        mlo = at("mlo", [P, RING, SEQ], f32r, hh0 + 12288)
        y = at("y", [P, TT, D], f32, hh0)

        ps = ctx.enter_context(nc.psum_tensor("ps", [P, 8, 512], f32))

        def bank(b, n=1):
            return ps[:, b:b + n, :].rearrange("p b c -> p (b c)")

        w_loaded = [S(f"w_loaded{s}") for s in range(RING)]
        hi_made, lo_made, tile_used = S("hi_made"), S("lo_made"), S("tile_used")

        def wait(eng, sem, value):
            if not isinstance(value, int) or value > 0:
                eng.wait_ge(sem, value)

        def tiles(eng, name, body, start=0, stop=None, loop=True):
            n = COUNT[name] if stop is None else stop
            head = start + 4 if start == 0 else start
            tail = n - 4 if (name, n) == ("v", COUNT["v"]) else n
            m = (tail - head) // 4
            if m < 2 or not loop:
                m, head = 0, start
            for j in range(start, head):
                body(0, j)
            if m:
                with eng.Fori(0, m) as i:
                    for s in range(4):
                        body(i, head + s)
            for j in range(head + 4 * m, n):
                body(0, j)

        def pick(t, j):
            if isinstance(j, int):
                return t[:, j]
            return t[:, bass.ds(j, 1)].rearrange("p o t -> p (o t)")

        def col(t, j):
            return t[:, j:j + 1] if isinstance(j, int) else t[:, bass.ds(j, 1)]

        def load(sp, name):
            def body(i, j):
                g = BASE[name] + j
                wait(sp, lo_made, 4 * i + (g - (RING - 1)))
                src = A["w_" + name]
                src = src[4 * i + j] if isinstance(i, int) else src[bass.ds(4 * i + j, 1)].rearrange("o p c -> p (o c)")
                sp.dma_start(raw[:, g % RING, :], src).then_inc(w_loaded[g % RING], 16)
            return body

        def split_hi(act, g, i=0):
            if g < TOTAL:
                act.wait_ge(w_loaded[g % RING], 16 * i + 16 * (g // RING + 1))
                wait(act, tile_used, 4 * i + (g - (RING - 1)))
                act.activation(whi[:, g % RING, :], raw[:, g % RING, :], ACT.Copy).then_inc(hi_made, 1)

        def split_lo(dve, g, i=0):
            if g < TOTAL:
                dve.wait_ge(hi_made, 4 * i + (g + 1))
                dve.tensor_tensor(wlo[:, g % RING, :], raw[:, g % RING, :], whi[:, g % RING, :].bitcast(f32), sub).then_inc(lo_made, 1)

        def products(pe, g, o, cols, bh, bl, start, stop):
            wh, wl = whi[:, g % RING, cols], wlo[:, g % RING, cols]
            pe.matmul(o, wh, bh, start=start, stop=False, skip_group_check=True)
            pe.matmul(o, wh, bl, start=False, stop=False, skip_group_check=True)
            return pe.matmul(o, wl, bh, start=False, stop=stop, skip_group_check=True)

        def chunk_bank(g):
            return ps[:, 6 + g % 2, 0:SEQ]

        def segment_T(pe, name, bh, bl, kept, count0=0, nk=KC):
            def body(i, j):
                g, per = BASE[name] + j, KC // nk
                pe.wait_ge(lo_made, 4 * i + (g + 1))
                for u in range(per):
                    if per * j + u >= 2:
                        pe.wait_ge(S(kept), per * 4 * i + (count0 + per * j + u - 1))
                    for k in range(nk):
                        last = products(pe, g, chunk_bank(g * per + u), slice((u * nk + k) * P, (u * nk + k + 1) * P),
                                        bh[:, k, :], bl[:, k, :], k == 0, k == nk - 1)
                last.then_inc(tile_used, 1)
            return body

        block = ctx.enter_context(nc.Block())
        @block.sync
        def _(sp):
            sp.dma_start(cst[:, :], A["c_cst"]).then_inc(S("prm_in"), 16)
            sp.dma_start(prm[:, :], A["prm"]).then_inc(S("prm_in"), 16)
            sp.dma_start(x[:, :, :], A["xT"]).then_inc(S("x_in"), 16)
            for name, _ in SEGMENTS:
                tiles(sp, name, load(sp, name))
            sp.wait_ge(S("y_made"), TT)
            for t in range(TT):
                sp.dma_start(out[0, t * P:(t + 1) * P, :], y[:, t, :]).then_inc(S("stored"), 16)
            sp.wait_ge(S("stored"), 16 * TT)

        @block.gpsimd
        def _(pool):
            pool.dma_start(lvl[:, :, :], A["c_lvl"]).then_inc(S("mix1_in"), 16)
            pool.dma_start(nmask[:, :], A["c_nmask"]).then_inc(S("mix1_in"), 16)
            pool.dma_start(cmask[:, :, :], A["c_cmask"]).then_inc(S("mix1_in"), 16)
            pool.dma_start(wsm[:, :, :], A["wsm"]).then_inc(S("mix1_in"), 16)
            pool.dma_start(w2[:, :, :], A["w2"]).then_inc(S("mix1_in"), 16)
            pool.wait_ge(S("x_new"), KC)
            pool.dma_start(upc[:, :, :], A["upc"]).then_inc(S("up_in"), 16)
            pool.wait_ge(S("x_new"), 2 * KC)
            pool.dma_start(prm2[:, :], A["prm2"]).then_inc(S("prm2_in"), 16)
            for dst, src in ((rot[:, :], "c_rot"), (dec[:, :, :], "c_dec"), (relhot[:, :], "c_relhot"), (relb[:, :], "relb")):
                pool.dma_start(dst, A[src]).then_inc(S("mix2_in"), 16)
            pool.wait_ge(S("line_made"), 2)
            pool.dma_start(A["line"], line[:, :]).then_inc(S("line_out"), 16)
            pool.wait_ge(S("line_out"), 16)
            for h in range(MH):
                for t in range(TT):
                    pool.dma_start(bias[:, t, h, 0:(t + 1) * P],
                                   bass.AP(tensor=A["line"].tensor, offset=h * 2 * SEQ + (1 - t) * P,
                                           ap=[[1, P], [1, (t + 1) * P]])).then_inc(S("bias_in"), 16)

        @block.tensor
        def _(pe):
            def norm(k):
                pe.wait_ge(S("norm_squared"), k + 1)
                if k == 0:
                    pe.wait_ge(S("prm_in"), 32)
                for c in range(KC):
                    last = pe.matmul(ps[:, 0, 0:SEQ], ones, tmp[:, c, :], start=c == 0, stop=c == KC - 1)
                last.then_inc(S("norm_summed"), 1)

            norm(0)
            pe.wait_ge(S("c_lo"), 1)

            def ada(i, j):
                g = BASE["ada"] + j
                pe.wait_ge(lo_made, 4 * i + (g + 1))
                o = ps[:, 1, 2 * j:2 * j + 2] if isinstance(i, int) else ps[:, 1, bass.ds(8 * i + 2 * j, 2)]
                for k in range(KC):
                    last = products(pe, g, o, slice(k * P, (k + 1) * P), chi[:, k, :], clo[:, k, :], k == 0, k == KC - 1)
                last.then_inc(tile_used, 1)
            tiles(pe, "ada", ada)

            pe.wait_ge(S("h_lo"), 1)
            tiles(pe, "win", segment_T(pe, "win", hhi, hlo, "win_kept"))

            def tok(i, j):
                slot = (BASE["tok"] + j) % RING
                pe.wait_ge(lo_made, BASE["tok"] + j + 1)
                for t in range(TT):
                    for kk in range(4):
                        k, w = 4 * j + kk, slice(kk * 256, kk * 256 + 256)
                        s = slice(t * P, (t + 1) * P)
                        pe.matmul(ps[:, 4 + t, 0:256], hhi[:, k, s], whi[:, slot, w], start=k == 0, stop=False)
                        pe.matmul(ps[:, 4 + t, 0:256], hlo[:, k, s], whi[:, slot, w], start=False, stop=False)
                        last = pe.matmul(ps[:, 4 + t, 0:256], hhi[:, k, s], wlo[:, slot, w], start=False, stop=k == KC - 1)
                last.then_inc(tile_used, 1)
            tiles(pe, "tok", tok)
            pe.wait_ge(S("mix1_in"), 5 * 16)
            pe.wait_ge(S("h_made"), 1)
            for t in range(TT):
                for k in range(KC):
                    last = pe.matmul(ps[:, 3, 32 * t:32 * t + 20], tmp[:, k, t * P:(t + 1) * P], wsm[:, k, :], start=k == 0, stop=k == KC - 1)
            last.then_inc(S("small_made"), 1)
            pe.wait_ge(S("blk_lo"), 1)

            def cmp(i, j):
                g = BASE["cmp"] + j
                pe.wait_ge(lo_made, g + 1)
                kv = j // 4
                for k in range(8):
                    m = (j % 4) * 8 + k
                    last = products(pe, g, ps[:, kv, 0:CPAD], slice(k * P, (k + 1) * P), bhi[:, kv, m, :], blo[:, kv, m, :], m == 0, m == 31)
                last.then_inc(tile_used, 1)
            tiles(pe, "cmp", cmp)
            pe.wait_ge(S("hid_made"), 1)
            pe.matmul(ps[:, 2, 0:CPAD], w2[:, 0, :], hid[:, 0, :], start=True, stop=True)
            pe.matmul(ps[0:CPAD, 2, P:2 * P], hid[:, 1, :], w2[:, 1, :], start=True, stop=True).then_inc(S("cmp_made"), 1)
            pe.wait_ge(S("heads_squared"), 1)
            pe.wait_ge(S("cmp_squared"), 1)
            pe.wait_ge(S("vc_made"), 1)
            for b in range(7):
                pe.matmul(ps[:, b, :], ones, sq[:, b * 512:(b + 1) * 512], start=True, stop=True)
            pe.matmul(ps[:, 7, 0:CPAD], ones, sqc[:, :], start=True, stop=True).then_inc(S("heads_summed"), 1)

            pe.wait_ge(S("decay_made"), 1)
            for p in range(8):
                t, h = p // 4, p % 4
                pe.matmul(ps[:, p // 4, h * P:(h + 1) * P], gsm[:, p:p + 1].to_broadcast([P, P]), tri, start=True, stop=True)
            for t in range(TT):
                pe.matmul(ps[:, 4, 4 * t:4 * t + 4], tri, gsm[:, 4 * t:4 * t + 4], start=True, stop=True)
            for p in range(8):
                last = pe.matmul(ps[:, 2 + p // 4, (p % 4) * P:(p % 4 + 1) * P], gsm[:, 8 + p:9 + p].to_broadcast([P, P]), ident, start=True, stop=True)
            last.then_inc(S("sums_made"), 1)
            pe.wait_ge(S("kbT_made"), 1)

            def tt(p):
                return slice((p // 4) * P, (p // 4 + 1) * P)
            for p in range(8):
                h, b, c = p % 4, p // 4, slice((p % 4) * P, (p % 4 + 1) * P)
                pe.matmul(ps[:, b, c], proj[:, C_GK + h, tt(p)], kbT[:, h, tt(p)], start=True, stop=True)
                pe.matmul(ps[:, 2 + b, c], proj[:, C_GK + h, tt(p)], proj[:, C_GQ + h, tt(p)], start=True, stop=True)
            for p in range(8):
                h, b, c = p % 4, p // 4, slice((p % 4) * P, (p % 4 + 1) * P)
                pe.transpose(ps[:, 4 + b, c], proj[:, C_GK + h, tt(p)], ident)
                last = pe.transpose(ps[:, 6 + b, c], proj[:, C_GV + h, tt(p)], ident)
            last.then_inc(S("kk_made"), 1)
            pe.wait_ge(S("kv_scaled"), 1)
            for l in range(LEVELS):
                for b in range(2):
                    pe.wait_ge(S("lvl_masked"), 2 * l + b + 1)
                    if l:
                        pe.wait_ge(S("inv_updated"), 2 * (l - 1) + b + 1)
                    for p in range(4 * b, 4 * b + 4):
                        last = pe.matmul(ps[:, b, (p % 4) * P:(p % 4 + 1) * P], BT[:, p, :], Tm[:, p, :], start=True, stop=True)
                    last.then_inc(S("inv_x"), 1)
                for b in range(2):
                    pe.wait_ge(S("inv_xs"), 2 * l + b + 1)
                    for p in range(4 * b, 4 * b + 4):
                        c = slice((p % 4) * P, (p % 4 + 1) * P)
                        pe.matmul(ps[:, 2 + b, c], TTm[:, p, :], Xs[:, p, :], start=True, stop=True)
                        last = pe.matmul(ps[:, 4 + b, c], Xs[:, p, :], TTm[:, p, :], start=True, stop=True)
                    last.then_inc(S("inv_y"), 1)
            pe.wait_ge(S("inv_updated"), 2 * LEVELS)
            for p in range(8):
                c = slice((p % 4) * P, (p % 4 + 1) * P)
                pe.matmul(ps[:, p // 4, c], TTm[:, p, :], vb[:, p, :], start=True, stop=True)
            for h in range(GH):
                last = pe.matmul(ps[:, 2, h * P:(h + 1) * P], kw[:, 4 + h, :], TTm[:, 4 + h, :], start=True, stop=True)
            last.then_inc(S("uw_made"), 1)
            pe.wait_ge(S("uw_kept"), 1)
            for h in range(GH):
                last = pe.matmul(ps[:, 3, h * P:(h + 1) * P], kw[:, h, :], U[:, h, :], start=True, stop=True)
            last.then_inc(S("state_made"), 1)
            pe.wait_ge(S("state_kept"), 1)
            for h in range(GH):
                last = pe.matmul(ps[:, 4, h * P:(h + 1) * P], wT[:, h, :], St[:, h, :], start=True, stop=True)
            last.then_inc(S("ws_made"), 1)
            for h in range(GH):
                pe.matmul(ps[:, 5, h * P:(h + 1) * P], U[:, h, :], QT[:, h, :], start=True, stop=True)
            pe.wait_ge(S("vnew_made"), 1)
            for h in range(GH):
                c = slice(h * P, (h + 1) * P)
                pe.matmul(ps[:, 6, c], St[:, h, :], qd[:, h, :], start=True, stop=False)
                last = pe.matmul(ps[:, 6, c], U[:, 4 + h, :], QT[:, 4 + h, :], start=False, stop=True)
            last.then_inc(S("og_made"), 1)
            pe.wait_ge(S("og_squared"), 1)
            for b in range(2):
                last = pe.matmul(ps[:, b, :], ones, ogsq[:, b * 512:(b + 1) * 512], start=True, stop=True)
            last.then_inc(S("og_summed"), 1)

            for t in range(TT):
                W = (t + 1) * P
                pe.wait_ge(S("og_lo"), 1)
                if t:
                    pe.wait_ge(S("mix_lo"), t)
                for h in range(NH):
                    q = proj[:, C_NQ + h, t * P:(t + 1) * P]
                    pe.matmul(ps[:, h, 0:W], q, proj[:, C_KS, 0:W], start=True, stop=True)
                    pe.matmul(ps[:, h, 256:256 + W], q, proj[:, C_KW, 0:W], start=True, stop=True)
                for h in range(NH):
                    last = pe.matmul(ps[:, 4, h * CPAD:(h + 1) * CPAD], proj[:, C_NQ + h, t * P:(t + 1) * P], kc[:, :], start=True, stop=True)
                last.then_inc(S("nsa_s"), 1)
                pe.wait_ge(S("nsa_p"), t + 1)
                for h in range(NH):
                    m = 4 * t + h
                    if m >= 2:
                        pe.wait_ge(S("nsa_pt"), m - 1)
                    z = 5 if m % 2 == 0 else 6
                    n = 0
                    for kk in range(2):
                        for u in range(t + 1):
                            pe.transpose(ps[:, z, n * P:(n + 1) * P], sp_[:, h, kk * 256 + u * P:kk * 256 + (u + 1) * P], ident)
                            n += 1
                    pe.transpose(ps[0:CPAD, 4, P + (m % 2) * P:P + (m % 2 + 1) * P], spc[:, h, :], ident).then_inc(S("nsa_tr"), 1)
                    pe.wait_ge(S("nsa_pt"), m + 1)
                    o = ps[:, 7, h * P:(h + 1) * P]
                    n = 0
                    for kk in range(2):
                        for u in range(t + 1):
                            pe.matmul(o, vtok[:, u, kk * P:(kk + 1) * P], pt[:, m % 2, n * P:(n + 1) * P], start=n == 0, stop=False)
                            n += 1
                    last = pe.matmul(o, vc[0:CPAD, :], ptc[0:CPAD, m % 2, :], start=False, stop=True)
                last.then_inc(S("nsa_o"), 1)

            pe.wait_ge(S("mix_lo"), TT)
            tiles(pe, "wout", segment_T(pe, "wout", hhi, hlo, "x_new"))
            norm(1)
            pe.wait_ge(S("h_lo"), 2)
            tiles(pe, "up", segment_T(pe, "up", hhi, hlo, "up_kept"))
            pe.wait_ge(S("zeros_made"), 1)
            for b in range(4):
                pe.matmul(ps[:, b, :], zz[:, 0:P], zz[:, :], start=True, stop=False, skip_group_check=True)
            pe.wait_ge(S("act_lo"), FC)

            def down(i, j):
                g = BASE["down"] + j
                pe.wait_ge(lo_made, 4 * i + (g + 1))
                for c in range(KC):
                    last = products(pe, g, ps[:, c // 2, (c % 2) * SEQ:(c % 2 + 1) * SEQ], slice(c * P, (c + 1) * P),
                                    pick(ahi, 4 * i + j), pick(alo, 4 * i + j), False, False)
                last.then_inc(tile_used, 1)
            tiles(pe, "down", down)

            norm(2)
            pe.wait_ge(S("mix2_in"), 4 * 16)
            pe.matmul(ps[0:MH, 5, :], relb[:, :], relhot[:, :], start=True, stop=True).then_inc(S("line_psum"), 1)
            pe.wait_ge(S("h_lo"), 3)
            tiles(pe, "in2", segment_T(pe, "in2", hhi, hlo, "in2_kept"))

            def tok2(i, j):
                g, n = BASE["tok2"] + j, j // 4
                pe.wait_ge(lo_made, g + 1)
                if j == 8:
                    pe.wait_ge(S("tok2_kept"), 2)
                for t in range(TT):
                    for kk in range(2):
                        k, w, s = 2 * (j % 4) + kk, slice(kk * 512, kk * 512 + 512), slice(t * P, (t + 1) * P)
                        o = ps[:, 2 * (n % 2) + t, :]
                        pe.matmul(o, hhi[:, k, s], whi[:, g % RING, w], start=k == 0, stop=False)
                        pe.matmul(o, hlo[:, k, s], whi[:, g % RING, w], start=False, stop=False)
                        last = pe.matmul(o, hhi[:, k, s], wlo[:, g % RING, w], start=False, stop=k == KC - 1)
                last.then_inc(tile_used, 1)
            tiles(pe, "tok2", tok2, loop=False)
            pe.wait_ge(S("in2_kept"), 40)
            pe.wait_ge(S("tok2_kept"), 6)
            for c in range(8):
                last = pe.matmul(ps[:, c // 2, (c % 2) * SEQ:(c % 2 + 1) * SEQ], rot[:, 0:P], proj2[:, C_RQ + c, :], start=True, stop=True)
            last.then_inc(S("rot_made"), 1)
            pe.wait_ge(S("rotated"), 1)
            pe.wait_ge(S("v_centred"), 1)

            def ret_s(h):
                r = slice(64 * (h % 2), 64 * (h % 2) + 64)
                if h >= 2:
                    pe.wait_ge(S("ret_p"), h - 1)
                pe.matmul(ps[:, h % 2, 0:SEQ], proj2[r, C_RK + h // 2, 0:P], proj2[r, C_RQ + h // 2, :], start=True, stop=True)
                pe.matmul(ps[:, h % 2, SEQ:SEQ + P], proj2[r, C_RK + h // 2, P:SEQ], proj2[r, C_RQ + h // 2, P:SEQ], start=True, stop=True).then_inc(S("ret_s"), 1)

            def ret_o(h):
                pe.wait_ge(S("ret_p"), h + 1)
                if h >= 2:
                    pe.wait_ge(S("ro_kept"), h - 1)
                c = slice(h * RV, (h + 1) * RV)
                pe.matmul(ps[:, 2 + h % 2, 0:P], vtok2[:, 0, c], pr[:, h % 2, 0:P], start=True, stop=True)
                pe.matmul(ps[:, 2 + h % 2, P:SEQ], vtok2[:, 0, c], pr[:, h % 2, P:SEQ], start=True, stop=False)
                pe.matmul(ps[:, 2 + h % 2, P:SEQ], vtok2[:, 1, c], pr[:, h % 2, SEQ:SEQ + P], start=False, stop=True).then_inc(S("ret_o"), 1)
            ret_s(0)
            for h in range(RH):
                if h + 1 < RH:
                    ret_s(h + 1)
                ret_o(h)
            pe.wait_ge(S("ro_squared"), 1)
            for b in range(4):
                last = pe.matmul(ps[:, b, :], ones, tmp[:, 2 * b:2 * b + 2, :].rearrange("p c t -> p (c t)"), start=True, stop=True)
            last.then_inc(S("ro_summed"), 1)
            pe.wait_ge(S("m_squared"), 1)
            pe.wait_ge(S("ro_var"), 1)
            for b in range(4):
                last = pe.matmul(ps[:, b, :], rot[:, P + 2 * SEQ:2 * P + 2 * SEQ], tmp[:, 2 * b:2 * b + 2, :].rearrange("p c t -> p (c t)"), start=True, stop=True)
            last.then_inc(S("m_summed"), 1)
            pe.wait_ge(S("mk_normed"), 1)
            pe.wait_ge(S("bias_in"), 16 * MH * TT)
            for n in range(4):
                t, hg = n // 2, n % 2
                W = (t + 1) * P
                if n >= 2:
                    pe.wait_ge(S("m_exp"), 4 * (n - 1))
                for h in range(4):
                    hh = 4 * hg + h
                    r = slice(64 * (hh % 2), 64 * (hh % 2) + 64)
                    o = ps[:, 2 * (n % 2) + h % 2, (h // 2) * SEQ:(h // 2) * SEQ + W]
                    pe.matmul(o, proj2[r, C_MQ + hh // 2, t * P:(t + 1) * P], proj2[r, C_MK + hh // 2, 0:W], start=True, stop=False)
                    last = pe.matmul(o, rot[:, 2 * P + 2 * SEQ:3 * P + 2 * SEQ], bias[:, t, hh, 0:W], start=False, stop=True)
                last.then_inc(S("m_s"), 1)
                pe.wait_ge(S("m_p"), n + 1)
                if n >= 2:
                    pe.wait_ge(S("m_lo"), n - 1)
                for h in range(4):
                    m, hh = 4 * n + h, 4 * hg + h
                    if m >= 2:
                        pe.wait_ge(S("m_pt"), m - 1)
                    for u in range(t + 1):
                        last = pe.transpose(ps[:, 4 + m % 2, u * P:(u + 1) * P], sp2[:, h, u * P:(u + 1) * P], ident)
                    last.then_inc(S("m_tr"), 1)
                    pe.wait_ge(S("m_pt"), m + 1)
                    r = 64 * (hh % 2)
                    for u in range(t + 1):
                        last = pe.matmul(ps[r:r + 64, 6 + n % 2, (h // 2) * P:(h // 2 + 1) * P], vtok2[:, u, 1024 + hh * MD:1024 + (hh + 1) * MD],
                                         pt2[:, m % 2, u * P:(u + 1) * P], start=u == 0, stop=u == t)
                last.then_inc(S("m_o"), 1)
            pe.wait_ge(S("m_lo"), 4)
            tiles(pe, "retw", segment_T(pe, "retw", hhi, hlo, "ya_kept"))
            pe.wait_ge(S("ya_kept"), KC)
            tiles(pe, "mobw", segment_T(pe, "mobw", mbhi, mblo, "yb_kept", nk=4))
            pe.wait_ge(S("merged_lo"), 1)
            tiles(pe, "out2", segment_T(pe, "out2", hhi, hlo, "x_new", count0=2 * KC))
            norm(3)
            pe.wait_ge(S("h_lo"), 4)

            tiles(pe, "pq", segment_T(pe, "pq", hhi, hlo, "q_lo"))
            pe.wait_ge(S("q_lo"), 16)

            def subk(i, j):
                g = BASE["subk"] + j
                pe.wait_ge(lo_made, g + 1)
                for t in range(TT):
                    for c in range(8):
                        s, w = slice(t * P, (t + 1) * P), slice(c * P, (c + 1) * P)
                        o = ps[:, 4 * j + 2 * t + c // 4, (c % 4) * P:(c % 4 + 1) * P]
                        pe.matmul(o, qhi[:, 8 * j + c, s], whi[:, g % RING, w], start=True, stop=False)
                        pe.matmul(o, qlo[:, 8 * j + c, s], whi[:, g % RING, w], start=False, stop=False)
                        last = pe.matmul(o, qhi[:, 8 * j + c, s], wlo[:, g % RING, w], start=False, stop=True)
                last.then_inc(tile_used, 1)
            tiles(pe, "subk", subk, loop=False)
            pe.wait_ge(S("scores_kept"), 2 * TT)
            pre = segment_T(pe, "u", hhi, hlo, "g_made")
            tiles(pe, "u", pre, 0, 84)
            pe.wait_ge(S("gates_made"), 1)
            for n in range(3):
                for t in range(TT):
                    s = ctop[:, t, :, :] if n == 2 else pidx[:, n, t, :, :]
                    last = pe.transpose(ps[:, 3 + n, t * P:(t + 1) * P], s.rearrange("p h k -> p (h k)"), ident)
            last.then_inc(S("pairs_turned"), 1)
            tiles(pe, "u", pre, 84, 128)

            def outer(i, q):
                pe.wait_ge(S("e_made"), 2 * i + (q + 1))
                wait(pe, S("outer_multiplied"), 2 * i + (q - 1))
                for a in range(4):
                    last = pe.matmul(ps[:, 4 + q % 2, a * P:(a + 1) * P], e1[:, q % 2, a, :], e2[:, q % 2, a, :], start=True, stop=True)
                last.then_inc(S("outer_made"), 1)
            outer(0, 0)
            outer(0, 1)
            with pe.Fori(0, SEQ // 8 - 1) as i:
                outer(i, 2)
                outer(i, 3)
            for t in range(TT):
                for c in range(KC):
                    pe.matmul(ps[:, 2 * t + c // 4, (c % 4) * P:(c % 4 + 1) * P], x[:, c, t * P:(t + 1) * P], ident, start=c % 4 == 0, stop=False, skip_group_check=True)

            def vals(i, j):
                g = BASE["v"] + j
                pe.wait_ge(lo_made, 4 * i + (g + 1))
                pe.wait_ge(S("mlo_made"), 4 * i + (j + 1))
                for t in range(TT):
                    for n in range(2):
                        o, s, w = ps[:, 2 * t + n, :], slice(t * P, (t + 1) * P), slice(n * 512, n * 512 + 512)
                        stop = isinstance(i, int) and j == NKEY - 1
                        pe.matmul(o, mhi[:, g % RING, s], whi[:, g % RING, w], start=False, stop=False, skip_group_check=True)
                        pe.matmul(o, mhi[:, g % RING, s], wlo[:, g % RING, w], start=False, stop=False, skip_group_check=True)
                        last = pe.matmul(o, mlo[:, g % RING, s], whi[:, g % RING, w], start=False, stop=stop, skip_group_check=True)
                last.then_inc(tile_used, 1)
            tiles(pe, "v", vals)

        @block.scalar
        def _(act):
            steps = [0]

            def link(ins):
                steps[0] += 1
                ins.then_inc(S("act_step"), 1)
                act.wait_ge(S("act_step"), steps[0])

            def hi_only(name):
                return lambda i, j: split_hi(act, BASE[name] + j + LEAD, i)

            def norm_square(k):
                act.activation(tmp[:, :, :], x[:, :, :], ACT.Square).then_inc(S("norm_squared"), 1)

            def norm_root(k):
                act.wait_ge(S("norm_var"), k + 1)
                act.activation(rs[:, 0, :], rs[:, 0, :], ACT.Sqrt).then_inc(S("norm_root"), 1)

            def norm_out(k):
                act.wait_ge(S("norm_scaled"), k + 1)
                for c in range(KC):
                    last = act.activation(tmp[:, c, :], tmp[:, c, :], ACT.Identity, bias=shifts[:, k, c:c + 1], scale=gains[:, k, c:c + 1])
                last.then_inc(S("h_made"), 1)
                act.wait_ge(S("h_made"), k + 1)
                act.activation(hhi[:, :, :], tmp[:, :, :], ACT.Copy).then_inc(S("h_hi"), 1)

            act.wait_ge(S("prm_in"), 32)
            act.wait_ge(S("pad_zero"), 1)
            act.activation(csl[:, :, 0:1], prm[:, 96:104].rearrange("p (k o) -> p k o", o=1), ACT.Silu).then_inc(S("c_silu"), 1)
            act.wait_ge(S("c_silu"), 1)
            act.activation(chi[:, :, :], csl[:, :, :], ACT.Copy).then_inc(S("c_hi"), 1)
            for g in range(LEAD):
                split_hi(act, g)
            act.wait_ge(S("x_in"), 16)
            norm_square(0)
            norm_root(0)
            tiles(act, "ada", hi_only("ada"))
            norm_out(0)

            def win(i, j):
                g = BASE["win"] + j
                split_hi(act, g + LEAD, i)
                act.wait_ge(tile_used, 4 * i + (g + 1))
                act.activation(pick(proj, 4 * i + j), chunk_bank(g), ACT.Copy).then_inc(S("win_kept"), 1)
            tiles(act, "win", win)
            tiles(act, "tok", hi_only("tok"))
            act.wait_ge(tile_used, BASE["tok"] + 2)
            for t in range(TT):
                act.activation(vtok[:, t, :], ps[:, 4 + t, 0:256], ACT.Copy).then_inc(S("vtok_made"), 1)
            act.wait_ge(S("small_made"), 1)
            act.activation(small[:, :, :], ps[:, 3, 0:64].rearrange("p (t c) -> p t c", t=2)[:, :, 0:20], ACT.Copy).then_inc(S("small_kept"), 1)
            act.wait_ge(S("blk_made"), 1)
            act.activation(bhi[:, :, :, :].rearrange("p a b c -> p (a b c)"), blk[:, :, :, :].rearrange("p a b c -> p (a b c)"), ACT.Copy).then_inc(S("blk_hi"), 1)
            tiles(act, "cmp", hi_only("cmp"))
            act.wait_ge(S("conv_made"), 1)
            act.wait_ge(tile_used, BASE["cmp"] + 8)
            act.activation(hid[:, :, :], ps[:, 0:2, 0:CPAD], ACT.Silu).then_inc(S("hid_made"), 1)
            act.activation(proj[:, 0:8, :], cv[:, 0:8, :], ACT.Silu).then_inc(S("conv_silu"), 1)
            act.activation(proj[:, C_GV:C_GV + 4, :], cv[:, 8:12, :], ACT.Silu).then_inc(S("conv_silu"), 1)
            act.activation(proj[:, C_GZ:C_GZ + 4, :], proj[:, C_GZ:C_GZ + 4, :], ACT.Silu).then_inc(S("conv_silu"), 1)
            act.wait_ge(S("conv_silu"), 3)
            act.activation(sq[:, :].rearrange("p (c t) -> p c t", t=SEQ), proj[:, 0:14, :], ACT.Square).then_inc(S("heads_squared"), 1)
            act.wait_ge(S("cmp_made"), 1)
            link(act.activation(kc[:, :], ps[:, 2, 0:CPAD], ACT.Copy))
            act.activation(sqc[:, :], kc[:, :], ACT.Square).then_inc(S("cmp_squared"), 1)
            act.activation(vc[0:CPAD, :], ps[0:CPAD, 2, P:2 * P], ACT.Copy).then_inc(S("vc_made"), 1)
            act.wait_ge(S("heads_var"), 1)
            act.activation(rs[:, :, :], rs[:, :, :], ACT.Sqrt).then_inc(S("heads_root"), 1)
            act.activation(rsc[:, :], rsc[:, :], ACT.Sqrt).then_inc(S("heads_root"), 1)
            act.wait_ge(S("z_made"), 1)
            link(act.activation(gsm[:, 16:24], gsm[:, 16:24], ACT.Exp, scale=-1.0))
            link(act.activation(gsm[:, 16:24], gsm[:, 16:24], ACT.Ln, bias=1.0))
            act.activation(gsm[:, 24:28], prm[:, 89:93], ACT.Exp)
            act.activation(small[:, :, 4:20], small[:, :, 4:20], ACT.Exp, scale=-1.0).then_inc(S("gates_exp"), 1)
            act.wait_ge(S("diff_made"), 1)
            act.activation(DT[:, :, :], DT[:, :, :], ACT.Exp).then_inc(S("DT_exp"), 1)
            act.wait_ge(S("sums_kept"), 1)
            act.activation(gsm[:, 40:48], gsm[:, 32:40], ACT.Exp)
            for h in range(GH):
                act.activation(gsm[:, 48 + h:49 + h], gsm[:, 32 + h:33 + h], ACT.Exp, bias=gcB[:, h, P - 1:P], scale=-1.0)
            act.activation(eg[:, :, :], gcB[:, 4:8, :], ACT.Exp).then_inc(S("eg_made"), 1)
            act.wait_ge(S("kk_made"), 1)
            act.activation(vb[:, :, :].rearrange("p a b -> p (a b)"), bank(6, 2), ACT.Copy).then_inc(S("vt_kept"), 1)
            for l in range(LEVELS):
                for b in range(2):
                    act.wait_ge(S("inv_x"), 2 * l + b + 1)
                    if l:
                        act.wait_ge(S("inv_y"), 2 * (l - 1) + b + 1)
                    act.activation(Xs[:, 4 * b:4 * b + 4, :].rearrange("p a b -> p (a b)"), bank(b), ACT.Copy).then_inc(S("inv_xs"), 1)
            act.wait_ge(S("uw_made"), 1)
            act.activation(wT[:, :, :].rearrange("p a b -> p (a b)"), bank(2), ACT.Copy)
            act.activation(U[:, :, :].rearrange("p a b -> p (a b)"), bank(0, 2), ACT.Copy).then_inc(S("uw_kept"), 1)
            act.wait_ge(S("state_made"), 1)
            act.activation(St[:, :, :].rearrange("p a b -> p (a b)"), bank(3), ACT.Copy).then_inc(S("state_kept"), 1)
            act.wait_ge(S("og_made"), 1)
            link(act.activation(og[:, :, 0:P], ps[:, 5, :].rearrange("p (h t) -> p h t", h=GH), ACT.Copy))
            link(act.activation(og[:, :, P:SEQ], ps[:, 6, :].rearrange("p (h t) -> p h t", h=GH), ACT.Copy))
            act.activation(ogsq[:, :], og[:, :, :].rearrange("p h t -> p (h t)"), ACT.Square).then_inc(S("og_squared"), 1)
            act.wait_ge(S("og_var"), 1)
            act.activation(rs[:, 0:4, :], rs[:, 0:4, :], ACT.Sqrt).then_inc(S("og_root"), 1)
            act.wait_ge(S("og_done"), 1)
            act.activation(hhi[:, 0:4, :], og[:, :, :], ACT.Copy).then_inc(S("og_hi"), 1)
            for t in range(TT):
                W = (t + 1) * P
                act.wait_ge(S("nsa_max"), t + 1)
                for h in range(NH):
                    for kk in range(2):
                        act.activation(sp_[:, h, kk * 256:kk * 256 + W], sp_[:, h, kk * 256:kk * 256 + W], ACT.Exp,
                                       bias=nst[:, 2 * h + kk:2 * h + kk + 1], accum_out=nst[:, 16 + 2 * h + kk:17 + 2 * h + kk])
                    act.activation(spc[:, h, :], spc[:, h, :], ACT.Exp, bias=nst[:, 8 + h:9 + h], accum_out=nst[:, 24 + h:25 + h]).then_inc(S("nsa_exp"), 1)
                for h in range(NH):
                    m = 4 * t + h
                    act.wait_ge(S("nsa_tr"), m + 1)
                    z = 5 if m % 2 == 0 else 6
                    act.activation(pt[:, m % 2, 0:2 * W], ps[:, z, 0:2 * W], ACT.Copy)
                    act.activation(ptc[0:CPAD, m % 2, :], ps[0:CPAD, 4, P + (m % 2) * P:P + (m % 2 + 1) * P], ACT.Copy).then_inc(S("nsa_pt"), 1)
                act.wait_ge(S("nsa_o"), t + 1)
                act.activation(hhi[:, 4:8, t * P:(t + 1) * P], ps[:, 7, :].rearrange("p (h q) -> p h q", h=NH), ACT.Copy).then_inc(S("mix_hi"), 1)
            act.wait_ge(S("mix_lo"), TT)
            tiles(act, "wout", hi_only("wout"))
            act.wait_ge(S("x_new"), KC)
            norm_square(1)
            norm_root(1)
            norm_out(1)

            def up(i, j):
                g, m = BASE["up"] + j, j // 2
                split_hi(act, g + LEAD, i)
                act.wait_ge(tile_used, 4 * i + (g + 1))
                wait(act, S("up_used"), 2 * i + (m - 1))
                w = pick(upc, 4 * i + j)
                act.activation(uc[:, j % 4, :], chunk_bank(g), ACT.Identity, bias=w[:, 3:4], scale=w[:, 2:3]).then_inc(S("up_scaled"), 1)
                if j % 2:
                    act.wait_ge(S("up_kept"), 4 * i + j)
                    act.activation(uc[:, j % 4 - 1, :], uc[:, j % 4 - 1, :], ACT.Silu).then_inc(S("up_silu"), 1)
                    if j > 1:
                        act_hi(i, m - 1)

            def act_hi(i, m):
                act.wait_ge(S("up_used"), 2 * i + (m + 1))
                act.activation(pick(ahi, 2 * i + m), upp[:, m % 2, :], ACT.Copy).then_inc(S("act_hi"), 1)

            act.wait_ge(S("up_in"), 16)
            act.wait_ge(S("zf_made"), 1)
            act.activation(zz[:, :], zf[:, :], ACT.Copy).then_inc(S("zeros_made"), 1)
            tiles(act, "up", up)
            act_hi(0, FC - 1)
            tiles(act, "down", hi_only("down"))
            act.wait_ge(S("x_new"), 2 * KC)
            norm_square(2)
            norm_root(2)
            norm_out(2)

            act.wait_ge(S("line_psum"), 1)
            act.activation(line[:, :], ps[0:MH, 5, :], ACT.Copy).then_inc(S("line_made"), 1)

            def in2(i, j):
                g = BASE["in2"] + j
                split_hi(act, g + LEAD, i)
                act.wait_ge(tile_used, 4 * i + (g + 1))
                act.activation(pick(proj2, 4 * i + j), chunk_bank(g), ACT.Copy).then_inc(S("in2_kept"), 1)
            tiles(act, "in2", in2)

            def tok2(i, j):
                split_hi(act, BASE["tok2"] + j + LEAD)
                if j % 4 == 3:
                    n = j // 4
                    act.wait_ge(tile_used, BASE["tok2"] + j + 1)
                    for t in range(TT):
                        act.activation(vtok2[:, t, n * 512:(n + 1) * 512], ps[:, 2 * (n % 2) + t, :], ACT.Copy).then_inc(S("tok2_kept"), 1)
            tiles(act, "tok2", tok2, loop=False)
            act.activation(proj2[:, C_RG:C_RG + 8, :], proj2[:, C_RG:C_RG + 8, :], ACT.Silu).then_inc(S("rg_silu"), 1)
            act.activation(proj2[:, C_GA:C_GA + 16, :], proj2[:, C_GA:C_GA + 16, :], ACT.Sigmoid).then_inc(S("ab_sig"), 1)
            for h in range(RH):
                act.wait_ge(S("ret_o"), h + 1)
                act.activation(ro[:, h, :], ps[:, 2 + h % 2, 0:SEQ], ACT.Copy).then_inc(S("ro_kept"), 1)
            act.wait_ge(S("ro_kept"), RH)
            act.activation(tmp[:, :, :], ro[:, :, :], ACT.Square).then_inc(S("ro_squared"), 1)
            act.wait_ge(S("ro_var"), 1)
            act.activation(rs[:, 0:8, :], rs[:, 0:8, :], ACT.Sqrt).then_inc(S("ro_root"), 1)
            act.wait_ge(S("ro_done"), 1)
            act.activation(hhi[:, :, :], ro[:, :, :], ACT.Copy).then_inc(S("ro_hi"), 1)
            act.activation(tmp[:, :, :], proj2[:, C_MQ:C_MQ + 8, :], ACT.Square).then_inc(S("m_squared"), 1)
            act.wait_ge(S("m_var"), 1)
            act.activation(rs[:, 0:8, :], rs[:, 0:8, :], ACT.Sqrt).then_inc(S("m_root"), 1)
            for n in range(4):
                t, hg = n // 2, n % 2
                W = (t + 1) * P
                act.wait_ge(S("m_max"), n + 1)
                if n:
                    act.wait_ge(S("m_tr"), 4 * n)
                for h in range(4):
                    act.activation(sp2[:, h, 0:W], ps[:, 2 * (n % 2) + h % 2, (h // 2) * SEQ:(h // 2) * SEQ + W], ACT.Exp, bias=mst[:, h:h + 1], accum_out=mst[:, 4 + h:5 + h]).then_inc(S("m_exp"), 1)
                for h in range(4):
                    m = 4 * n + h
                    act.wait_ge(S("m_tr"), m + 1)
                    act.activation(pt2[:, m % 2, 0:W], ps[:, 4 + m % 2, 0:W], ACT.Copy).then_inc(S("m_pt"), 1)
                act.wait_ge(S("m_o"), n + 1)
                act.activation(mbhi[:, 2 * hg:2 * hg + 2, t * P:(t + 1) * P], ps[:, 6 + n % 2, 0:2 * P].rearrange("p (c q) -> p c q", c=2), ACT.Copy).then_inc(S("m_hi"), 1)
            tiles(act, "retw", hi_only("retw"))
            tiles(act, "mobw", hi_only("mobw"))
            act.wait_ge(S("merged"), 1)
            act.activation(hhi[:, :, :], ya[:, :, :], ACT.Copy).then_inc(S("merged_hi"), 1)
            tiles(act, "out2", hi_only("out2"))
            act.wait_ge(S("x_new"), 3 * KC)
            norm_square(3)
            norm_root(3)
            norm_out(3)

            def pq(i, j):
                g = BASE["pq"] + j
                split_hi(act, g + LEAD, i)
                act.wait_ge(tile_used, 4 * i + (g + 1))
                act.activation(pick(qhi, 4 * i + j), chunk_bank(g), ACT.Copy).then_inc(S("q_hi"), 1)
            tiles(act, "pq", pq)

            def subk(i, j):
                split_hi(act, BASE["subk"] + j + LEAD)
                act.wait_ge(tile_used, BASE["subk"] + j + 1)
                for t in range(TT):
                    act.activation(sc[:, t * 16 + 8 * j:t * 16 + 8 * j + 8, :].rearrange("p a b -> p (a b)"), bank(4 * j + 2 * t, 2), ACT.Copy).then_inc(S("scores_kept"), 1)
            tiles(act, "subk", subk, loop=False)

            def exps(i, j):
                g = BASE["u"] + j
                split_hi(act, g + LEAD, i)
                act.wait_ge(tile_used, 4 * i + (g + 1))
                act.activation(pick(G, 4 * i + j), chunk_bank(g), ACT.Gelu).then_inc(S("g_made"), 1)
            tiles(act, "u", exps, 0, 80)
            act.wait_ge(S("gate_shifted"), 1)
            act.activation(ctop[:, :, :, :].rearrange("p a b c -> p (a b c)"), ctop[:, :, :, :].rearrange("p a b c -> p (a b c)"), ACT.Exp).then_inc(S("gate_exp"), 1)
            tiles(act, "u", exps, 80, 96)
            act.wait_ge(S("routed"), 1)
            tiles(act, "u", exps, 96, 128)
            act.wait_ge(S("outer_multiplied"), SEQ // 4)

            def m_hi(i, j):
                if j < NKEY:
                    act.activation(mhi[:, (BASE["v"] + j) % RING, :], pick(G, 4 * i + j), ACT.Copy).then_inc(S("mhi_made"), 1)
            for j in range(LEAD):
                m_hi(0, j)

            def vals(i, j):
                split_hi(act, BASE["v"] + j + LEAD, i)
                m_hi(i, j + LEAD)
            tiles(act, "v", vals)
            act.wait_ge(tile_used, TOTAL)
            for t in range(TT):
                act.activation(y[:, t, :], bank(2 * t, 2), ACT.Copy).then_inc(S("y_made"), 1)

        @block.vector
        def _(dve):
            steps = [0]

            def link(ins):
                steps[0] += 1
                ins.then_inc(S("dve_step"), 1)
                dve.wait_ge(S("dve_step"), steps[0])

            def lo_only(name):
                return lambda i, j: split_lo(dve, BASE[name] + j + LEAD, i)

            def over(t, n):
                return t.rearrange("p (o t) -> p o t", o=1).to_broadcast([P, n, t.shape[-1]])

            def flat(t):
                return t.rearrange("p a b -> p (a b)")

            def norm_stats(k):
                dve.wait_ge(S("norm_summed"), k + 1)
                dve.tensor_scalar(rs[:, 0, :], ps[:, 0, 0:SEQ], 1.0 / D, EPS, mul, add).then_inc(S("norm_var"), 1)
                dve.wait_ge(S("norm_root"), k + 1)
                link(dve.reciprocal(rs[:, 0, :], rs[:, 0, :]))

            def norm_rest(k):
                dve.tensor_tensor(tmp[:, :, :], x[:, :, :], over(rs[:, 0, :], KC), mul).then_inc(S("norm_scaled"), 1)
                dve.wait_ge(S("h_hi"), k + 1)
                dve.tensor_tensor(hlo[:, :, :], tmp[:, :, :], hhi[:, :, :].bitcast(f32), sub).then_inc(S("h_lo"), 1)

            dve.memset(shifts[:, :, :], 0.0)
            dve.memset(blk[:, :, :, :], 0.0)
            dve.memset(csl[:, :, :], 0.0).then_inc(S("pad_zero"), 1)
            dve.wait_ge(S("c_hi"), 1)
            dve.tensor_tensor(clo[:, :, :], csl[:, :, :], chi[:, :, :].bitcast(f32), sub).then_inc(S("c_lo"), 1)
            for g in range(LEAD):
                split_lo(dve, g)
            dve.wait_ge(S("x_in"), 16)
            norm_stats(0)
            tiles(dve, "ada", lo_only("ada"))
            dve.wait_ge(tile_used, BASE["ada"] + 48)
            link(dve.tensor_tensor(mod[:, :], ps[:, 1, 0:96].rearrange("p (c two) -> p c two", two=2)[:, :, 0], prm[:, 104:152], add))
            for k in range(2):
                dve.scalar_tensor_tensor(gains[:, k, :], mod[:, 24 * k + 8:24 * k + 16], 1.0, prm[:, 8 * k:8 * k + 8], add, mul)
                dve.tensor_copy(shifts[:, k, :], mod[:, 24 * k:24 * k + 8])
                dve.tensor_copy(gains[:, 2 + k, :], prm[:, 16 + 8 * k:24 + 8 * k])
            link(dve.memset(gsm[:, :], 0.0))
            norm_rest(0)
            tiles(dve, "win", lo_only("win"))
            tiles(dve, "tok", lo_only("tok"))
            dve.wait_ge(S("win_kept"), 24)
            for kv in range(2):
                src = proj[:, C_KC + kv, :]
                span = bass.AP(tensor=src.tensor, offset=src.offset, ap=[src.ap[0], [1, CMP_BLOCK], [CMP_STRIDE, N_CMP]])
                pos = prm[:, 152 + 32 * kv:184 + 32 * kv].rearrange("p (l o) -> p l o", o=1).to_broadcast([P, CMP_BLOCK, N_CMP])
                last = dve.tensor_tensor(blk[:, kv, :, 0:N_CMP], span, pos, add)
            last.then_inc(S("blk_made"), 1)
            dve.wait_ge(S("blk_hi"), 1)
            dve.tensor_tensor(flat(blo[:, :, :, :].rearrange("p a b c -> p a (b c)")), flat(blk[:, :, :, :].rearrange("p a b c -> p a (b c)")), flat(bhi[:, :, :, :].rearrange("p a b c -> p a (b c)")).bitcast(f32), sub).then_inc(S("blk_lo"), 1)
            tiles(dve, "cmp", lo_only("cmp"))
            for n in range(12):
                c = n if n < 8 else C_GV + n - 8
                last = dve.tensor_scalar(cv[:, n, :], proj[:, c, :], prm[:, 35 + 4 * n:36 + 4 * n], None, mul)
            link(last)
            for tap in range(1, 4):
                if tap > 1:
                    link(last)
                for n in range(12):
                    c = n if n < 8 else C_GV + n - 8
                    last = dve.scalar_tensor_tensor(cv[:, n, tap:SEQ], proj[:, c, 0:SEQ - tap], prm[:, 35 - tap + 4 * n:36 - tap + 4 * n], cv[:, n, tap:SEQ], mul, add)
            last.then_inc(S("conv_made"), 1)
            dve.wait_ge(S("small_kept"), 1)
            for t in range(TT):
                last = dve.tensor_tensor(gsm[:, 4 * t:4 * t + 4], small[:, t, 0:4], prm[:, 85:89], add)
            link(last)
            dve.tensor_scalar(gsm[:, 56:64], gsm[:, 0:8], 0.0, None, ALU.max)
            link(dve.tensor_scalar(gsm[:, 64:72], gsm[:, 0:8], -1.0, None, mul))
            dve.tensor_tensor(gsm[:, 16:24], gsm[:, 0:8], gsm[:, 64:72], ALU.max).then_inc(S("z_made"), 1)
            dve.wait_ge(S("heads_summed"), 1)
            dve.tensor_scalar(flat(rs[:, 0:8, :]), bank(0, 4), EPS, None, add)
            dve.tensor_scalar(flat(rs[:, 8:14, :]), bank(4, 3), 1.0 / HEAD, EPS, mul, add)
            dve.tensor_scalar(rsc[:, :], ps[:, 7, 0:CPAD], 1.0 / HEAD, EPS, mul, add).then_inc(S("heads_var"), 1)
            dve.wait_ge(S("heads_root"), 2)
            dve.reciprocal(rsc[:, :], rsc[:, :])
            link(dve.reciprocal(flat(rs[:, :, :]), flat(rs[:, :, :])))
            dve.wait_ge(S("conv_silu"), 3)
            root = float(HEAD) ** -0.5
            dve.scalar_tensor_tensor(flat(proj[:, 0:4, :]), flat(proj[:, 0:4, :]), root, flat(rs[:, 0:4, :]), mul, mul)
            dve.tensor_tensor(flat(proj[:, 4:8, :]), flat(proj[:, 4:8, :]), flat(rs[:, 4:8, :]), mul)
            link(dve.scalar_tensor_tensor(flat(proj[:, 8:12, :]), flat(proj[:, 8:12, :]), prm[:, 81:82], flat(rs[:, 8:12, :]), mul, mul))
            link(dve.tensor_scalar(flat(proj[:, 8:12, :]), flat(proj[:, 8:12, :]), root, None, mul))
            dve.scalar_tensor_tensor(proj[:, C_KS, :], proj[:, C_KS, :], prm[:, 83:84], rs[:, 12, :], mul, mul)
            dve.scalar_tensor_tensor(proj[:, C_KW, :], proj[:, C_KW, :], prm[:, 84:85], rs[:, 13, :], mul, mul)
            dve.scalar_tensor_tensor(kc[:, :], kc[:, :], prm[:, 82:83], rsc[:, :], mul, mul)
            dve.wait_ge(S("gates_exp"), 1)
            link(dve.tensor_scalar(small[:, :, 4:20], small[:, :, 4:20], 1.0, None, add))
            link(dve.reciprocal(small[:, :, 4:20], small[:, :, 4:20]))
            link(dve.tensor_tensor(gsm[:, 56:64], gsm[:, 56:64], gsm[:, 16:24], add))
            for t in range(TT):
                dve.scalar_tensor_tensor(gsm[:, 4 * t:4 * t + 4], gsm[:, 56 + 4 * t:60 + 4 * t], -1.0, gsm[:, 24:28], mul, mul)
                last = dve.tensor_copy(gsm[:, 8 + 4 * t:12 + 4 * t], small[:, t, 4:8])
            last.then_inc(S("decay_made"), 1)
            dve.wait_ge(S("sums_made"), 1)
            dve.tensor_copy(flat(gcB[:, :, :]), bank(0, 2))
            dve.tensor_copy(gsm[:, 32:40], ps[:, 4, 0:8]).then_inc(S("sums_kept"), 1)
            for t in range(TT):
                last = dve.tensor_tensor(kbT[:, :, t * P:(t + 1) * P], ps[:, 2 + t, :].rearrange("p (h c) -> p h c", h=GH), proj[:, 4:8, t * P:(t + 1) * P], mul)
            last.then_inc(S("kbT_made"), 1)
            dve.wait_ge(S("sums_kept"), 1)
            for p in range(8):
                last = dve.tensor_scalar(DT[:, p, :], gcB[:, p, :], gsm[:, 32 + p:33 + p], 0.0, sub, ALU.min)
            last.then_inc(S("diff_made"), 1)
            for t in (Tm, TTm):
                last = dve.tensor_copy(t[:, :, :], over(ident, 8))
            dve.wait_ge(S("DT_exp"), 1)
            link(dve.tensor_tensor(DT[:, :, :], DT[:, :, :], over(tri, 8), mul))
            dve.wait_ge(S("kk_made"), 1)
            dve.tensor_tensor(flat(QT[:, :, :]), flat(DT[:, :, :]), bank(2, 2), mul)
            link(dve.tensor_tensor(flat(AT[:, :, :]), flat(DT[:, :, :]), bank(0, 2), mul))

            def masked(l):
                for b in range(2):
                    if l:
                        dve.wait_ge(S("inv_x"), 2 * (l - 1) + b + 1)
                    dve.tensor_tensor(BT[:, 4 * b:4 * b + 4, :], AT[:, 4 * b:4 * b + 4, :], over(lvl[:, l, :], 4), mul).then_inc(S("lvl_masked"), 1)
            masked(0)
            dve.wait_ge(S("eg_made"), 1)
            link(dve.tensor_tensor(gsm[:, 52:56], gsm[:, 12:16], gsm[:, 44:48], mul))
            dve.tensor_tensor(qd[:, :, :], proj[:, 0:4, P:SEQ], eg[:, :, :], mul)
            dve.wait_ge(S("vt_kept"), 1)
            for p in range(8):
                h = p % 4
                dve.tensor_scalar(vb[:, p, :], vb[:, p, :], gsm[:, 8 + p:9 + p], None, mul)
                f = 52 + h if p >= 4 else 48 + h
                last = dve.tensor_scalar(kw[:, p, :], ps[:, 4 + p // 4, h * P:(h + 1) * P], gsm[:, f:f + 1], None, mul)
            last.then_inc(S("kv_scaled"), 1)
            for l in range(LEVELS):
                if l + 1 < LEVELS:
                    masked(l + 1)
                for b in range(2):
                    dve.wait_ge(S("inv_y"), 2 * l + b + 1)
                    o = slice(4 * b, 4 * b + 4)
                    dve.tensor_tensor(flat(Tm[:, o, :]), flat(Tm[:, o, :]), bank(2 + b), sub)
                    dve.tensor_tensor(flat(TTm[:, o, :]), flat(TTm[:, o, :]), bank(4 + b), sub).then_inc(S("inv_updated"), 1)
            dve.wait_ge(S("uw_kept"), 1)
            dve.wait_ge(S("ws_made"), 1)
            dve.tensor_tensor(flat(U[:, 4:8, :]), flat(U[:, 4:8, :]), bank(4), sub).then_inc(S("vnew_made"), 1)
            dve.wait_ge(S("og_summed"), 1)
            dve.tensor_scalar(flat(rs[:, 0:4, :]), bank(0, 2), 1.0 / HEAD, EPS, mul, add).then_inc(S("og_var"), 1)
            dve.wait_ge(S("og_root"), 1)
            link(dve.reciprocal(flat(rs[:, 0:4, :]), flat(rs[:, 0:4, :])))
            link(dve.scalar_tensor_tensor(flat(og[:, :, :]), flat(og[:, :, :]), prm[:, 80:81], flat(rs[:, 0:4, :]), mul, mul))
            dve.tensor_tensor(og[:, :, :], og[:, :, :], proj[:, C_GZ:C_GZ + 4, :], mul).then_inc(S("og_done"), 1)
            dve.wait_ge(S("og_hi"), 1)
            dve.tensor_tensor(hlo[:, 0:4, :], og[:, :, :], hhi[:, 0:4, :].bitcast(f32), sub).then_inc(S("og_lo"), 1)

            for t in range(TT):
                W = (t + 1) * P
                dve.wait_ge(S("nsa_s"), t + 1)
                for h in range(NH):
                    for kk in range(2):
                        a = kk * 256
                        if t:
                            dve.tensor_copy(sp_[:, h, a:a + P], ps[:, h, a:a + P])
                        dve.tensor_tensor(sp_[:, h, a + t * P:a + W], ps[:, h, a + t * P:a + W], nmask[:, :], add)
                link(dve.tensor_tensor(spc[:, :, :], ps[:, 4, 0:NH * CPAD].rearrange("p (h c) -> p h c", h=NH), over(cmask[:, t, 0:CPAD], NH), add))
                dve.tensor_reduce(nst[:, 0:8], sp_[:, :, :].rearrange("p h (b k) -> p (h b) k", b=2)[:, :, 0:W], X, ALU.max, negate=True)
                dve.tensor_reduce(nst[:, 8:12], spc[:, :, :], X, ALU.max, negate=True).then_inc(S("nsa_max"), 1)
                dve.wait_ge(S("nsa_exp"), NH * (t + 1))
                link(dve.reciprocal(nst[:, 32:44], nst[:, 16:28]))
                g = small[:, t, 8:20].rearrange("p (h b) -> p h b", b=3)
                dve.tensor_tensor(nst[:, 0:8].rearrange("p (h b) -> p h b", b=2), nst[:, 32:40].rearrange("p (h b) -> p h b", b=2), g[:, :, 1:3], mul)
                link(dve.scalar_tensor_tensor(nst[:, 8:12], nst[:, 40:44], cmask[:, t, CPAD:CPAD + 1], g[:, :, 0], mul, mul))
                for h in range(NH):
                    for kk in range(2):
                        a = kk * 256
                        dve.tensor_scalar(sp_[:, h, a:a + W], sp_[:, h, a:a + W], nst[:, 2 * h + kk:2 * h + kk + 1], None, mul)
                    last = dve.tensor_scalar(spc[:, h, :], spc[:, h, :], nst[:, 8 + h:9 + h], None, mul)
                last.then_inc(S("nsa_p"), 1)
                dve.wait_ge(S("mix_hi"), t + 1)
                dve.tensor_tensor(hlo[:, 4:8, t * P:(t + 1) * P], ps[:, 7, :].rearrange("p (h q) -> p h q", h=NH), hhi[:, 4:8, t * P:(t + 1) * P].bitcast(f32), sub).then_inc(S("mix_lo"), 1)

            def wout(i, j):
                g = BASE["wout"] + j
                split_lo(dve, g + LEAD)
                dve.wait_ge(tile_used, g + 1)
                dve.scalar_tensor_tensor(x[:, j, :], chunk_bank(g), mod[:, 16 + j:17 + j], x[:, j, :], mul, add).then_inc(S("x_new"), 1)
            tiles(dve, "wout", wout)
            dve.memset(zf[:, :], 0.0).then_inc(S("zf_made"), 1)
            norm_stats(1)
            norm_rest(1)

            def up(i, j):
                g, m, o = BASE["up"] + j, j // 2, uc[:, j % 4, :]
                split_lo(dve, g + LEAD, i)
                dve.wait_ge(S("up_scaled"), 4 * i + (j + 1))
                w = pick(upc, 4 * i + j)
                b = chunk_bank(g)
                dve.scalar_tensor_tensor(o[:, 1:SEQ], b[:, 0:SEQ - 1], w[:, 1:2], o[:, 1:SEQ], mul, add).then_inc(S("up_tap"), 1)
                dve.wait_ge(S("up_tap"), 4 * i + (j + 1))
                dve.scalar_tensor_tensor(o[:, 2:SEQ], b[:, 0:SEQ - 2], w[:, 0:1], o[:, 2:SEQ], mul, add).then_inc(S("up_kept"), 1)
                if j % 2:
                    dve.wait_ge(S("up_silu"), 2 * i + (m + 1))
                    dve.wait_ge(S("up_kept"), 4 * i + (j + 1))
                    dve.tensor_tensor(upp[:, m % 2, :], uc[:, j % 4 - 1, :], o, mul).then_inc(S("up_used"), 1)
                    if j > 1:
                        act_lo(i, m - 1)

            def act_lo(i, m):
                dve.wait_ge(S("act_hi"), 2 * i + (m + 1))
                dve.tensor_tensor(pick(alo, 2 * i + m), upp[:, m % 2, :], pick(ahi, 2 * i + m).bitcast(f32), sub).then_inc(S("act_lo"), 1)
            tiles(dve, "up", up)
            act_lo(0, FC - 1)
            tiles(dve, "down", lo_only("down"))
            dve.wait_ge(tile_used, BASE["down"] + FC)
            for c in range(KC):
                dve.scalar_tensor_tensor(x[:, c, :], ps[:, c // 2, (c % 2) * SEQ:(c % 2 + 1) * SEQ], mod[:, 40 + c:41 + c], x[:, c, :], mul, add).then_inc(S("x_new"), 1)
            dve.wait_ge(S("x_new"), 2 * KC)
            norm_stats(2)
            norm_rest(2)

            dve.wait_ge(S("line_made"), 1)
            dve.memset(line[:, SEQ:2 * SEQ], NEG).then_inc(S("line_made"), 1)
            tiles(dve, "in2", lo_only("in2"))
            tiles(dve, "tok2", lo_only("tok2"), loop=False)
            dve.wait_ge(S("rot_made"), 1)
            dve.tensor_tensor(proj2[:, 0:8, :], proj2[:, 0:8, :], over(rot[:, P:P + SEQ], 8), mul)
            link(dve.tensor_tensor(tmp[:, :, :], ps[:, 0:4, :].rearrange("p b (c t) -> p (b c) t", c=2), over(rot[:, P + SEQ:P + 2 * SEQ], 8), mul))
            dve.tensor_tensor(flat(proj2[:, 0:8, :]), flat(proj2[:, 0:8, :]), flat(tmp[:, :, :]), add).then_inc(S("rotated"), 1)
            for t in range(TT):
                link(dve.tensor_reduce(vmean[:, 8 * t:8 * t + 8], vtok2[:, t, 0:1024].rearrange("p (h d) -> p h d", h=RH), X, add))
                link(dve.tensor_scalar(vmean[:, 8 * t:8 * t + 8], vmean[:, 8 * t:8 * t + 8], 1.0 / RV, None, mul))
                v3 = vtok2[:, t, 0:1024].rearrange("p (h d) -> p h d", h=RH)
                last = dve.tensor_tensor(v3, v3, vmean[:, 8 * t:8 * t + 8].rearrange("p (h o) -> p h o", o=1).to_broadcast([P, RH, RV]), sub)
            last.then_inc(S("v_centred"), 1)
            for h in range(RH):
                dve.wait_ge(S("ret_s"), h + 1)
                if h >= 2:
                    dve.wait_ge(S("ret_o"), h - 1)
                dve.tensor_tensor(pr[:, h % 2, 0:SEQ], ps[:, h % 2, 0:SEQ], dec[:, h, :], mul)
                dve.tensor_tensor(pr[:, h % 2, SEQ:SEQ + P], ps[:, h % 2, SEQ:SEQ + P], dec[:, h, 0:P], mul).then_inc(S("ret_p"), 1)
            dve.wait_ge(S("ro_summed"), 1)
            dve.tensor_scalar(flat(rs[:, 0:8, :]), bank(0, 4), 1.0 / RV, EPS, mul, add).then_inc(S("ro_var"), 1)
            dve.wait_ge(S("ro_root"), 1)
            dve.wait_ge(S("rg_silu"), 1)
            link(dve.reciprocal(flat(rs[:, 0:8, :]), flat(rs[:, 0:8, :])))
            link(dve.tensor_tensor(flat(ro[:, :, :]), flat(ro[:, :, :]), flat(rs[:, 0:8, :]), mul))
            dve.tensor_tensor(flat(ro[:, :, :]), flat(ro[:, :, :]), flat(proj2[:, C_RG:C_RG + 8, :]), mul).then_inc(S("ro_done"), 1)
            dve.wait_ge(S("ro_hi"), 1)
            dve.tensor_tensor(hlo[:, :, :], ro[:, :, :], hhi[:, :, :].bitcast(f32), sub).then_inc(S("ro_lo"), 1)
            dve.wait_ge(S("m_summed"), 1)
            dve.tensor_scalar(flat(rs[:, 0:8, :]), bank(0, 4), 1.0 / MD, EPS, mul, add).then_inc(S("m_var"), 1)
            dve.tensor_scalar(prm2[:, 2:3], prm2[:, 0:1], float(MD) ** -0.5, None, mul)
            dve.wait_ge(S("m_root"), 1)
            link(dve.reciprocal(flat(rs[:, 0:8, :]), flat(rs[:, 0:8, :])))
            dve.scalar_tensor_tensor(flat(proj2[:, C_MQ:C_MQ + 4, :]), flat(proj2[:, C_MQ:C_MQ + 4, :]), prm2[:, 2:3], flat(rs[:, 0:4, :]), mul, mul)
            dve.scalar_tensor_tensor(flat(proj2[:, C_MK:C_MK + 4, :]), flat(proj2[:, C_MK:C_MK + 4, :]), prm2[:, 1:2], flat(rs[:, 4:8, :]), mul, mul).then_inc(S("mk_normed"), 1)
            for n in range(4):
                t, hg = n // 2, n % 2
                W = (t + 1) * P
                dve.wait_ge(S("m_s"), n + 1)
                for b in range(2):
                    last = dve.tensor_reduce(mst[:, b:4:2], ps[:, 2 * (n % 2) + b, :].rearrange("p (h k) -> p h k", h=2)[:, :, 0:W], X, ALU.max, negate=True)
                last.then_inc(S("m_max"), 1)
                dve.wait_ge(S("m_exp"), 4 * (n + 1))
                link(dve.reciprocal(mst[:, 8:12], mst[:, 4:8]))
                for h in range(4):
                    last = dve.tensor_scalar(sp2[:, h, 0:W], sp2[:, h, 0:W], mst[:, 8 + h:9 + h], None, mul)
                last.then_inc(S("m_p"), 1)
                dve.wait_ge(S("m_hi"), n + 1)
                o = (slice(2 * hg, 2 * hg + 2), slice(t * P, (t + 1) * P))
                dve.tensor_tensor(mblo[:, o[0], o[1]], ps[:, 6 + n % 2, 0:2 * P].rearrange("p (c q) -> p c q", c=2), mbhi[:, o[0], o[1]].bitcast(f32), sub).then_inc(S("m_lo"), 1)

            dve.wait_ge(S("ab_sig"), 1)

            def retw(i, j):
                g = BASE["retw"] + j
                split_lo(dve, g + LEAD)
                dve.wait_ge(tile_used, g + 1)
                dve.tensor_tensor(ya[:, j, :], chunk_bank(g), proj2[:, C_GA + j, :], mul).then_inc(S("ya_kept"), 1)
            tiles(dve, "retw", retw)

            def mobw(i, j):
                g = BASE["mobw"] + j
                split_lo(dve, g + LEAD)
                dve.wait_ge(tile_used, g + 1)
                for u in range(2):
                    c = 2 * j + u
                    dve.tensor_tensor(proj2[:, C_GB + c, :], chunk_bank(u), proj2[:, C_GB + c, :], mul).then_inc(S("yb_kept"), 1)
            tiles(dve, "mobw", mobw)
            dve.wait_ge(S("yb_kept"), KC)
            dve.wait_ge(S("ya_kept"), KC)
            dve.tensor_tensor(flat(ya[:, :, :]), flat(ya[:, :, :]), flat(proj2[:, C_GB:C_GB + 8, :]), add).then_inc(S("merged"), 1)
            dve.wait_ge(S("merged_hi"), 1)
            dve.tensor_tensor(hlo[:, :, :], ya[:, :, :], hhi[:, :, :].bitcast(f32), sub).then_inc(S("merged_lo"), 1)

            def out2(i, j):
                g = BASE["out2"] + j
                split_lo(dve, g + LEAD)
                dve.wait_ge(tile_used, g + 1)
                dve.tensor_tensor(x[:, j, :], chunk_bank(g), x[:, j, :], add).then_inc(S("x_new"), 1)
            tiles(dve, "out2", out2)
            dve.wait_ge(S("x_new"), 3 * KC)
            norm_stats(3)
            norm_rest(3)

            def pq(i, j):
                g = BASE["pq"] + j
                split_lo(dve, g + LEAD, i)
                dve.wait_ge(S("q_hi"), 4 * i + (j + 1))
                dve.tensor_tensor(pick(qlo, 4 * i + j), chunk_bank(g), pick(qhi, 4 * i + j).bitcast(f32), sub).then_inc(S("q_lo"), 1)
            tiles(dve, "pq", pq)
            tiles(dve, "subk", lo_only("subk"), loop=False)
            u_lo = lo_only("u")
            for j in range(4):
                u_lo(0, j)
            dve.wait_ge(S("scores_kept"), 2 * TT)

            def route(u):
                def step(ins):
                    dve.drain()

                def top16(best, place, values, rest):
                    step(dve.max(best[:, 0:8], values))
                    step(dve.match_replace(rest, in_to_replace=best[:, 0:8], in_values=values, imm_value=-3e38))
                    step(dve.max(best[:, 8:16], rest))
                    dve.max_index(place[:, 0:8], best[:, 0:8], values)
                    step(dve.max_index(place[:, 8:16], best[:, 8:16], rest))

                unit = sc[:, bass.ds(2 * u, 2), :]
                step(dve.tensor_copy(scu[:, :, :], unit))
                for c in range(2):
                    top16(top8[:, c, :], tix[:, c, :], scu[:, c, :], scr[:, :])
                step(dve.tensor_copy(tixf[:, :, :], tix[:, :, :]))
                wide = [P, TOPK, TOPK]

                def along(t):
                    return t.rearrange("p (o e) -> p o e", o=1).to_broadcast(wide)

                def down_(t):
                    return t.rearrange("p (k o) -> p k o", o=1).to_broadcast(wide)
                step(dve.tensor_tensor(cand[:, :, :], down_(top8[:, 0, :]), along(top8[:, 1, :]), add))
                cbest = pick(ctop[:, :, :, :].rearrange("p t h k -> p (t h) k"), u)
                top16(cbu[:, :], cix[:, :], cand[:, :, :].rearrange("p a b -> p (a b)"), cand2[:, :])
                dve.tensor_copy(cbest, cbu[:, :])
                dve.tensor_scalar(cau[:, 0, :], cix[:, :], 4, None, ALU.logical_shift_right)
                step(dve.tensor_scalar(cau[:, 1, :], cix[:, :], TOPK - 1, None, ALU.bitwise_and))
                step(dve.tensor_copy(cab[:, :, :], cau[:, :, :]))
                for c in range(2):
                    step(dve.tensor_tensor(eq[:, :, :], down_(cab[:, c, :]), along(iota[:, 0:TOPK]), ALU.is_equal))
                    step(dve.tensor_tensor(eq[:, :, :], eq[:, :, :], along(tixf[:, c, :]), mul))
                    where = pick(pidx[:, c, :, :, :].rearrange("p t h k -> p (t h) k"), u)
                    step(dve.tensor_reduce(where, eq[:, :, :], X, add))

            with dve.Fori(0, TT * PH) as u:
                for s in range(4):
                    u_lo(u, 4 + s)
                route(u)
            best = ctop[:, :, :, :].rearrange("p t h k -> p (t h) k")
            link(dve.tensor_copy(gden[:, 0, :], best[:, :, 0]))
            dve.tensor_tensor(best, best, gden[:, 0, :].rearrange("p (u o) -> p u o", o=1).to_broadcast([P, 16, TOPK]), sub).then_inc(S("gate_shifted"), 1)
            tiles(dve, "u", u_lo, 68, 84)
            dve.wait_ge(S("gate_exp"), 1)
            link(dve.tensor_reduce(gden[:, 0, :], best, X, add))
            link(dve.reciprocal(gden[:, 1, :], gden[:, 0, :]))
            dve.tensor_tensor(best, best, gden[:, 1, :].rearrange("p (u o) -> p u o", o=1).to_broadcast([P, 16, TOPK]), mul).then_inc(S("gates_made"), 1)
            tiles(dve, "u", u_lo, 84, 88)
            dve.wait_ge(S("pairs_turned"), 1)
            dve.tensor_copy(pair[:, :, :], ps[:, 3:6, 0:SEQ]).then_inc(S("routed"), 1)
            tiles(dve, "u", u_lo, 88, 128)
            dve.wait_ge(S("routed"), 1)

            def rows(i, q):
                for a in range(4):
                    tok = 4 * q + a if isinstance(i, int) else 8 * i + (4 * q + a)
                    first, second, gate = (col(pair[:, n, :], tok) for n in range(3))
                    dve.tensor_scalar(e1[:, q % 2, a, :], iota, first, None, ALU.is_equal)
                    last = dve.tensor_scalar(e2[:, q % 2, a, :], iota, second, gate, ALU.is_equal, mul)
                last.then_inc(S("e_made"), 1)

            def weigh(i, q):
                dve.wait_ge(S("outer_made"), 2 * i + (q + 1))
                toks = G[:, :, 4 * q:4 * q + 4] if isinstance(i, int) else G[:, :, bass.ds(8 * i + 4 * q, 4)]
                toks = toks.rearrange("p j t -> p t j")
                dve.tensor_tensor(toks, ps[:, 4 + q % 2, :].rearrange("p (t j) -> p t j", t=4), toks, mul).then_inc(S("outer_multiplied"), 1)
            dve.wait_ge(tile_used, BASE["v"])
            rows(0, 0)
            dve.wait_ge(S("g_made"), NKEY)
            rows(0, 1)
            weigh(0, 0)
            with dve.Fori(0, SEQ // 8 - 1) as i:
                rows(i, 2)
                weigh(i, 1)
                rows(i, 3)
                weigh(i, 2)
            weigh(0, SEQ // 4 - 1)

            def m_lo(i, j):
                if j < NKEY:
                    dve.wait_ge(S("mhi_made"), 4 * i + (j + 1))
                    s = (BASE["v"] + j) % RING
                    dve.tensor_tensor(mlo[:, s, :], pick(G, 4 * i + j), mhi[:, s, :].bitcast(f32), sub).then_inc(S("mlo_made"), 1)
            dve.wait_ge(S("outer_multiplied"), SEQ // 4)
            for j in range(LEAD):
                m_lo(0, j)

            def vals(i, j):
                split_lo(dve, BASE["v"] + j + LEAD, i)
                m_lo(i, j + LEAD)
            tiles(dve, "v", vals)


_PARAMS = ["xT", "prm", "wsm", "w2", "upc", "prm2", "relb"]
_CONSTS = ["c_cst", "c_lvl", "c_nmask", "c_cmask", "c_rot", "c_dec", "c_relhot"]


def _constants():
    f = np.float32
    n = np.arange(P)
    cst = np.concatenate([np.eye(P), np.ones((P, P)), n[:, None] <= n[None, :], np.broadcast_to(n, (P, P))], 1).astype(f)
    lvl = np.zeros((P, LEVELS, P), f)
    for l in range(LEVELS):
        b = 1 << l
        same = (n[:, None] // (2 * b)) == (n[None, :] // (2 * b))
        lvl[:, l, :] = same & (n[:, None] % (2 * b) < b) & (n[None, :] % (2 * b) >= b)
    nmask = np.where(n[None, :] <= n[:, None], 0, NEG).astype(f)
    cmask = np.zeros((P, TT, CPAD + 1), f)
    for t in range(TT):
        q = t * P + n
        ends = np.arange(CPAD) * CMP_STRIDE + CMP_BLOCK - 1
        seen = (ends[None, :] <= q[:, None]) & (np.arange(CPAD) < N_CMP)[None, :]
        cmask[:, t, :CPAD] = np.where(seen, 0, NEG)
        cmask[:, t, CPAD] = seen.any(1)
    half = RQK // 2
    inv = f(10000.0) ** (-np.arange(half, dtype=f) / half)
    ang = np.arange(SEQ, dtype=f)[None, :] * inv.astype(f)[:, None]
    cos, sin = np.tile(np.cos(ang), (4, 1)), np.tile(np.sin(ang), (4, 1))
    perm = np.zeros((P, P), f)
    for m in range(P):
        if m % RQK < half:
            perm[m + half, m] = -1
        else:
            perm[m - half, m] = 1
    halves = (n[:, None] // MD == n[None, :] // MD)
    rot = np.concatenate([perm, cos, sin, halves, np.eye(P)[::-1]], 1).astype(f)
    log_g = np.log1p(-np.exp2(-5.0 - np.arange(RH)))
    d = np.arange(SEQ)[None, :] - n[:, None]
    dec = np.where(d[:, None, :] >= 0, np.exp(np.maximum(d, 0)[:, None, :] * log_g[None, :, None]), 0) * RQK ** -0.5
    dist = np.maximum(SEQ - 1 - np.arange(2 * SEQ), 0)
    exact = BUCKETS // 2
    large = exact + (np.log(np.maximum(dist, 1).astype(f) / exact) / f(math.log(MAXDIST / exact)) * (BUCKETS - exact)).astype(np.int32)
    bucket = np.where(dist < exact, dist, np.minimum(large, BUCKETS - 1))
    relhot = (np.arange(BUCKETS)[:, None] == bucket[None, :]).astype(f)
    return dict(c_cst=cst, c_lvl=lvl, c_nmask=nmask, c_cmask=cmask, c_rot=rot, c_dec=dec.astype(f), c_relhot=relhot)


def _chunks(w, nk=KC):
    n = w.shape[1] // P
    return w.reshape(nk, P, n, P).transpose(2, 1, 0, 3).reshape(n, P, nk * P)


def _rows(w, kk):
    return w.reshape(-1, kk, P, w.shape[1]).transpose(0, 2, 1, 3).reshape(-1, P, kk * w.shape[1])


def _layout(a):
    f = {k: np.asarray(v) for k, v in a.items()}
    g = {k: v[0] for k, v in f.items()}
    w = g["w_in"]
    cuts = np.cumsum([0, 512, 512, 512, 512, 4, 4, 512, 128, 128, 128, 128, 128, 128, 12])
    gq, gk, gv, gz, ga, gb, nq, kc, vc, ks, vs, kw, vw, ng = (w[:, s:e] for s, e in zip(cuts[:-1], cuts[1:]))
    w2 = g["w_in_2"]
    cut2 = np.cumsum([0, 512, 512, 1024, 1024, 512, 512, 512, 1024, 1024])
    rq, rk, rv, rg, mq, mk, mv, a2, b2 = (w2[:, s:e] for s, e in zip(cut2[:-1], cut2[1:]))
    up = _chunks(g["ffn_w_up"]).reshape(2, FC, P, TILE).transpose(1, 0, 2, 3).reshape(2 * FC, P, TILE)
    mob = _chunks(g["moba_w_branch_2"], 4).reshape(4, 2, P, 512).transpose(0, 2, 1, 3).reshape(4, P, TILE)
    tok2 = _rows(np.concatenate([rv, mv], 1), 1).reshape(4, 2, P, 3, 512).transpose(3, 0, 2, 1, 4).reshape(12, P, TILE)
    cmpw = np.stack([g["cmp_k_w1"], g["cmp_v_w1"]]).reshape(2, 4, 8, P, P).transpose(0, 1, 3, 2, 4).reshape(8, P, TILE)
    subk = g["peer_sub_keys_2"].reshape(2, 8, NKEY, P).transpose(0, 3, 1, 2).reshape(2, P, TILE)
    u = g["peer_u_2"].reshape(NKEY, NKEY, KC, P).transpose(1, 3, 2, 0).reshape(NKEY, P, TILE)
    v = g["peer_v_2"].reshape(NKEY, NKEY, D).transpose(1, 0, 2)
    c = {
        "ada": _chunks(g["ada_w"]), "win": _chunks(np.concatenate([gq, gk, nq, ks, kw, gv, gz, kc, vc], 1)),
        "tok": _rows(np.concatenate([vs, vw], 1), 4), "cmp": cmpw, "wout": _chunks(g["w_out"]), "up": up,
        "down": g["ffn_w_down"].reshape(FC, P, D), "in2": _chunks(np.concatenate([rq, rk, rg, mq, mk, a2, b2], 1)),
        "tok2": tok2, "retw": _chunks(g["ret_w_branch_2"]), "mobw": mob, "out2": _chunks(g["w_out_2"]),
        "pq": _chunks(g["peer_w_q_2"]), "subk": subk, "u": u, "v": v,
    }
    out = {"w_" + k: x for k, x in c.items()}
    cols = lambda x: x.reshape(-1, P).T
    every = lambda x: np.broadcast_to(x.reshape(1, -1), (P, x.size))
    convw = g["gdn_conv_w"].reshape(4, 12, P).transpose(2, 1, 0).reshape(P, 48)
    prm = [cols(g["norm1_w"]), cols(g["norm2_w"]), cols(g["mix_norm_g_2"]), cols(g["ffn_norm_g_2"]), convw,
           cols(g["gdn_out_norm_w"]), cols(g["nsa_q_norm_w"]), cols(g["nsa_k_norm_cmp"]), cols(g["nsa_k_norm_slc"]),
           cols(g["nsa_k_norm_win"]), every(g["gdn_dt_bias"]), every(g["gdn_A_log"]), np.zeros((P, 3), np.float32),
           cols(f["c"][0]), cols(g["ada_b"]), g["cmp_k_pos"].T, g["cmp_v_pos"].T]
    prm = np.concatenate(prm, 1)
    out["prm"] = np.concatenate([prm, np.zeros((P, 256 - prm.shape[1]), np.float32)], 1)
    out["xT"] = f["x"][0].T.reshape(KC, P, SEQ).transpose(1, 0, 2)
    out["wsm"] = np.concatenate([ga, gb, ng], 1).reshape(KC, P, 20).transpose(1, 0, 2)
    out["w2"] = np.stack([g["cmp_k_w2"], g["cmp_v_w2"]], 1)
    taps = np.concatenate([g["ffn_conv_w"], g["ffn_conv_b"][None]], 0)
    out["upc"] = taps.reshape(4, 2, FC, P).transpose(3, 2, 1, 0).reshape(P, 2 * FC, 4)
    gains = np.stack([np.tile(g["moba_q_gain_2"], 2), np.tile(g["moba_k_gain_2"], 2)], 1)
    out["prm2"] = np.concatenate([gains, np.zeros((P, 14), np.float32)], 1)
    out["relb"] = f["rel_bias_2"]
    return out


def kernel(**inputs):
    from concourse import bacc
    from concourse.bass_utils import run_bass_kernel_spmd

    nc = bacc.Bacc("TRN2", target_bir_lowering=False, num_devices=1)
    arrays = {k: np.ascontiguousarray(v) for k, v in {**_layout(inputs), **_constants()}.items()}
    A = {k: nc.dram_tensor("in_" + k, v.shape, mybir.dt.from_np(v.dtype), kind="ExternalInput").ap() for k, v in arrays.items()}
    A["line"] = nc.dram_tensor("bias_lines", (MH, 2 * SEQ), mybir.dt.float32).ap()
    out = nc.dram_tensor("out_x", (1, SEQ, D), mybir.dt.float32, kind="ExternalOutput").ap()
    build_program(nc, A, out)
    r = run_bass_kernel_spmd(nc, [{"in_" + k: v for k, v in arrays.items()}], core_ids=[0])
    return r.results[0]["out_x"]
```

```python
import math
import numpy as np
import concourse.bass as bass
from concourse import mybir
from contextlib import ExitStack

P = 128
SEQ, D = 256, 1024
KC = D // P
TT = SEQ // P
HEAD = 128
EPS = 1e-6
NEG = -1e30
TILE = 1024
RING = 4
LEAD = 2

FF = 2816
FC = FF // P
GH = 4
NH = 4
CMP_BLOCK, CMP_STRIDE = 32, 16
N_CMP = (SEQ - CMP_BLOCK) // CMP_STRIDE + 1
CPAD = 16
LEVELS = 7

RH, RQK, RV = 8, 64, 128
MH, MD = 8, 64
BUCKETS, MAXDIST = 32, 2048
PH, NKEY, TOPK = 8, 128, 16
NPAIR = PH * TOPK
NEXP = NKEY * NKEY

C_GQ, C_GK, C_GV, C_NQ, C_KS, C_KW, C_GZ, C_KC, C_VC = 0, 4, 8, 12, 16, 17, 18, 22, 23
CONV = 12
C_RQ, C_RK, C_RG, C_MQ, C_MK, C_GA, C_GB = 0, 4, 8, 16, 20, 24, 32

SEGMENTS = [("ada1", 16), ("win", 24), ("tok", 2), ("cmp", 8), ("ada2", 32), ("wout", 8), ("up", 2 * FC), ("down", FC),
            ("in2", 40), ("tok2", 12), ("retw", 8), ("mobw", 4), ("out2", 8), ("pq", 16), ("subk", 2),
            ("u", NKEY), ("v", NKEY)]
BASE, _at = {}, 0
for _name, _n in SEGMENTS:
    BASE[_name] = _at
    _at += _n
COUNT = dict(SEGMENTS)
TOTAL = _at
RAW1, RAW2 = COUNT["ada1"], COUNT["ada2"]


def is_raw(g):
    return g < RAW1 or 0 <= g - BASE["ada2"] < RAW2


def nth(g):
    raw = min(g + 1, RAW1) + min(max(g + 1 - BASE["ada2"], 0), RAW2)
    return raw if is_raw(g) else g + 1 - raw


def build_program(nc, A, out):
    f32, f32r = mybir.dt.float32, mybir.dt.float32r
    u32 = mybir.dt.uint32
    ALU, ACT = mybir.AluOpType, mybir.ActivationFunctionType
    X = mybir.AxisListType.X
    add, sub, mul = ALU.add, ALU.subtract, ALU.mult

    ctx = ExitStack()
    with ctx:
        sems = {}

        def S(name):
            if name not in sems:
                sems[name] = ctx.enter_context(nc.semaphore(name))
            return sems[name]

        top = [-(-nc.sbuf_base // 32) * 32]

        def span(shape):
            return -(-4 * int(np.prod(shape[1:])) // 32) * 32

        def at(name, shape, dt, offset=None):
            size = span(shape)
            if offset is None:
                offset = top[0]
                top[0] = offset + size
            assert offset + size <= nc.sbuf_usable_end, (name, offset, size)
            return nc.alloc_sbuf_tensor_at(name, list(shape), dt, offset=offset)

        raw = at("raw", [P, RING, TILE], f32)
        whi = at("whi", [P, RING, TILE], f32r)
        wlo = at("wlo", [P, RING, TILE], f32r)
        raw_end = top[0]
        x = at("x", [P, KC, SEQ], f32)
        hhi = at("hhi", [P, KC, SEQ], f32r)
        hlo = at("hlo", [P, KC, SEQ], f32r)
        cst = at("cst", [P, 4 * P], f32)
        ident, ones, tri, iota = (cst[:, i * P:(i + 1) * P] for i in range(4))
        gains = at("gains", [P, 4, KC], f32)
        shifts = at("shifts", [P, 4, KC], f32)
        mod = at("mod", [P, 48], f32)
        epsc = at("epsc", [P, 1], f32)
        PAIR0 = top[0]
        G0 = PAIR0 + 3 * SEQ * 4
        up_at = [G0]

        def big(name, shape, dt=f32, offset=None):
            if offset is None:
                offset = up_at[0]
                up_at[0] += span(shape)
            return at(name, shape, dt, offset)

        tmp = big("tmp", [P, KC, SEQ])
        rs = big("rs", [P, 14, SEQ])
        R1 = up_at[0]
        acc2 = big("acc2", [P, 2, TILE], offset=G0)
        prm = big("prm", [P, 256])
        proj = big("proj", [P, 24, SEQ])
        vtok = big("vtok", [P, TT, 256])
        small = big("small", [P, TT, 20])
        wsm = big("wsm", [P, KC, 20])
        w2 = big("w2", [P, 2, P])
        lvl = big("lvl", [P, LEVELS, P])
        nmask = big("nmask", [P, P])
        cmask = big("cmask", [P, TT, CPAD + 1])
        csl = big("csl", [P, KC])
        hid = big("hid", [P, 2, CPAD])
        kc = big("kc", [P, CPAD])
        sqc = big("sqc", [P, CPAD])
        rsc = big("rsc", [P, CPAD])
        vc = big("vc", [P, P])
        blk = big("blk", [P, 2, CMP_BLOCK, CPAD])
        B0 = up_at[0]
        bhi = big("bhi", [P, 2, CMP_BLOCK, CPAD], f32r)
        blo = big("blo", [P, 2, CMP_BLOCK, CPAD], f32r)
        gsm = big("gsm", [P, 96])
        gcB = big("gcB", [P, 8, P])
        Xs = big("Xs", [P, 8, P], offset=B0)
        wT = big("wT", [P, GH, P], offset=B0 + 4096)
        St = big("St", [P, GH, P], offset=B0 + 6144)
        kbT = big("kbT", [P, GH, SEQ])
        R2 = up_at[0]
        DT = big("DT", [P, 8, P])
        AT = big("AT", [P, 8, P])
        QT = big("QT", [P, 8, P])
        BT = big("BT", [P, 8, P])
        Tm = big("Tm", [P, 8, P])
        TTm = big("TTm", [P, 8, P])
        vb = big("vb", [P, 8, P])
        kw = big("kw", [P, 8, P])
        U = big("U", [P, 8, P])
        qd = big("qd", [P, GH, P])
        eg = big("eg", [P, GH, P])
        og = big("og", [P, GH, SEQ])
        ogsq = big("ogsq", [P, 1024])
        acc = big("acc", [P, 2, 2, TILE], offset=R2 + 16 * 1024)
        cv = big("cv", [P, 12, SEQ], offset=R2)
        sq = big("sq", [P, 14 * SEQ], offset=R2)
        sp_ = big("sp_", [P, NH, 512], offset=R2)
        spc = big("spc", [P, NH, CPAD], offset=R2 + 8192)
        nst = big("nst", [P, 48], offset=R2 + 8448)
        pt = big("pt", [P, 2, 512], offset=R2 + 8704)
        ptc = big("ptc", [P, 2, P], offset=R2 + 12800)
        ahi = big("ahi", [P, FC, SEQ], f32r, offset=R1)
        alo = big("alo", [P, FC, SEQ], f32r, offset=R1 + FC * 1024)
        o_ = R1 + 2 * FC * 1024
        upc = big("upc", [P, 2 * FC, 4], offset=o_)
        uc = big("uc", [P, 4, SEQ], offset=o_ + 1024)
        upp = big("upp", [P, 2, SEQ], offset=o_ + 5120)
        zz = big("zz", [P, 512], f32r, offset=o_ + 7168)
        zf = big("zf", [P, 512], offset=o_ + 9216)
        up_at[0] = R1
        proj2 = big("proj2", [P, 40, SEQ])
        vtok2 = big("vtok2", [P, TT, 1536])
        bias = big("bias", [P, TT, MH, SEQ])
        dec = big("dec", [P, RH, SEQ])
        rot = big("rot", [P, 3 * P + 2 * SEQ])
        relhot = big("relhot", [BUCKETS, 2 * SEQ])
        relb = big("relb", [BUCKETS, MH])
        line = big("line", [MH, 2 * SEQ])
        prm2 = big("prm2", [P, 16])
        ro = big("ro", [P, RH, SEQ])
        ya = big("ya", [P, KC, SEQ])
        mbhi = big("mbhi", [P, 4, SEQ], f32r)
        mblo = big("mblo", [P, 4, SEQ], f32r)
        mst = big("mst", [P, 32])
        vmean = big("vmean", [P, 16])
        RS = 8192 + G0
        pr = big("pr", [P, 2, 384], offset=RS + 2048)
        sp2 = big("sp2", [P, 4, SEQ], offset=RS + 1024 * 6)
        pt2 = big("pt2", [P, 2, SEQ], offset=RS + 1024 * 11)
        pair = at("pair", [P, 3, SEQ], f32, PAIR0)
        G = at("G", [P, NKEY, SEQ], f32, G0)
        qhi = at("qhi", [P, 16, SEQ], f32r, G0 + 48 * 1024)
        qlo = at("qlo", [P, 16, SEQ], f32r, G0 + 64 * 1024)
        sc = at("sc", [P, TT * PH * 2, NKEY], f32, G0 + 104 * 1024)
        o_ = G0 + 120 * 1024
        scu = at("scu", [P, 4, NKEY], f32, o_)
        scr = at("scr", [P, 4, NKEY], f32, o_ + 2048)
        cand = at("cand", [P, 2, TOPK, TOPK], f32, o_ + 2048)
        cand2 = at("cand2", [P, 2, TOPK * TOPK], f32, o_)
        eq = at("eq", [P, 2, 2, TOPK, TOPK], f32, o_)
        top8 = at("top8", [P, 4, TOPK], f32, o_ + 4096)
        tix = at("tix", [P, 4, TOPK], u32, o_ + 4352)
        tixf = at("tixf", [P, 4, TOPK], f32, o_ + 4608)
        cbu = at("cbu", [P, 2, TOPK], f32, o_ + 4864)
        cix = at("cix", [P, 2, TOPK], u32, o_ + 4992)
        cau = at("cau", [P, 2, 2, TOPK], u32, o_ + 5120)
        cab = at("cab", [P, 2, 2, TOPK], f32, o_ + 5376)
        gden = at("gden", [P, 2, TT * PH], f32, o_ + 5632)
        ctop = at("ctop", [P, TT * PH, TOPK], f32, PAIR0)
        pidx = at("pidx", [P, 2, TT * PH, TOPK], f32, PAIR0 + 1024)
        hh0 = raw_end + KC * SEQ * 4
        e1 = at("e1", [P, 2, 4, P], f32, hh0)
        e2 = at("e2", [P, 2, 4, P], f32, hh0 + 4096)
        mhi = at("mhi", [P, RING, SEQ], f32r, hh0 + 8192)
        dist = at("dist", [P, 4, 4, P], f32, hh0 + 8192)
        mlo = at("mlo", [P, RING, SEQ], f32r, hh0 + 12288)
        y = at("y", [P, TT, D], f32, hh0)

        ps = ctx.enter_context(nc.psum_tensor("ps", [P, 8, 512], f32))

        def bank(b, n=1):
            return ps[:, b:b + n, :].rearrange("p b c -> p (b c)")

        w_loaded = [S(f"w_loaded{s}") for s in range(RING)]
        hi_made, lo_made, tile_used, raw_used = S("hi_made"), S("lo_made"), S("tile_used"), S("raw_used")

        def wait(eng, sem, value):
            if not isinstance(value, int) or value > 0:
                eng.wait_ge(sem, value)

        def tiles(eng, name, body, start=0, stop=None, loop=True):
            n = COUNT[name] if stop is None else stop
            head = start + 4 if start == 0 else start
            tail = n - 4 if (name, n) == ("v", COUNT["v"]) else n
            m = (tail - head) // 4
            if m < 2 or not loop:
                m, head = 0, start
            for j in range(start, head):
                body(0, j)
            if m:
                with eng.Fori(0, m) as i:
                    for s in range(4):
                        body(i, head + s)
            for j in range(head + 4 * m, n):
                body(0, j)

        def pick(t, j):
            if isinstance(j, int):
                return t[:, j]
            return t[:, bass.ds(j, 1)].rearrange("p o t -> p (o t)")

        def col(t, j):
            return t[:, j:j + 1] if isinstance(j, int) else t[:, bass.ds(j, 1)]

        def load(sp, name):
            def body(i, j):
                g = BASE[name] + j
                if g >= RING:
                    sp.wait_ge(raw_used if is_raw(g - RING) else lo_made, 4 * i + nth(g - RING))
                src = A["w_" + name]
                src = src[4 * i + j] if isinstance(i, int) else src[bass.ds(4 * i + j, 1)].rearrange("o p c -> p (o c)")
                sp.dma_start(raw[:, g % RING, :], src).then_inc(w_loaded[g % RING], 16)
            return body

        def split_hi(act, g, i=0):
            if g < TOTAL and not is_raw(g):
                act.wait_ge(w_loaded[g % RING], 16 * i + 16 * (g // RING + 1))
                if nth(g) > RING:
                    act.wait_ge(tile_used, 4 * i + nth(g) - RING)
                act.activation(whi[:, g % RING, :], raw[:, g % RING, :], ACT.Copy).then_inc(hi_made, 1)

        def split_lo(dve, g, i=0):
            if g < TOTAL and not is_raw(g):
                dve.wait_ge(hi_made, 4 * i + nth(g))
                dve.tensor_tensor(wlo[:, g % RING, :], raw[:, g % RING, :], whi[:, g % RING, :].bitcast(f32), sub).then_inc(lo_made, 1)

        def products(pe, g, o, cols, bh, bl, start, stop):
            wh, wl = whi[:, g % RING, cols], wlo[:, g % RING, cols]
            pe.matmul(o, wh, bh, start=start, stop=False, skip_group_check=True)
            pe.matmul(o, wh, bl, start=False, stop=False, skip_group_check=True)
            return pe.matmul(o, wl, bh, start=False, stop=stop, skip_group_check=True)

        def chunk_bank(g):
            return ps[:, 6 + g % 2, 0:SEQ]

        def segment_T(pe, name, bh, bl, kept, count0=0, nk=KC, norm=None):
            def body(i, j):
                g, per = BASE[name] + j, KC // nk
                pe.wait_ge(lo_made, 4 * i + nth(g))
                for u in range(per):
                    if per * j + u >= 2:
                        pe.wait_ge(S(kept), per * 4 * i + (count0 + per * j + u - 1))
                    for k in range(nk):
                        if norm is not None and isinstance(i, int) and j == 0:
                            pe.wait_ge(S("h_lo"), KC * norm + k + 1)
                        last = products(pe, g, chunk_bank(g * per + u), slice((u * nk + k) * P, (u * nk + k + 1) * P),
                                        bh[:, k, :], bl[:, k, :], k == 0, k == nk - 1)
                last.then_inc(tile_used, 1)
            return body

        block = ctx.enter_context(nc.Block())
        @block.sync
        def _(sp):
            sp.dma_start(cst[:, :], A["c_cst"]).then_inc(S("prm_in"), 16)
            sp.dma_start(prm[:, :], A["prm"]).then_inc(S("prm_in"), 16)
            sp.dma_start(x[:, :, :], A["xT"]).then_inc(S("x_in"), 16)
            for name, _ in SEGMENTS:
                tiles(sp, name, load(sp, name))
            sp.wait_ge(S("y_made"), TT)
            for t in range(TT):
                sp.dma_start(out[0, t * P:(t + 1) * P, :], y[:, t, :]).then_inc(S("stored"), 16)
            sp.wait_ge(S("stored"), 16 * TT)

        @block.gpsimd
        def _(pool):
            pool.dma_start(lvl[:, :, :], A["c_lvl"]).then_inc(S("mix1_in"), 16)
            pool.dma_start(nmask[:, :], A["c_nmask"]).then_inc(S("mix1_in"), 16)
            pool.dma_start(cmask[:, :, :], A["c_cmask"]).then_inc(S("mix1_in"), 16)
            pool.dma_start(wsm[:, :, :], A["wsm"]).then_inc(S("mix1_in"), 16)
            pool.dma_start(w2[:, :, :], A["w2"]).then_inc(S("mix1_in"), 16)
            pool.wait_ge(S("x_new"), KC)
            pool.dma_start(upc[:, :, :], A["upc"]).then_inc(S("up_in"), 16)
            pool.wait_ge(S("x_new"), 2 * KC)
            pool.dma_start(prm2[:, :], A["prm2"]).then_inc(S("prm2_in"), 16)
            for dst, src in ((rot[:, :], "c_rot"), (dec[:, :, :], "c_dec"), (relhot[:, :], "c_relhot"), (relb[:, :], "relb")):
                pool.dma_start(dst, A[src]).then_inc(S("mix2_in"), 16)
            pool.wait_ge(S("line_made"), 2)
            pool.dma_start(A["line"], line[:, :]).then_inc(S("line_out"), 16)
            pool.wait_ge(S("line_out"), 16)
            for h in range(MH):
                for t in range(TT):
                    pool.dma_start(bias[:, t, h, 0:(t + 1) * P],
                                   bass.AP(tensor=A["line"].tensor, offset=h * 2 * SEQ + (1 - t) * P,
                                           ap=[[1, P], [1, (t + 1) * P]])).then_inc(S("bias_in"), 16)

        @block.tensor
        def _(pe):
            def norm_sum(k, c):
                pe.wait_ge(S("norm_squared"), KC * k + c + 1)
                last = pe.matmul(ps[:, 4, 0:SEQ], ones, tmp[:, c, :], start=c == 0, stop=c == KC - 1, skip_group_check=True)
                if c == KC - 1:
                    last.then_inc(S("norm_summed"), 1)

            def norm(k):
                for c in range(KC):
                    norm_sum(k, c)

            def new_x(name, k, count0):
                seg = segment_T(pe, name, hhi, hlo, "x_new", count0=count0)

                def body(i, j):
                    seg(i, j)
                    if j >= 2:
                        norm_sum(k, j - 2)
                tiles(pe, name, body)
                for c in range(KC - 2, KC):
                    norm_sum(k, c)

            pe.wait_ge(S("prm_in"), 32)
            norm(0)
            def mod_sum(n):
                pe.wait_ge(raw_used, KC * (n + 1))
                for m in range(KC):
                    w = slice(m * P, (m + 1) * P)
                    if n < 2:
                        o = ps[:, 1, KC * n + m:KC * n + m + 1]
                        pe.matmul(o, acc[:, n, 0, w], ones[:, 0:1], start=True, stop=False)
                        last = pe.matmul(o, acc[:, n, 1, w], ones[:, 0:1], start=False, stop=True)
                    else:
                        o = ps[:, 7, KC * (n - 2) + m:KC * (n - 2) + m + 1]
                        last = pe.matmul(o, acc2[:, n % 2, w], ones[:, 0:1], start=True, stop=True)
                last.then_inc(S("mod_summed"), 1)
            mod_sum(0)
            mod_sum(1)

            tiles(pe, "win", segment_T(pe, "win", hhi, hlo, "win_kept", norm=0))

            def tok(i, j):
                slot = (BASE["tok"] + j) % RING
                pe.wait_ge(lo_made, nth(BASE["tok"] + j))
                for t in range(TT):
                    for kk in range(4):
                        k, w = 4 * j + kk, slice(kk * 256, kk * 256 + 256)
                        s = slice(t * P, (t + 1) * P)
                        pe.matmul(ps[:, 4 + t, 0:256], hhi[:, k, s], whi[:, slot, w], start=k == 0, stop=False)
                        pe.matmul(ps[:, 4 + t, 0:256], hlo[:, k, s], whi[:, slot, w], start=False, stop=False)
                        last = pe.matmul(ps[:, 4 + t, 0:256], hhi[:, k, s], wlo[:, slot, w], start=False, stop=k == KC - 1)
                last.then_inc(tile_used, 1)
            tiles(pe, "tok", tok)
            pe.wait_ge(S("mix1_in"), 5 * 16)
            pe.wait_ge(S("h_made"), 1)
            for t in range(TT):
                for k in range(KC):
                    last = pe.matmul(ps[:, 3, 32 * t:32 * t + 20], tmp[:, k, t * P:(t + 1) * P], wsm[:, k, :], start=k == 0, stop=k == KC - 1)
            last.then_inc(S("small_made"), 1)
            pe.wait_ge(S("blk_lo"), 1)

            def cmp(i, j):
                g = BASE["cmp"] + j
                pe.wait_ge(lo_made, nth(g))
                kv = j // 4
                for k in range(8):
                    m = (j % 4) * 8 + k
                    last = products(pe, g, ps[:, kv, 0:CPAD], slice(k * P, (k + 1) * P), bhi[:, kv, m, :], blo[:, kv, m, :], m == 0, m == 31)
                last.then_inc(tile_used, 1)
            tiles(pe, "cmp", cmp)
            pe.wait_ge(S("hid_made"), 1)
            pe.matmul(ps[:, 2, 0:CPAD], w2[:, 0, :], hid[:, 0, :], start=True, stop=True)
            pe.matmul(ps[0:CPAD, 2, P:2 * P], hid[:, 1, :], w2[:, 1, :], start=True, stop=True).then_inc(S("cmp_made"), 1)
            pe.wait_ge(S("heads_squared"), 2)
            pe.wait_ge(S("cmp_squared"), 1)
            pe.wait_ge(S("vc_made"), 1)
            for b in range(7):
                pe.matmul(ps[:, b, :], ones, sq[:, b * 512:(b + 1) * 512], start=True, stop=True)
            pe.matmul(ps[:, 7, 0:CPAD], ones, sqc[:, :], start=True, stop=True).then_inc(S("heads_summed"), 1)

            pe.wait_ge(S("decay_made"), 1)
            for p in range(8):
                t, h = p // 4, p % 4
                pe.matmul(ps[:, p // 4, h * P:(h + 1) * P], gsm[:, p:p + 1].to_broadcast([P, P]), tri, start=True, stop=True)
            for t in range(TT):
                pe.matmul(ps[:, 4, 4 * t:4 * t + 4], tri, gsm[:, 4 * t:4 * t + 4], start=True, stop=True)
            for p in range(8):
                last = pe.matmul(ps[:, 2 + p // 4, (p % 4) * P:(p % 4 + 1) * P], gsm[:, 8 + p:9 + p].to_broadcast([P, P]), ident, start=True, stop=True)
            last.then_inc(S("sums_made"), 1)
            pe.wait_ge(S("kbT_made"), 1)

            def tt(p):
                return slice((p // 4) * P, (p // 4 + 1) * P)
            for p in range(8):
                h, b, c = p % 4, p // 4, slice((p % 4) * P, (p % 4 + 1) * P)
                pe.matmul(ps[:, b, c], proj[:, C_GK + h, tt(p)], kbT[:, h, tt(p)], start=True, stop=True)
                pe.matmul(ps[:, 2 + b, c], proj[:, C_GK + h, tt(p)], proj[:, C_GQ + h, tt(p)], start=True, stop=True)
            for p in range(8):
                h, b, c = p % 4, p // 4, slice((p % 4) * P, (p % 4 + 1) * P)
                pe.transpose(ps[:, 4 + b, c], proj[:, C_GK + h, tt(p)], ident)
                last = pe.transpose(ps[:, 6 + b, c], proj[:, C_GV + h, tt(p)], ident)
            last.then_inc(S("kk_made"), 1)
            pe.wait_ge(S("kv_scaled"), 1)
            for l in range(LEVELS):
                if l in (1, 4):
                    mod_sum(2 + l // 4)
                for b in range(2):
                    pe.wait_ge(S("lvl_masked"), 2 * l + b + 1)
                    if l:
                        pe.wait_ge(S("inv_updated"), 2 * (l - 1) + b + 1)
                    for p in range(4 * b, 4 * b + 4):
                        last = pe.matmul(ps[:, b, (p % 4) * P:(p % 4 + 1) * P], BT[:, p, :], Tm[:, p, :], start=True, stop=True)
                    last.then_inc(S("inv_x"), 1)
                for b in range(2):
                    pe.wait_ge(S("inv_xs"), 2 * l + b + 1)
                    for p in range(4 * b, 4 * b + 4):
                        c = slice((p % 4) * P, (p % 4 + 1) * P)
                        pe.matmul(ps[:, 2 + b, c], TTm[:, p, :], Xs[:, p, :], start=True, stop=True)
                        last = pe.matmul(ps[:, 4 + b, c], Xs[:, p, :], TTm[:, p, :], start=True, stop=True)
                    last.then_inc(S("inv_y"), 1)
            pe.wait_ge(S("inv_updated"), 2 * LEVELS)
            for p in range(8):
                c = slice((p % 4) * P, (p % 4 + 1) * P)
                pe.matmul(ps[:, p // 4, c], TTm[:, p, :], vb[:, p, :], start=True, stop=True)
            for h in range(GH):
                last = pe.matmul(ps[:, 2, h * P:(h + 1) * P], kw[:, 4 + h, :], TTm[:, 4 + h, :], start=True, stop=True)
            last.then_inc(S("uw_made"), 1)
            pe.wait_ge(S("uw_kept"), 1)
            for h in range(GH):
                last = pe.matmul(ps[:, 3, h * P:(h + 1) * P], kw[:, h, :], U[:, h, :], start=True, stop=True)
            last.then_inc(S("state_made"), 1)
            pe.wait_ge(S("state_kept"), 1)
            for h in range(GH):
                last = pe.matmul(ps[:, 4, h * P:(h + 1) * P], wT[:, h, :], St[:, h, :], start=True, stop=True)
            last.then_inc(S("ws_made"), 1)
            for h in range(GH):
                pe.matmul(ps[:, 5, h * P:(h + 1) * P], U[:, h, :], QT[:, h, :], start=True, stop=True)
            pe.wait_ge(S("vnew_made"), 1)
            for h in range(GH):
                c = slice(h * P, (h + 1) * P)
                pe.matmul(ps[:, 6, c], St[:, h, :], qd[:, h, :], start=True, stop=False)
                last = pe.matmul(ps[:, 6, c], U[:, 4 + h, :], QT[:, 4 + h, :], start=False, stop=True)
            last.then_inc(S("og_made"), 1)
            pe.wait_ge(S("og_squared"), 1)
            for b in range(2):
                last = pe.matmul(ps[:, b, :], ones, ogsq[:, b * 512:(b + 1) * 512], start=True, stop=True)
            last.then_inc(S("og_summed"), 1)
            mod_sum(4)
            mod_sum(5)

            for t in range(TT):
                W = (t + 1) * P
                pe.wait_ge(S("og_lo"), 1)
                if t:
                    pe.wait_ge(S("mix_lo"), t)
                for h in range(NH):
                    q = proj[:, C_NQ + h, t * P:(t + 1) * P]
                    pe.matmul(ps[:, h, 0:W], q, proj[:, C_KS, 0:W], start=True, stop=True)
                    pe.matmul(ps[:, h, 256:256 + W], q, proj[:, C_KW, 0:W], start=True, stop=True)
                for h in range(NH):
                    last = pe.matmul(ps[:, 4, h * CPAD:(h + 1) * CPAD], proj[:, C_NQ + h, t * P:(t + 1) * P], kc[:, :], start=True, stop=True)
                last.then_inc(S("nsa_s"), 1)
                pe.wait_ge(S("nsa_p"), t + 1)
                for h in range(NH):
                    m = 4 * t + h
                    if m >= 2:
                        pe.wait_ge(S("nsa_pt"), m - 1)
                    z = 5 if m % 2 == 0 else 6
                    n = 0
                    for kk in range(2):
                        for u in range(t + 1):
                            pe.transpose(ps[:, z, n * P:(n + 1) * P], sp_[:, h, kk * 256 + u * P:kk * 256 + (u + 1) * P], ident)
                            n += 1
                    pe.transpose(ps[0:CPAD, 4, P + (m % 2) * P:P + (m % 2 + 1) * P], spc[:, h, :], ident).then_inc(S("nsa_tr"), 1)
                    pe.wait_ge(S("nsa_pt"), m + 1)
                    o = ps[:, 7, h * P:(h + 1) * P]
                    n = 0
                    for kk in range(2):
                        for u in range(t + 1):
                            pe.matmul(o, vtok[:, u, kk * P:(kk + 1) * P], pt[:, m % 2, n * P:(n + 1) * P], start=n == 0, stop=False)
                            n += 1
                    last = pe.matmul(o, vc[0:CPAD, :], ptc[0:CPAD, m % 2, :], start=False, stop=True)
                last.then_inc(S("nsa_o"), 1)

            pe.wait_ge(S("mix_lo"), TT)
            new_x("wout", 1, 0)
            tiles(pe, "up", segment_T(pe, "up", hhi, hlo, "up_kept", norm=1))
            pe.wait_ge(S("zeros_made"), 1)
            for b in range(4):
                pe.matmul(ps[:, b, :], zz[:, 0:P], zz[:, :], start=True, stop=False, skip_group_check=True)
            pe.wait_ge(S("act_lo"), FC)

            def down(i, j):
                g = BASE["down"] + j
                pe.wait_ge(lo_made, 4 * i + nth(g))
                for c in range(KC):
                    last = products(pe, g, ps[:, c // 2, (c % 2) * SEQ:(c % 2 + 1) * SEQ], slice(c * P, (c + 1) * P),
                                    pick(ahi, 4 * i + j), pick(alo, 4 * i + j), False, False)
                last.then_inc(tile_used, 1)
            tiles(pe, "down", down)

            norm(2)
            pe.wait_ge(S("mix2_in"), 4 * 16)
            pe.matmul(ps[0:MH, 5, :], relb[:, :], relhot[:, :], start=True, stop=True).then_inc(S("line_psum"), 1)
            tiles(pe, "in2", segment_T(pe, "in2", hhi, hlo, "in2_kept", norm=2))

            def tok2(i, j):
                g, n = BASE["tok2"] + j, j // 4
                pe.wait_ge(lo_made, nth(g))
                if j == 8:
                    pe.wait_ge(S("tok2_kept"), 2)
                for t in range(TT):
                    for kk in range(2):
                        k, w, s = 2 * (j % 4) + kk, slice(kk * 512, kk * 512 + 512), slice(t * P, (t + 1) * P)
                        o = ps[:, 2 * (n % 2) + t, :]
                        pe.matmul(o, hhi[:, k, s], whi[:, g % RING, w], start=k == 0, stop=False)
                        pe.matmul(o, hlo[:, k, s], whi[:, g % RING, w], start=False, stop=False)
                        last = pe.matmul(o, hhi[:, k, s], wlo[:, g % RING, w], start=False, stop=k == KC - 1)
                last.then_inc(tile_used, 1)
            tiles(pe, "tok2", tok2, loop=False)
            pe.wait_ge(S("in2_kept"), 40)
            pe.wait_ge(S("tok2_kept"), 6)
            for c in range(8):
                last = pe.matmul(ps[:, c // 2, (c % 2) * SEQ:(c % 2 + 1) * SEQ], rot[:, 0:P], proj2[:, C_RQ + c, :], start=True, stop=True)
            last.then_inc(S("rot_made"), 1)
            pe.wait_ge(S("rotated"), 1)
            pe.wait_ge(S("v_centred"), 1)

            def ret_s(h):
                r = slice(64 * (h % 2), 64 * (h % 2) + 64)
                if h >= 2:
                    pe.wait_ge(S("ret_p"), h - 1)
                pe.matmul(ps[:, h % 2, 0:SEQ], proj2[r, C_RK + h // 2, 0:P], proj2[r, C_RQ + h // 2, :], start=True, stop=True)
                pe.matmul(ps[:, h % 2, SEQ:SEQ + P], proj2[r, C_RK + h // 2, P:SEQ], proj2[r, C_RQ + h // 2, P:SEQ], start=True, stop=True).then_inc(S("ret_s"), 1)

            def ret_o(h):
                pe.wait_ge(S("ret_p"), h + 1)
                if h >= 2:
                    pe.wait_ge(S("ro_kept"), h - 1)
                c = slice(h * RV, (h + 1) * RV)
                pe.matmul(ps[:, 2 + h % 2, 0:P], vtok2[:, 0, c], pr[:, h % 2, 0:P], start=True, stop=True)
                pe.matmul(ps[:, 2 + h % 2, P:SEQ], vtok2[:, 0, c], pr[:, h % 2, P:SEQ], start=True, stop=False)
                pe.matmul(ps[:, 2 + h % 2, P:SEQ], vtok2[:, 1, c], pr[:, h % 2, SEQ:SEQ + P], start=False, stop=True).then_inc(S("ret_o"), 1)
            ret_s(0)
            for h in range(RH):
                if h + 1 < RH:
                    ret_s(h + 1)
                ret_o(h)
            pe.wait_ge(S("ro_squared"), 1)
            for b in range(4):
                last = pe.matmul(ps[:, b, :], ones, tmp[:, 2 * b:2 * b + 2, :].rearrange("p c t -> p (c t)"), start=True, stop=True)
            last.then_inc(S("ro_summed"), 1)
            pe.wait_ge(S("m_squared"), 1)
            pe.wait_ge(S("ro_var"), 1)
            for b in range(4):
                last = pe.matmul(ps[:, b, :], rot[:, P + 2 * SEQ:2 * P + 2 * SEQ], tmp[:, 2 * b:2 * b + 2, :].rearrange("p c t -> p (c t)"), start=True, stop=True)
            last.then_inc(S("m_summed"), 1)
            pe.wait_ge(S("mk_normed"), 1)
            pe.wait_ge(S("bias_in"), 16 * MH * TT)
            for n in range(4):
                t, hg = n // 2, n % 2
                W = (t + 1) * P
                if n >= 2:
                    pe.wait_ge(S("m_exp"), 4 * (n - 1))
                for h in range(4):
                    hh = 4 * hg + h
                    r = slice(64 * (hh % 2), 64 * (hh % 2) + 64)
                    o = ps[:, 2 * (n % 2) + h % 2, (h // 2) * SEQ:(h // 2) * SEQ + W]
                    pe.matmul(o, proj2[r, C_MQ + hh // 2, t * P:(t + 1) * P], proj2[r, C_MK + hh // 2, 0:W], start=True, stop=False)
                    last = pe.matmul(o, rot[:, 2 * P + 2 * SEQ:3 * P + 2 * SEQ], bias[:, t, hh, 0:W], start=False, stop=True)
                last.then_inc(S("m_s"), 1)
                pe.wait_ge(S("m_p"), n + 1)
                if n >= 2:
                    pe.wait_ge(S("m_lo"), n - 1)
                for h in range(4):
                    m, hh = 4 * n + h, 4 * hg + h
                    if m >= 2:
                        pe.wait_ge(S("m_pt"), m - 1)
                    for u in range(t + 1):
                        last = pe.transpose(ps[:, 4 + m % 2, u * P:(u + 1) * P], sp2[:, h, u * P:(u + 1) * P], ident)
                    last.then_inc(S("m_tr"), 1)
                    pe.wait_ge(S("m_pt"), m + 1)
                    r = 64 * (hh % 2)
                    for u in range(t + 1):
                        last = pe.matmul(ps[r:r + 64, 6 + n % 2, (h // 2) * P:(h // 2 + 1) * P], vtok2[:, u, 1024 + hh * MD:1024 + (hh + 1) * MD],
                                         pt2[:, m % 2, u * P:(u + 1) * P], start=u == 0, stop=u == t)
                last.then_inc(S("m_o"), 1)
            pe.wait_ge(S("m_lo"), 4)
            tiles(pe, "retw", segment_T(pe, "retw", hhi, hlo, "ya_kept"))
            pe.wait_ge(S("ya_kept"), KC)
            tiles(pe, "mobw", segment_T(pe, "mobw", mbhi, mblo, "yb_kept", nk=4))
            pe.wait_ge(S("merged_lo"), 1)
            new_x("out2", 3, 2 * KC)

            tiles(pe, "pq", segment_T(pe, "pq", hhi, hlo, "q_lo", norm=3))
            pe.wait_ge(S("q_lo"), 16)

            def subk(i, j):
                g = BASE["subk"] + j
                pe.wait_ge(lo_made, nth(g))
                for t in range(TT):
                    for c in range(8):
                        s, w = slice(t * P, (t + 1) * P), slice(c * P, (c + 1) * P)
                        o = ps[:, 4 * j + 2 * t + c // 4, (c % 4) * P:(c % 4 + 1) * P]
                        pe.matmul(o, qhi[:, 8 * j + c, s], whi[:, g % RING, w], start=True, stop=False)
                        pe.matmul(o, qlo[:, 8 * j + c, s], whi[:, g % RING, w], start=False, stop=False)
                        last = pe.matmul(o, qhi[:, 8 * j + c, s], wlo[:, g % RING, w], start=False, stop=True)
                last.then_inc(tile_used, 1)
            tiles(pe, "subk", subk, loop=False)
            pe.wait_ge(S("scores_kept"), 2 * TT)
            pre = segment_T(pe, "u", hhi, hlo, "g_made")
            tiles(pe, "u", pre, 0, 104)
            pe.wait_ge(S("gates_made"), 1)
            for n in range(3):
                for t in range(TT):
                    s = ctop[:, t * PH:(t + 1) * PH, :] if n == 2 else pidx[:, n, t * PH:(t + 1) * PH, :]
                    last = pe.transpose(ps[:, 3 + n, t * P:(t + 1) * P], s.rearrange("p h k -> p (h k)"), ident)
            last.then_inc(S("pairs_turned"), 1)
            tiles(pe, "u", pre, 104, 128)

            def outer(i, q):
                pe.wait_ge(S("e1_made"), 2 * i + (q + 1))
                pe.wait_ge(S("e2_made"), 2 * i + (q + 1))
                wait(pe, S("outer_multiplied"), 2 * i + (q - 1))
                for a in range(4):
                    last = pe.matmul(ps[:, 4 + q % 2, a * P:(a + 1) * P], e1[:, q % 2, a, :], e2[:, q % 2, a, :], start=True, stop=True)
                last.then_inc(S("outer_made"), 1)
            outer(0, 0)
            outer(0, 1)
            with pe.Fori(0, SEQ // 8 - 1) as i:
                outer(i, 2)
                outer(i, 3)
            for t in range(TT):
                for c in range(KC):
                    pe.matmul(ps[:, 2 * t + c // 4, (c % 4) * P:(c % 4 + 1) * P], x[:, c, t * P:(t + 1) * P], ident, start=c % 4 == 0, stop=False, skip_group_check=True)

            def vals(i, j):
                g = BASE["v"] + j
                pe.wait_ge(lo_made, 4 * i + nth(g))
                pe.wait_ge(S("mlo_made"), 4 * i + (j + 1))
                for t in range(TT):
                    for n in range(2):
                        o, s, w = ps[:, 2 * t + n, :], slice(t * P, (t + 1) * P), slice(n * 512, n * 512 + 512)
                        stop = isinstance(i, int) and j == NKEY - 1
                        pe.matmul(o, mhi[:, g % RING, s], whi[:, g % RING, w], start=False, stop=False, skip_group_check=True)
                        pe.matmul(o, mhi[:, g % RING, s], wlo[:, g % RING, w], start=False, stop=False, skip_group_check=True)
                        last = pe.matmul(o, mlo[:, g % RING, s], whi[:, g % RING, w], start=False, stop=stop, skip_group_check=True)
                last.then_inc(tile_used, 1)
            tiles(pe, "v", vals)

        @block.scalar
        def _(act):
            steps = [0]

            def link(ins):
                steps[0] += 1
                ins.then_inc(S("act_step"), 1)
                act.wait_ge(S("act_step"), steps[0])

            def hi_only(name):
                return lambda i, j: split_hi(act, BASE[name] + j + LEAD, i)

            def norm_square(k, c):
                if k:
                    act.wait_ge(S("x_new"), KC * (k - 1) + c + 1)
                act.activation(tmp[:, c, :], x[:, c, :], ACT.Square).then_inc(S("norm_squared"), 1)

            def norm_squares(k):
                for c in range(KC):
                    norm_square(k, c)

            def new_x(name, k):
                def body(i, j):
                    split_hi(act, BASE[name] + j + LEAD)
                    if j:
                        norm_square(k, j - 1)
                tiles(act, name, body)
                norm_square(k, KC - 1)

            def norm_root(k):
                act.wait_ge(S("norm_summed"), k + 1)
                link(act.activation(rs[:, 0, :], ps[:, 4, 0:SEQ], ACT.Ln, bias=epsc[:, :], scale=1.0 / D))
                act.activation(rs[:, 0, :], rs[:, 0, :], ACT.Exp, scale=-0.5).then_inc(S("norm_root"), 1)

            def norm_out(k):
                for c in range(KC):
                    act.wait_ge(S("norm_scaled"), KC * k + c + 1)
                    act.activation(hhi[:, c, :], tmp[:, c, :], ACT.Identity, bias=shifts[:, k, c:c + 1]).then_inc(S("h_hi"), 1)

            act.wait_ge(S("prm_in"), 32)
            act.activation(csl[:, :], prm[:, 96:104], ACT.Silu).then_inc(S("c_silu"), 1)
            act.wait_ge(S("x_in"), 16)
            norm_squares(0)
            act.wait_ge(S("eps_made"), 1)
            norm_root(0)
            for g in range(LEAD):
                split_hi(act, RAW1 + g)
            norm_out(0)

            def win(i, j):
                g = BASE["win"] + j
                split_hi(act, g + LEAD, i)
                act.wait_ge(tile_used, 4 * i + nth(g))
                act.activation(pick(proj, 4 * i + j), chunk_bank(g), ACT.Copy).then_inc(S("win_kept"), 1)
            tiles(act, "win", win)
            act.wait_ge(S("h_lo"), KC)
            for c in range(KC):
                last = act.activation(tmp[:, c, :], tmp[:, c, :], ACT.Identity, bias=shifts[:, 0, c:c + 1])
                if c % 4 == 3:
                    split_hi(act, BASE["tok"] + c // 4 + LEAD)
            last.then_inc(S("h_made"), 1)
            act.wait_ge(tile_used, nth(BASE["tok"] + 1))
            for t in range(TT):
                act.activation(vtok[:, t, :], ps[:, 4 + t, 0:256], ACT.Copy).then_inc(S("vtok_made"), 1)
            act.wait_ge(S("small_made"), 1)
            act.activation(small[:, :, :], ps[:, 3, 0:64].rearrange("p (t c) -> p t c", t=2)[:, :, 0:20], ACT.Copy).then_inc(S("small_kept"), 1)
            act.wait_ge(S("blk_made"), 1)
            act.activation(bhi[:, :, :, :].rearrange("p a b c -> p (a b c)"), blk[:, :, :, :].rearrange("p a b c -> p (a b c)"), ACT.Copy).then_inc(S("blk_hi"), 1)

            def cmp(i, j):
                split_hi(act, BASE["cmp"] + j + LEAD)
                if j == 1:
                    act.wait_ge(S("conv_tap"), 4 * CONV)
                    act.activation(proj[:, 0:CONV, :], cv[:, :, :], ACT.Silu).then_inc(S("conv_silu"), 1)
                if j == 3:
                    act.activation(proj[:, C_GZ:C_GZ + 4, :], proj[:, C_GZ:C_GZ + 4, :], ACT.Silu).then_inc(S("conv_silu"), 1)
                if j == 5:
                    act.wait_ge(S("conv_silu"), 2)
                    act.activation(sq[:, 0:8 * SEQ], proj[:, 0:8, :].rearrange("p c t -> p (c t)"), ACT.Square).then_inc(S("heads_squared"), 1)
                if j == 7:
                    act.activation(sq[:, 8 * SEQ:14 * SEQ], proj[:, C_NQ:C_NQ + 6, :].rearrange("p c t -> p (c t)"), ACT.Square).then_inc(S("heads_squared"), 1)
            tiles(act, "cmp", cmp)
            act.wait_ge(tile_used, nth(BASE["cmp"] + 7))
            act.activation(hid[:, :, :], ps[:, 0:2, 0:CPAD], ACT.Silu).then_inc(S("hid_made"), 1)
            act.wait_ge(S("cmp_made"), 1)
            link(act.activation(kc[:, :], ps[:, 2, 0:CPAD], ACT.Copy))
            act.activation(sqc[:, :], kc[:, :], ACT.Square).then_inc(S("cmp_squared"), 1)
            act.activation(vc[0:CPAD, :], ps[0:CPAD, 2, P:2 * P], ACT.Copy).then_inc(S("vc_made"), 1)
            act.wait_ge(S("heads_summed"), 1)
            act.wait_ge(S("eps_made"), 1)
            act.activation(rs[:, 0:8, :].rearrange("p a b -> p (a b)"), bank(0, 4), ACT.Ln, bias=epsc[:, :])
            act.activation(rsc[:, :], ps[:, 7, 0:CPAD], ACT.Ln, bias=epsc[:, :], scale=1.0 / HEAD)
            link(act.activation(rs[:, 8:14, :].rearrange("p a b -> p (a b)"), bank(4, 3), ACT.Ln, bias=epsc[:, :], scale=1.0 / HEAD))
            act.activation(rsc[:, :], rsc[:, :], ACT.Exp, scale=-0.5)
            act.activation(rs[:, :, :], rs[:, :, :], ACT.Exp, scale=-0.5).then_inc(S("heads_root"), 1)
            act.wait_ge(S("z_made"), 1)
            link(act.activation(gsm[:, 16:24], gsm[:, 16:24], ACT.Exp, scale=-1.0))
            link(act.activation(gsm[:, 16:24], gsm[:, 16:24], ACT.Ln, bias=1.0))
            act.activation(gsm[:, 24:28], prm[:, 89:93], ACT.Exp)
            act.activation(small[:, :, 4:20], small[:, :, 4:20], ACT.Exp, scale=-1.0).then_inc(S("gates_exp"), 1)
            act.wait_ge(S("diff_made"), 1)
            act.activation(DT[:, :, :], DT[:, :, :], ACT.Exp).then_inc(S("DT_exp"), 1)
            act.wait_ge(S("sums_kept"), 1)
            act.activation(gsm[:, 40:48], gsm[:, 32:40], ACT.Exp)
            for h in range(GH):
                act.activation(gsm[:, 48 + h:49 + h], gsm[:, 32 + h:33 + h], ACT.Exp, bias=gcB[:, h, P - 1:P], scale=-1.0)
            act.activation(eg[:, :, :], gcB[:, 4:8, :], ACT.Exp).then_inc(S("eg_made"), 1)
            act.wait_ge(S("kk_made"), 1)
            act.activation(vb[:, :, :].rearrange("p a b -> p (a b)"), bank(6, 2), ACT.Copy).then_inc(S("vt_kept"), 1)
            for l in range(LEVELS):
                for b in range(2):
                    act.wait_ge(S("inv_x"), 2 * l + b + 1)
                    if l:
                        act.wait_ge(S("inv_y"), 2 * (l - 1) + b + 1)
                    act.activation(Xs[:, 4 * b:4 * b + 4, :].rearrange("p a b -> p (a b)"), bank(b), ACT.Copy).then_inc(S("inv_xs"), 1)
            act.wait_ge(S("uw_made"), 1)
            act.activation(wT[:, :, :].rearrange("p a b -> p (a b)"), bank(2), ACT.Copy)
            act.activation(U[:, :, :].rearrange("p a b -> p (a b)"), bank(0, 2), ACT.Copy).then_inc(S("uw_kept"), 1)
            act.wait_ge(S("state_made"), 1)
            act.activation(St[:, :, :].rearrange("p a b -> p (a b)"), bank(3), ACT.Copy).then_inc(S("state_kept"), 1)
            act.wait_ge(S("og_made"), 1)
            link(act.activation(og[:, :, 0:P], ps[:, 5, :].rearrange("p (h t) -> p h t", h=GH), ACT.Copy))
            link(act.activation(og[:, :, P:SEQ], ps[:, 6, :].rearrange("p (h t) -> p h t", h=GH), ACT.Copy))
            act.activation(ogsq[:, :], og[:, :, :].rearrange("p h t -> p (h t)"), ACT.Square).then_inc(S("og_squared"), 1)
            act.wait_ge(S("og_summed"), 1)
            link(act.activation(rs[:, 0:4, :].rearrange("p a b -> p (a b)"), bank(0, 2), ACT.Ln, bias=epsc[:, :], scale=1.0 / HEAD))
            act.activation(rs[:, 0:4, :], rs[:, 0:4, :], ACT.Exp, scale=-0.5).then_inc(S("og_root"), 1)
            for g in range(LEAD):
                split_hi(act, BASE["wout"] + g)
            act.wait_ge(S("og_done"), 1)
            act.activation(hhi[:, 0:4, :], og[:, :, :], ACT.Copy).then_inc(S("og_hi"), 1)
            for t in range(TT):
                W = (t + 1) * P
                act.wait_ge(S("nsa_max"), t + 1)
                for h in range(NH):
                    for kk in range(2):
                        act.activation(sp_[:, h, kk * 256:kk * 256 + W], sp_[:, h, kk * 256:kk * 256 + W], ACT.Exp,
                                       bias=nst[:, 2 * h + kk:2 * h + kk + 1], accum_out=nst[:, 16 + 2 * h + kk:17 + 2 * h + kk])
                    act.activation(spc[:, h, :], spc[:, h, :], ACT.Exp, bias=nst[:, 8 + h:9 + h], accum_out=nst[:, 24 + h:25 + h]).then_inc(S("nsa_exp"), 1)
                for h in range(NH):
                    m = 4 * t + h
                    act.wait_ge(S("nsa_tr"), m + 1)
                    z = 5 if m % 2 == 0 else 6
                    act.activation(pt[:, m % 2, 0:2 * W], ps[:, z, 0:2 * W], ACT.Copy)
                    act.activation(ptc[0:CPAD, m % 2, :], ps[0:CPAD, 4, P + (m % 2) * P:P + (m % 2 + 1) * P], ACT.Copy).then_inc(S("nsa_pt"), 1)
                act.wait_ge(S("nsa_o"), t + 1)
                act.activation(hhi[:, 4:8, t * P:(t + 1) * P], ps[:, 7, :].rearrange("p (h q) -> p h q", h=NH), ACT.Copy).then_inc(S("mix_hi"), 1)
            act.wait_ge(S("mix_lo"), TT)
            new_x("wout", 1)
            norm_root(1)
            norm_out(1)

            def up(i, j):
                g, m = BASE["up"] + j, j // 2
                split_hi(act, g + LEAD, i)
                act.wait_ge(tile_used, 4 * i + nth(g))
                wait(act, S("up_used"), 2 * i + (m - 1))
                w = pick(upc, 4 * i + j)
                act.activation(uc[:, j % 4, :], chunk_bank(g), ACT.Identity, bias=w[:, 3:4], scale=w[:, 2:3]).then_inc(S("up_scaled"), 1)
                if j % 2:
                    act.wait_ge(S("up_kept"), 4 * i + j)
                    act.activation(uc[:, j % 4 - 1, :], uc[:, j % 4 - 1, :], ACT.Silu).then_inc(S("up_silu"), 1)
                    if j > 1:
                        act_hi(i, m - 1)

            def act_hi(i, m):
                act.wait_ge(S("up_used"), 2 * i + (m + 1))
                act.activation(pick(ahi, 2 * i + m), upp[:, m % 2, :], ACT.Copy).then_inc(S("act_hi"), 1)

            act.wait_ge(S("up_in"), 16)
            act.wait_ge(S("zf_made"), 1)
            act.activation(zz[:, :], zf[:, :], ACT.Copy).then_inc(S("zeros_made"), 1)
            tiles(act, "up", up)
            act_hi(0, FC - 1)
            tiles(act, "down", hi_only("down"))
            norm_squares(2)
            norm_root(2)
            norm_out(2)

            act.wait_ge(S("line_psum"), 1)
            act.activation(line[:, :], ps[0:MH, 5, :], ACT.Copy).then_inc(S("line_made"), 1)

            def in2(i, j):
                g = BASE["in2"] + j
                split_hi(act, g + LEAD, i)
                act.wait_ge(tile_used, 4 * i + nth(g))
                act.activation(pick(proj2, 4 * i + j), chunk_bank(g), ACT.Copy).then_inc(S("in2_kept"), 1)
            tiles(act, "in2", in2)

            def tok2(i, j):
                split_hi(act, BASE["tok2"] + j + LEAD)
                if j % 4 == 3:
                    n = j // 4
                    act.wait_ge(tile_used, nth(BASE["tok2"] + j))
                    for t in range(TT):
                        act.activation(vtok2[:, t, n * 512:(n + 1) * 512], ps[:, 2 * (n % 2) + t, :], ACT.Copy).then_inc(S("tok2_kept"), 1)
            tiles(act, "tok2", tok2, loop=False)
            act.activation(proj2[:, C_RG:C_RG + 8, :], proj2[:, C_RG:C_RG + 8, :], ACT.Silu).then_inc(S("rg_silu"), 1)
            act.activation(proj2[:, C_GA:C_GA + 16, :], proj2[:, C_GA:C_GA + 16, :], ACT.Sigmoid).then_inc(S("ab_sig"), 1)
            for h in range(RH):
                act.wait_ge(S("ret_o"), h + 1)
                act.activation(ro[:, h, :], ps[:, 2 + h % 2, 0:SEQ], ACT.Copy).then_inc(S("ro_kept"), 1)
            act.wait_ge(S("ro_kept"), RH)
            act.activation(tmp[:, :, :], ro[:, :, :], ACT.Square).then_inc(S("ro_squared"), 1)
            act.wait_ge(S("ro_summed"), 1)
            act.activation(rs[:, 0:8, :].rearrange("p a b -> p (a b)"), bank(0, 4), ACT.Ln, bias=prm2[:, 3:4], scale=1.0 / RV).then_inc(S("ro_var"), 1)
            act.wait_ge(S("ro_var"), 1)
            act.activation(rs[:, 0:8, :], rs[:, 0:8, :], ACT.Exp, scale=-0.5).then_inc(S("ro_root"), 1)
            act.wait_ge(S("ro_done"), 1)
            act.activation(hhi[:, :, :], ro[:, :, :], ACT.Copy).then_inc(S("ro_hi"), 1)
            act.activation(tmp[:, :, :], proj2[:, C_MQ:C_MQ + 8, :], ACT.Square).then_inc(S("m_squared"), 1)
            act.wait_ge(S("m_summed"), 1)
            link(act.activation(rs[:, 0:8, :].rearrange("p a b -> p (a b)"), bank(0, 4), ACT.Ln, bias=prm2[:, 3:4], scale=1.0 / MD))
            act.activation(rs[:, 0:8, :], rs[:, 0:8, :], ACT.Exp, scale=-0.5).then_inc(S("m_root"), 1)
            for n in range(4):
                t, hg = n // 2, n % 2
                W = (t + 1) * P
                act.wait_ge(S("m_max"), n + 1)
                if n:
                    act.wait_ge(S("m_tr"), 4 * n)
                for h in range(4):
                    act.activation(sp2[:, h, 0:W], ps[:, 2 * (n % 2) + h % 2, (h // 2) * SEQ:(h // 2) * SEQ + W], ACT.Exp, bias=mst[:, h:h + 1], accum_out=mst[:, 4 + h:5 + h]).then_inc(S("m_exp"), 1)
                for h in range(4):
                    m = 4 * n + h
                    act.wait_ge(S("m_tr"), m + 1)
                    act.activation(pt2[:, m % 2, 0:W], ps[:, 4 + m % 2, 0:W], ACT.Copy).then_inc(S("m_pt"), 1)
                act.wait_ge(S("m_o"), n + 1)
                act.activation(mbhi[:, 2 * hg:2 * hg + 2, t * P:(t + 1) * P], ps[:, 6 + n % 2, 0:2 * P].rearrange("p (c q) -> p c q", c=2), ACT.Copy).then_inc(S("m_hi"), 1)
            tiles(act, "retw", hi_only("retw"))
            tiles(act, "mobw", hi_only("mobw"))
            act.wait_ge(S("merged"), 1)
            act.activation(hhi[:, :, :], ya[:, :, :], ACT.Copy).then_inc(S("merged_hi"), 1)
            new_x("out2", 3)
            norm_root(3)
            norm_out(3)

            def pq(i, j):
                g = BASE["pq"] + j
                split_hi(act, g + LEAD, i)
                act.wait_ge(tile_used, 4 * i + nth(g))
                act.activation(pick(qhi, 4 * i + j), chunk_bank(g), ACT.Copy).then_inc(S("q_hi"), 1)
            tiles(act, "pq", pq)

            def subk(i, j):
                split_hi(act, BASE["subk"] + j + LEAD)
                act.wait_ge(tile_used, nth(BASE["subk"] + j))
                for t in range(TT):
                    act.activation(sc[:, t * 16 + 8 * j:t * 16 + 8 * j + 8, :].rearrange("p a b -> p (a b)"), bank(4 * j + 2 * t, 2), ACT.Copy).then_inc(S("scores_kept"), 1)
            tiles(act, "subk", subk, loop=False)

            def exps(i, j):
                g = BASE["u"] + j
                split_hi(act, g + LEAD, i)
                act.wait_ge(tile_used, 4 * i + nth(g))
                act.activation(pick(G, 4 * i + j), chunk_bank(g), ACT.Gelu).then_inc(S("g_made"), 1)
            tiles(act, "u", exps, 0, 100)
            act.wait_ge(S("gate_shifted"), 1)
            act.activation(ctop[:, :, :], ctop[:, :, :], ACT.Exp).then_inc(S("gate_exp"), 1)
            tiles(act, "u", exps, 100, 104)
            act.wait_ge(S("routed"), 1)
            tiles(act, "u", exps, 104, 128)
            def distances(i, q):
                for a in range(4):
                    tok = 4 * q + a if isinstance(i, int) else 16 * i + (4 * q + a)
                    act.activation(dist[:, q % 4, a, :], iota, ACT.Abs, bias=col(pair[:, 0, :], tok), scale=-1.0).then_inc(S("dist_made"), 1)

            def first_rows(i, q):
                if q + 1 < SEQ // 4:
                    distances(i, q + 1)
                act.wait_ge(S("dist_made"), 16 * i + 4 * (q + 1))
                wait(act, S("outer_made"), 4 * i + (q - 1))
                act.activation(e1[:, q % 2, :, :], dist[:, q % 4, :, :], ACT.Relu, bias=1.0, scale=-1.0).then_inc(S("e1_made"), 1)
            act.wait_ge(tile_used, nth(BASE["v"] - 1))
            distances(0, 0)
            for q in range(4):
                first_rows(0, q)
            with act.Fori(0, SEQ // 16 - 2) as i:
                for q in range(4, 8):
                    first_rows(i, q)
            for q in range(SEQ // 4 - 4, SEQ // 4):
                first_rows(0, q)
            act.wait_ge(S("outer_multiplied"), SEQ // 4)

            def m_hi(i, j):
                if j < NKEY:
                    act.activation(mhi[:, (BASE["v"] + j) % RING, :], pick(G, 4 * i + j), ACT.Copy).then_inc(S("mhi_made"), 1)
            for j in range(LEAD):
                m_hi(0, j)

            def vals(i, j):
                split_hi(act, BASE["v"] + j + LEAD, i)
                m_hi(i, j + LEAD)
            tiles(act, "v", vals)
            act.wait_ge(tile_used, nth(TOTAL - 1))
            for t in range(TT):
                act.activation(y[:, t, :], bank(2 * t, 2), ACT.Copy).then_inc(S("y_made"), 1)

        @block.vector
        def _(dve):
            steps = [0]

            def link(ins):
                steps[0] += 1
                ins.then_inc(S("dve_step"), 1)
                dve.wait_ge(S("dve_step"), steps[0])

            def lo_only(name):
                return lambda i, j: split_lo(dve, BASE[name] + j + LEAD, i)

            def over(t, n):
                return t.rearrange("p (o t) -> p o t", o=1).to_broadcast([P, n, t.shape[-1]])

            def flat(t):
                return t.rearrange("p a b -> p (a b)")

            def norm(k):
                dve.wait_ge(S("norm_root"), k + 1)

                def lower(c):
                    dve.wait_ge(S("h_hi"), KC * k + c + 1)
                    dve.scalar_tensor_tensor(hlo[:, c, :], tmp[:, c, :], shifts[:, k, c:c + 1], hhi[:, c, :].bitcast(f32), add, sub).then_inc(S("h_lo"), 1)
                for c in range(KC):
                    dve.scalar_tensor_tensor(tmp[:, c, :], x[:, c, :], gains[:, k, c:c + 1], rs[:, 0, :], mul, mul).then_inc(S("norm_scaled"), 1)
                    if c >= 2:
                        lower(c - 2)
                lower(KC - 2)
                lower(KC - 1)

            dve.memset(shifts[:, :, :], 0.0)
            dve.memset(blk[:, :, :, :], 0.0)
            dve.memset(epsc[:, :], EPS).then_inc(S("eps_made"), 1)
            dve.wait_ge(S("c_silu"), 1)
            def ada(g0, count):
                for r in range(g0, g0 + count):
                    n, k, g = r // KC, r % KC, r if r < RAW1 else BASE["ada2"] + r - RAW1
                    dve.wait_ge(w_loaded[g % RING], 16 * (g // RING + 1))
                    ways = 2 if n < 2 else 1
                    o = acc[:, n, k % 2, :] if n < 2 else acc2[:, n % 2, :]
                    if k < ways:
                        if n >= 4 and k == 0:
                            dve.wait_ge(S("mod_summed"), n - 1)
                        dve.tensor_scalar(o, raw[:, g % RING, :], csl[:, k:k + 1], None, mul).then_inc(raw_used, 1)
                    else:
                        dve.wait_ge(raw_used, r + 1 - ways)
                        dve.scalar_tensor_tensor(o, raw[:, g % RING, :], csl[:, k:k + 1], o, mul, add).then_inc(raw_used, 1)
            ada(0, RAW1)
            def factors(k, o, source):
                link(dve.tensor_tensor(mod[:, o], source, prm[:, 104 + o.start:104 + o.stop], add))
                dve.scalar_tensor_tensor(gains[:, k, :], mod[:, 24 * k + 8:24 * k + 16], 1.0, prm[:, 8 * k:8 * k + 8], add, mul)
                dve.tensor_copy(shifts[:, k, :], mod[:, 24 * k:24 * k + 8])
                dve.tensor_copy(gains[:, 2 + k, :], prm[:, 16 + 8 * k:24 + 8 * k])
            dve.wait_ge(S("mod_summed"), 2)
            factors(0, slice(0, 16), ps[:, 1, 0:16])
            link(dve.memset(gsm[:, :], 0.0))
            for g in range(LEAD):
                split_lo(dve, RAW1 + g)
            norm(0)

            def conv(i, j):
                dve.wait_ge(S("win_kept"), 4 * i + (j + 1))
                src, o = pick(proj, 4 * i + j), pick(cv, 4 * i + j)
                w = pick(prm[:, 32:80].rearrange("p (n t) -> p n t", t=4), 4 * i + j)
                dve.tensor_scalar(o, src, w[:, 3:4], None, mul).then_inc(S("conv_tap"), 1)
                for tap in range(1, 4):
                    dve.wait_ge(S("conv_tap"), 16 * i + (4 * j + tap))
                    dve.scalar_tensor_tensor(o[:, tap:SEQ], src[:, 0:SEQ - tap], w[:, 3 - tap:4 - tap], o[:, tap:SEQ], mul, add).then_inc(S("conv_tap"), 1)

            def win(i, j):
                split_lo(dve, BASE["win"] + j + LEAD, i)
                if j:
                    conv(i, j - 1)
            tiles(dve, "win", win, 0, CONV)
            conv(0, CONV - 1)
            tiles(dve, "win", lo_only("win"), CONV)
            tiles(dve, "tok", lo_only("tok"))
            dve.wait_ge(S("win_kept"), 24)
            for kv in range(2):
                src = proj[:, C_KC + kv, :]
                span = bass.AP(tensor=src.tensor, offset=src.offset, ap=[src.ap[0], [1, CMP_BLOCK], [CMP_STRIDE, N_CMP]])
                pos = prm[:, 152 + 32 * kv:184 + 32 * kv].rearrange("p (l o) -> p l o", o=1).to_broadcast([P, CMP_BLOCK, N_CMP])
                last = dve.tensor_tensor(blk[:, kv, :, 0:N_CMP], span, pos, add)
            last.then_inc(S("blk_made"), 1)
            dve.wait_ge(S("blk_hi"), 1)
            dve.tensor_tensor(flat(blo[:, :, :, :].rearrange("p a b c -> p a (b c)")), flat(blk[:, :, :, :].rearrange("p a b c -> p a (b c)")), flat(bhi[:, :, :, :].rearrange("p a b c -> p a (b c)")).bitcast(f32), sub).then_inc(S("blk_lo"), 1)
            tiles(dve, "cmp", lo_only("cmp"))
            dve.wait_ge(S("small_kept"), 1)
            for t in range(TT):
                last = dve.tensor_tensor(gsm[:, 4 * t:4 * t + 4], small[:, t, 0:4], prm[:, 85:89], add)
            link(last)
            dve.tensor_scalar(gsm[:, 56:64], gsm[:, 0:8], 0.0, None, ALU.max)
            link(dve.tensor_scalar(gsm[:, 64:72], gsm[:, 0:8], -1.0, None, mul))
            dve.tensor_tensor(gsm[:, 16:24], gsm[:, 0:8], gsm[:, 64:72], ALU.max).then_inc(S("z_made"), 1)
            ada(RAW1, 10)
            dve.wait_ge(S("heads_root"), 1)
            dve.wait_ge(S("conv_silu"), 2)
            root = float(HEAD) ** -0.5
            dve.scalar_tensor_tensor(flat(proj[:, 0:4, :]), flat(proj[:, 0:4, :]), root, flat(rs[:, 0:4, :]), mul, mul)
            dve.tensor_tensor(flat(proj[:, 4:8, :]), flat(proj[:, 4:8, :]), flat(rs[:, 4:8, :]), mul)
            link(dve.scalar_tensor_tensor(flat(proj[:, C_NQ:C_NQ + 4, :]), flat(proj[:, C_NQ:C_NQ + 4, :]), prm[:, 81:82], flat(rs[:, 8:12, :]), mul, mul))
            link(dve.tensor_scalar(flat(proj[:, C_NQ:C_NQ + 4, :]), flat(proj[:, C_NQ:C_NQ + 4, :]), root, None, mul))
            dve.scalar_tensor_tensor(proj[:, C_KS, :], proj[:, C_KS, :], prm[:, 83:84], rs[:, 12, :], mul, mul)
            dve.scalar_tensor_tensor(proj[:, C_KW, :], proj[:, C_KW, :], prm[:, 84:85], rs[:, 13, :], mul, mul)
            dve.scalar_tensor_tensor(kc[:, :], kc[:, :], prm[:, 82:83], rsc[:, :], mul, mul)
            dve.wait_ge(S("gates_exp"), 1)
            link(dve.tensor_scalar(small[:, :, 4:20], small[:, :, 4:20], 1.0, None, add))
            link(dve.reciprocal(small[:, :, 4:20], small[:, :, 4:20]))
            link(dve.tensor_tensor(gsm[:, 56:64], gsm[:, 56:64], gsm[:, 16:24], add))
            for t in range(TT):
                dve.scalar_tensor_tensor(gsm[:, 4 * t:4 * t + 4], gsm[:, 56 + 4 * t:60 + 4 * t], -1.0, gsm[:, 24:28], mul, mul)
                last = dve.tensor_copy(gsm[:, 8 + 4 * t:12 + 4 * t], small[:, t, 4:8])
            last.then_inc(S("decay_made"), 1)
            dve.wait_ge(S("sums_made"), 1)
            dve.tensor_copy(flat(gcB[:, :, :]), bank(0, 2))
            dve.tensor_copy(gsm[:, 32:40], ps[:, 4, 0:8]).then_inc(S("sums_kept"), 1)
            for t in range(TT):
                last = dve.tensor_tensor(kbT[:, :, t * P:(t + 1) * P], ps[:, 2 + t, :].rearrange("p (h c) -> p h c", h=GH), proj[:, 4:8, t * P:(t + 1) * P], mul)
            last.then_inc(S("kbT_made"), 1)
            dve.wait_ge(S("sums_kept"), 1)
            for p in range(8):
                last = dve.tensor_scalar(DT[:, p, :], gcB[:, p, :], gsm[:, 32 + p:33 + p], 0.0, sub, ALU.min)
            last.then_inc(S("diff_made"), 1)
            for t in (Tm, TTm):
                last = dve.tensor_copy(t[:, :, :], over(ident, 8))
            dve.wait_ge(S("DT_exp"), 1)
            link(dve.tensor_tensor(DT[:, :, :], DT[:, :, :], over(tri, 8), mul))
            dve.wait_ge(S("kk_made"), 1)
            dve.tensor_tensor(flat(QT[:, :, :]), flat(DT[:, :, :]), bank(2, 2), mul)
            link(dve.tensor_tensor(flat(AT[:, :, :]), flat(DT[:, :, :]), bank(0, 2), mul))

            def masked(l):
                for b in range(2):
                    if l:
                        dve.wait_ge(S("inv_x"), 2 * (l - 1) + b + 1)
                    dve.tensor_tensor(BT[:, 4 * b:4 * b + 4, :], AT[:, 4 * b:4 * b + 4, :], over(lvl[:, l, :], 4), mul).then_inc(S("lvl_masked"), 1)
            masked(0)
            dve.wait_ge(S("eg_made"), 1)
            link(dve.tensor_tensor(gsm[:, 52:56], gsm[:, 12:16], gsm[:, 44:48], mul))
            dve.tensor_tensor(qd[:, :, :], proj[:, 0:4, P:SEQ], eg[:, :, :], mul)
            dve.wait_ge(S("vt_kept"), 1)
            for p in range(8):
                h = p % 4
                dve.tensor_scalar(vb[:, p, :], vb[:, p, :], gsm[:, 8 + p:9 + p], None, mul)
                f = 52 + h if p >= 4 else 48 + h
                last = dve.tensor_scalar(kw[:, p, :], ps[:, 4 + p // 4, h * P:(h + 1) * P], gsm[:, f:f + 1], None, mul)
            last.then_inc(S("kv_scaled"), 1)
            for l in range(LEVELS):
                if l + 1 < LEVELS:
                    masked(l + 1)
                for b in range(2):
                    ada(RAW1 + 10 + 2 * l + b, 1)
                    dve.wait_ge(S("inv_y"), 2 * l + b + 1)
                    o = slice(4 * b, 4 * b + 4)
                    dve.tensor_tensor(flat(Tm[:, o, :]), flat(Tm[:, o, :]), bank(2 + b), sub)
                    dve.tensor_tensor(flat(TTm[:, o, :]), flat(TTm[:, o, :]), bank(4 + b), sub).then_inc(S("inv_updated"), 1)
            ada(RAW1 + 24, 2)
            dve.wait_ge(S("uw_kept"), 1)
            dve.wait_ge(S("ws_made"), 1)
            dve.tensor_tensor(flat(U[:, 4:8, :]), flat(U[:, 4:8, :]), bank(4), sub).then_inc(S("vnew_made"), 1)
            ada(RAW1 + 26, 6)
            dve.wait_ge(S("og_root"), 1)
            link(dve.scalar_tensor_tensor(flat(og[:, :, :]), flat(og[:, :, :]), prm[:, 80:81], flat(rs[:, 0:4, :]), mul, mul))
            dve.tensor_tensor(og[:, :, :], og[:, :, :], proj[:, C_GZ:C_GZ + 4, :], mul).then_inc(S("og_done"), 1)
            dve.wait_ge(S("mod_summed"), 6)
            factors(1, slice(16, 48), ps[:, 7, 0:32])
            for g in range(LEAD):
                split_lo(dve, BASE["wout"] + g)
            dve.wait_ge(S("og_hi"), 1)
            dve.tensor_tensor(hlo[:, 0:4, :], og[:, :, :], hhi[:, 0:4, :].bitcast(f32), sub).then_inc(S("og_lo"), 1)

            for t in range(TT):
                W = (t + 1) * P
                dve.wait_ge(S("nsa_s"), t + 1)
                for h in range(NH):
                    for kk in range(2):
                        a = kk * 256
                        if t:
                            dve.tensor_copy(sp_[:, h, a:a + P], ps[:, h, a:a + P])
                        dve.tensor_tensor(sp_[:, h, a + t * P:a + W], ps[:, h, a + t * P:a + W], nmask[:, :], add)
                link(dve.tensor_tensor(spc[:, :, :], ps[:, 4, 0:NH * CPAD].rearrange("p (h c) -> p h c", h=NH), over(cmask[:, t, 0:CPAD], NH), add))
                dve.tensor_reduce(nst[:, 0:8], sp_[:, :, :].rearrange("p h (b k) -> p (h b) k", b=2)[:, :, 0:W], X, ALU.max, negate=True)
                dve.tensor_reduce(nst[:, 8:12], spc[:, :, :], X, ALU.max, negate=True).then_inc(S("nsa_max"), 1)
                dve.wait_ge(S("nsa_exp"), NH * (t + 1))
                link(dve.reciprocal(nst[:, 32:44], nst[:, 16:28]))
                g = small[:, t, 8:20].rearrange("p (h b) -> p h b", b=3)
                dve.tensor_tensor(nst[:, 0:8].rearrange("p (h b) -> p h b", b=2), nst[:, 32:40].rearrange("p (h b) -> p h b", b=2), g[:, :, 1:3], mul)
                link(dve.scalar_tensor_tensor(nst[:, 8:12], nst[:, 40:44], cmask[:, t, CPAD:CPAD + 1], g[:, :, 0], mul, mul))
                for h in range(NH):
                    for kk in range(2):
                        a = kk * 256
                        dve.tensor_scalar(sp_[:, h, a:a + W], sp_[:, h, a:a + W], nst[:, 2 * h + kk:2 * h + kk + 1], None, mul)
                    last = dve.tensor_scalar(spc[:, h, :], spc[:, h, :], nst[:, 8 + h:9 + h], None, mul)
                last.then_inc(S("nsa_p"), 1)
                dve.wait_ge(S("mix_hi"), t + 1)
                dve.tensor_tensor(hlo[:, 4:8, t * P:(t + 1) * P], ps[:, 7, :].rearrange("p (h q) -> p h q", h=NH), hhi[:, 4:8, t * P:(t + 1) * P].bitcast(f32), sub).then_inc(S("mix_lo"), 1)

            def wout(i, j):
                g = BASE["wout"] + j
                split_lo(dve, g + LEAD)
                dve.wait_ge(tile_used, nth(g))
                dve.scalar_tensor_tensor(x[:, j, :], chunk_bank(g), mod[:, 16 + j:17 + j], x[:, j, :], mul, add).then_inc(S("x_new"), 1)
            tiles(dve, "wout", wout)
            dve.memset(zf[:, :], 0.0).then_inc(S("zf_made"), 1)
            norm(1)

            def up(i, j):
                g, m, o = BASE["up"] + j, j // 2, uc[:, j % 4, :]
                split_lo(dve, g + LEAD, i)
                dve.wait_ge(S("up_scaled"), 4 * i + (j + 1))
                w = pick(upc, 4 * i + j)
                b = chunk_bank(g)
                dve.scalar_tensor_tensor(o[:, 1:SEQ], b[:, 0:SEQ - 1], w[:, 1:2], o[:, 1:SEQ], mul, add).then_inc(S("up_tap"), 1)
                dve.wait_ge(S("up_tap"), 4 * i + (j + 1))
                dve.scalar_tensor_tensor(o[:, 2:SEQ], b[:, 0:SEQ - 2], w[:, 0:1], o[:, 2:SEQ], mul, add).then_inc(S("up_kept"), 1)
                if j % 2:
                    dve.wait_ge(S("up_silu"), 2 * i + (m + 1))
                    dve.wait_ge(S("up_kept"), 4 * i + (j + 1))
                    dve.tensor_tensor(upp[:, m % 2, :], uc[:, j % 4 - 1, :], o, mul).then_inc(S("up_used"), 1)
                    if j > 1:
                        act_lo(i, m - 1)

            def act_lo(i, m):
                dve.wait_ge(S("act_hi"), 2 * i + (m + 1))
                dve.tensor_tensor(pick(alo, 2 * i + m), upp[:, m % 2, :], pick(ahi, 2 * i + m).bitcast(f32), sub).then_inc(S("act_lo"), 1)
            tiles(dve, "up", up)
            act_lo(0, FC - 1)
            tiles(dve, "down", lo_only("down"))
            dve.wait_ge(tile_used, nth(BASE["down"] + FC - 1))
            for c in range(KC):
                dve.scalar_tensor_tensor(x[:, c, :], ps[:, c // 2, (c % 2) * SEQ:(c % 2 + 1) * SEQ], mod[:, 40 + c:41 + c], x[:, c, :], mul, add).then_inc(S("x_new"), 1)
            dve.wait_ge(S("x_new"), 2 * KC)
            norm(2)

            dve.wait_ge(S("line_made"), 1)
            dve.memset(line[:, SEQ:2 * SEQ], NEG).then_inc(S("line_made"), 1)
            tiles(dve, "in2", lo_only("in2"))
            tiles(dve, "tok2", lo_only("tok2"), loop=False)
            dve.wait_ge(S("rot_made"), 1)
            dve.tensor_tensor(proj2[:, 0:8, :], proj2[:, 0:8, :], over(rot[:, P:P + SEQ], 8), mul)
            link(dve.tensor_tensor(tmp[:, :, :], ps[:, 0:4, :].rearrange("p b (c t) -> p (b c) t", c=2), over(rot[:, P + SEQ:P + 2 * SEQ], 8), mul))
            dve.tensor_tensor(flat(proj2[:, 0:8, :]), flat(proj2[:, 0:8, :]), flat(tmp[:, :, :]), add).then_inc(S("rotated"), 1)
            for t in range(TT):
                link(dve.tensor_reduce(vmean[:, 8 * t:8 * t + 8], vtok2[:, t, 0:1024].rearrange("p (h d) -> p h d", h=RH), X, add))
                link(dve.tensor_scalar(vmean[:, 8 * t:8 * t + 8], vmean[:, 8 * t:8 * t + 8], 1.0 / RV, None, mul))
                v3 = vtok2[:, t, 0:1024].rearrange("p (h d) -> p h d", h=RH)
                last = dve.tensor_tensor(v3, v3, vmean[:, 8 * t:8 * t + 8].rearrange("p (h o) -> p h o", o=1).to_broadcast([P, RH, RV]), sub)
            last.then_inc(S("v_centred"), 1)
            for h in range(RH):
                dve.wait_ge(S("ret_s"), h + 1)
                if h >= 2:
                    dve.wait_ge(S("ret_o"), h - 1)
                dve.tensor_tensor(pr[:, h % 2, 0:SEQ], ps[:, h % 2, 0:SEQ], dec[:, h, :], mul)
                dve.tensor_tensor(pr[:, h % 2, SEQ:SEQ + P], ps[:, h % 2, SEQ:SEQ + P], dec[:, h, 0:P], mul).then_inc(S("ret_p"), 1)
            dve.wait_ge(S("ro_root"), 1)
            dve.wait_ge(S("rg_silu"), 1)
            link(dve.tensor_tensor(flat(ro[:, :, :]), flat(ro[:, :, :]), flat(rs[:, 0:8, :]), mul))
            dve.tensor_tensor(flat(ro[:, :, :]), flat(ro[:, :, :]), flat(proj2[:, C_RG:C_RG + 8, :]), mul).then_inc(S("ro_done"), 1)
            dve.wait_ge(S("ro_hi"), 1)
            dve.tensor_tensor(hlo[:, :, :], ro[:, :, :], hhi[:, :, :].bitcast(f32), sub).then_inc(S("ro_lo"), 1)
            link(dve.tensor_scalar(prm2[:, 2:3], prm2[:, 0:1], float(MD) ** -0.5, None, mul))
            dve.wait_ge(S("m_root"), 1)
            dve.scalar_tensor_tensor(flat(proj2[:, C_MQ:C_MQ + 4, :]), flat(proj2[:, C_MQ:C_MQ + 4, :]), prm2[:, 2:3], flat(rs[:, 0:4, :]), mul, mul)
            dve.scalar_tensor_tensor(flat(proj2[:, C_MK:C_MK + 4, :]), flat(proj2[:, C_MK:C_MK + 4, :]), prm2[:, 1:2], flat(rs[:, 4:8, :]), mul, mul).then_inc(S("mk_normed"), 1)
            for n in range(4):
                t, hg = n // 2, n % 2
                W = (t + 1) * P
                dve.wait_ge(S("m_s"), n + 1)
                for b in range(2):
                    last = dve.tensor_reduce(mst[:, b:4:2], ps[:, 2 * (n % 2) + b, :].rearrange("p (h k) -> p h k", h=2)[:, :, 0:W], X, ALU.max, negate=True)
                last.then_inc(S("m_max"), 1)
                dve.wait_ge(S("m_exp"), 4 * (n + 1))
                link(dve.reciprocal(mst[:, 8:12], mst[:, 4:8]))
                for h in range(4):
                    last = dve.tensor_scalar(sp2[:, h, 0:W], sp2[:, h, 0:W], mst[:, 8 + h:9 + h], None, mul)
                last.then_inc(S("m_p"), 1)
                dve.wait_ge(S("m_hi"), n + 1)
                o = (slice(2 * hg, 2 * hg + 2), slice(t * P, (t + 1) * P))
                dve.tensor_tensor(mblo[:, o[0], o[1]], ps[:, 6 + n % 2, 0:2 * P].rearrange("p (c q) -> p c q", c=2), mbhi[:, o[0], o[1]].bitcast(f32), sub).then_inc(S("m_lo"), 1)

            dve.wait_ge(S("ab_sig"), 1)

            def retw(i, j):
                g = BASE["retw"] + j
                split_lo(dve, g + LEAD)
                dve.wait_ge(tile_used, nth(g))
                dve.tensor_tensor(ya[:, j, :], chunk_bank(g), proj2[:, C_GA + j, :], mul).then_inc(S("ya_kept"), 1)
            tiles(dve, "retw", retw)

            def mobw(i, j):
                g = BASE["mobw"] + j
                split_lo(dve, g + LEAD)
                dve.wait_ge(tile_used, nth(g))
                for u in range(2):
                    c = 2 * j + u
                    dve.tensor_tensor(proj2[:, C_GB + c, :], chunk_bank(u), proj2[:, C_GB + c, :], mul).then_inc(S("yb_kept"), 1)
            tiles(dve, "mobw", mobw)
            dve.wait_ge(S("yb_kept"), KC)
            dve.wait_ge(S("ya_kept"), KC)
            dve.tensor_tensor(flat(ya[:, :, :]), flat(ya[:, :, :]), flat(proj2[:, C_GB:C_GB + 8, :]), add).then_inc(S("merged"), 1)
            dve.wait_ge(S("merged_hi"), 1)
            dve.tensor_tensor(hlo[:, :, :], ya[:, :, :], hhi[:, :, :].bitcast(f32), sub).then_inc(S("merged_lo"), 1)

            def out2(i, j):
                g = BASE["out2"] + j
                split_lo(dve, g + LEAD)
                dve.wait_ge(tile_used, nth(g))
                dve.tensor_tensor(x[:, j, :], chunk_bank(g), x[:, j, :], add).then_inc(S("x_new"), 1)
            tiles(dve, "out2", out2)
            dve.wait_ge(S("x_new"), 3 * KC)
            norm(3)

            def pq(i, j):
                g = BASE["pq"] + j
                split_lo(dve, g + LEAD, i)
                dve.wait_ge(S("q_hi"), 4 * i + (j + 1))
                dve.tensor_tensor(pick(qlo, 4 * i + j), chunk_bank(g), pick(qhi, 4 * i + j).bitcast(f32), sub).then_inc(S("q_lo"), 1)
            tiles(dve, "pq", pq)
            tiles(dve, "subk", lo_only("subk"), loop=False)
            u_lo = lo_only("u")
            for j in range(4):
                u_lo(0, j)
            dve.wait_ge(S("scores_kept"), 2 * TT)

            def route(u):
                tile = [4]

                def step():
                    if tile[0] < 16:
                        u_lo(3 * u, tile[0])
                        tile[0] += 1
                    dve.drain()

                def top16(n, best, place, values, rest):
                    for m in range(n):
                        dve.max(best[:, m, 0:8], values(m))
                    step()
                    for m in range(n):
                        dve.match_replace(rest(m), in_to_replace=best[:, m, 0:8], in_values=values(m), imm_value=-3e38)
                        dve.max_index(place[:, m, 0:8], best[:, m, 0:8], values(m))
                    step()
                    for m in range(n):
                        dve.max(best[:, m, 8:16], rest(m))
                    step()
                    for m in range(n):
                        dve.max_index(place[:, m, 8:16], best[:, m, 8:16], rest(m))
                    step()

                dve.drain()
                dve.tensor_copy(scu[:, :, :], sc[:, bass.ds(4 * u, 4), :])
                step()
                top16(4, top8, tix, lambda m: scu[:, m, :], lambda m: scr[:, m, :])
                wide = [P, TOPK, TOPK]

                def along(t):
                    return t.rearrange("p (o e) -> p o e", o=1).to_broadcast(wide)

                def down_(t):
                    return t.rearrange("p (k o) -> p k o", o=1).to_broadcast(wide)
                dve.tensor_copy(tixf[:, :, :], tix[:, :, :])
                for m in range(2):
                    dve.tensor_tensor(cand[:, m, :, :], down_(top8[:, 2 * m, :]), along(top8[:, 2 * m + 1, :]), add)
                step()
                top16(2, cbu, cix, lambda m: cand[:, m, :, :].rearrange("p a b -> p (a b)"), lambda m: cand2[:, m, :])
                dve.tensor_copy(ctop[:, bass.ds(2 * u, 2), :], cbu[:, :, :])
                dve.tensor_scalar(cau[:, :, 0, :], cix[:, :, :], 4, None, ALU.logical_shift_right)
                dve.tensor_scalar(cau[:, :, 1, :], cix[:, :, :], TOPK - 1, None, ALU.bitwise_and)
                step()
                dve.tensor_copy(cab[:, :, :, :], cau[:, :, :, :])
                step()
                for m in range(4):
                    dve.tensor_tensor(eq[:, m % 2, m // 2, :, :], down_(cab[:, m // 2, m % 2, :]), along(iota[:, 0:TOPK]), ALU.is_equal)
                step()
                for m in range(4):
                    dve.tensor_tensor(eq[:, m % 2, m // 2, :, :], eq[:, m % 2, m // 2, :, :], along(tixf[:, m, :]), mul)
                step()
                for c in range(2):
                    dve.tensor_reduce(pidx[:, c, bass.ds(2 * u, 2), :], eq[:, c, :, :, :], X, add)
                assert tile[0] == 16

            with dve.Fori(0, TT * PH // 2) as u:
                route(u)
            dve.drain()
            link(dve.tensor_copy(gden[:, 0, :], ctop[:, :, 0]))
            wide = [P, TT * PH, TOPK]
            dve.tensor_tensor(ctop[:, :, :], ctop[:, :, :], gden[:, 0, :].rearrange("p (u o) -> p u o", o=1).to_broadcast(wide), sub).then_inc(S("gate_shifted"), 1)
            tiles(dve, "u", u_lo, 100, 104)
            dve.wait_ge(S("gate_exp"), 1)
            link(dve.tensor_reduce(gden[:, 0, :], ctop[:, :, :], X, add))
            link(dve.reciprocal(gden[:, 1, :], gden[:, 0, :]))
            dve.tensor_tensor(ctop[:, :, :], ctop[:, :, :], gden[:, 1, :].rearrange("p (u o) -> p u o", o=1).to_broadcast(wide), mul).then_inc(S("gates_made"), 1)
            dve.wait_ge(S("pairs_turned"), 1)
            dve.tensor_copy(pair[:, :, :], ps[:, 3:6, 0:SEQ]).then_inc(S("routed"), 1)
            tiles(dve, "u", u_lo, 104, 128)
            dve.wait_ge(S("routed"), 1)

            def rows(i, q):
                for a in range(4):
                    tok = 4 * q + a if isinstance(i, int) else 8 * i + (4 * q + a)
                    second, gate = col(pair[:, 1, :], tok), col(pair[:, 2, :], tok)
                    last = dve.tensor_scalar(e2[:, q % 2, a, :], iota, second, gate, ALU.is_equal, mul)
                last.then_inc(S("e2_made"), 1)

            def weigh(i, q):
                dve.wait_ge(S("outer_made"), 2 * i + (q + 1))
                toks = G[:, :, 4 * q:4 * q + 4] if isinstance(i, int) else G[:, :, bass.ds(8 * i + 4 * q, 4)]
                toks = toks.rearrange("p j t -> p t j")
                dve.tensor_tensor(toks, ps[:, 4 + q % 2, :].rearrange("p (t j) -> p t j", t=4), toks, mul).then_inc(S("outer_multiplied"), 1)
            dve.wait_ge(tile_used, nth(BASE["v"] - 1))
            rows(0, 0)
            dve.wait_ge(S("g_made"), NKEY)
            rows(0, 1)
            weigh(0, 0)
            with dve.Fori(0, SEQ // 8 - 1) as i:
                rows(i, 2)
                weigh(i, 1)
                rows(i, 3)
                weigh(i, 2)
            weigh(0, SEQ // 4 - 1)

            def m_lo(i, j):
                if j < NKEY:
                    dve.wait_ge(S("mhi_made"), 4 * i + (j + 1))
                    s = (BASE["v"] + j) % RING
                    dve.tensor_tensor(mlo[:, s, :], pick(G, 4 * i + j), mhi[:, s, :].bitcast(f32), sub).then_inc(S("mlo_made"), 1)
            dve.wait_ge(S("outer_multiplied"), SEQ // 4)
            for j in range(LEAD):
                m_lo(0, j)

            def vals(i, j):
                split_lo(dve, BASE["v"] + j + LEAD, i)
                m_lo(i, j + LEAD)
            tiles(dve, "v", vals)


_PARAMS = ["xT", "prm", "wsm", "w2", "upc", "prm2", "relb"]
_CONSTS = ["c_cst", "c_lvl", "c_nmask", "c_cmask", "c_rot", "c_dec", "c_relhot"]


def _constants():
    f = np.float32
    n = np.arange(P)
    cst = np.concatenate([np.eye(P), np.ones((P, P)), n[:, None] <= n[None, :], np.broadcast_to(n, (P, P))], 1).astype(f)
    lvl = np.zeros((P, LEVELS, P), f)
    for l in range(LEVELS):
        b = 1 << l
        same = (n[:, None] // (2 * b)) == (n[None, :] // (2 * b))
        lvl[:, l, :] = same & (n[:, None] % (2 * b) < b) & (n[None, :] % (2 * b) >= b)
    nmask = np.where(n[None, :] <= n[:, None], 0, NEG).astype(f)
    cmask = np.zeros((P, TT, CPAD + 1), f)
    for t in range(TT):
        q = t * P + n
        ends = np.arange(CPAD) * CMP_STRIDE + CMP_BLOCK - 1
        seen = (ends[None, :] <= q[:, None]) & (np.arange(CPAD) < N_CMP)[None, :]
        cmask[:, t, :CPAD] = np.where(seen, 0, NEG)
        cmask[:, t, CPAD] = seen.any(1)
    half = RQK // 2
    inv = f(10000.0) ** (-np.arange(half, dtype=f) / half)
    ang = np.arange(SEQ, dtype=f)[None, :] * inv.astype(f)[:, None]
    cos, sin = np.tile(np.cos(ang), (4, 1)), np.tile(np.sin(ang), (4, 1))
    perm = np.zeros((P, P), f)
    for m in range(P):
        if m % RQK < half:
            perm[m + half, m] = -1
        else:
            perm[m - half, m] = 1
    halves = (n[:, None] // MD == n[None, :] // MD)
    rot = np.concatenate([perm, cos, sin, halves, np.eye(P)[::-1]], 1).astype(f)
    log_g = np.log1p(-np.exp2(-5.0 - np.arange(RH)))
    d = np.arange(SEQ)[None, :] - n[:, None]
    dec = np.where(d[:, None, :] >= 0, np.exp(np.maximum(d, 0)[:, None, :] * log_g[None, :, None]), 0) * RQK ** -0.5
    dist = np.maximum(SEQ - 1 - np.arange(2 * SEQ), 0)
    exact = BUCKETS // 2
    large = exact + (np.log(np.maximum(dist, 1).astype(f) / exact) / f(math.log(MAXDIST / exact)) * (BUCKETS - exact)).astype(np.int32)
    bucket = np.where(dist < exact, dist, np.minimum(large, BUCKETS - 1))
    relhot = (np.arange(BUCKETS)[:, None] == bucket[None, :]).astype(f)
    return dict(c_cst=cst, c_lvl=lvl, c_nmask=nmask, c_cmask=cmask, c_rot=rot, c_dec=dec.astype(f), c_relhot=relhot)


def _chunks(w, nk=KC):
    n = w.shape[1] // P
    return w.reshape(nk, P, n, P).transpose(2, 1, 0, 3).reshape(n, P, nk * P)


def _rows(w, kk):
    return w.reshape(-1, kk, P, w.shape[1]).transpose(0, 2, 1, 3).reshape(-1, P, kk * w.shape[1])


def _layout(a):
    f = {k: np.asarray(v) for k, v in a.items()}
    g = {k: v[0] for k, v in f.items()}
    w = g["w_in"]
    cuts = np.cumsum([0, 512, 512, 512, 512, 4, 4, 512, 128, 128, 128, 128, 128, 128, 12])
    gq, gk, gv, gz, ga, gb, nq, kc, vc, ks, vs, kw, vw, ng = (w[:, s:e] for s, e in zip(cuts[:-1], cuts[1:]))
    w2 = g["w_in_2"]
    cut2 = np.cumsum([0, 512, 512, 1024, 1024, 512, 512, 512, 1024, 1024])
    rq, rk, rv, rg, mq, mk, mv, a2, b2 = (w2[:, s:e] for s, e in zip(cut2[:-1], cut2[1:]))
    up = _chunks(g["ffn_w_up"]).reshape(2, FC, P, TILE).transpose(1, 0, 2, 3).reshape(2 * FC, P, TILE)
    mob = _chunks(g["moba_w_branch_2"], 4).reshape(4, 2, P, 512).transpose(0, 2, 1, 3).reshape(4, P, TILE)
    tok2 = _rows(np.concatenate([rv, mv], 1), 1).reshape(4, 2, P, 3, 512).transpose(3, 0, 2, 1, 4).reshape(12, P, TILE)
    cmpw = np.stack([g["cmp_k_w1"], g["cmp_v_w1"]]).reshape(2, 4, 8, P, P).transpose(0, 1, 3, 2, 4).reshape(8, P, TILE)
    subk = g["peer_sub_keys_2"].reshape(2, 8, NKEY, P).transpose(0, 3, 1, 2).reshape(2, P, TILE)
    u = g["peer_u_2"].reshape(NKEY, NKEY, KC, P).transpose(1, 3, 2, 0).reshape(NKEY, P, TILE)
    v = g["peer_v_2"].reshape(NKEY, NKEY, D).transpose(1, 0, 2)
    ada = g["ada_w"].reshape(KC, P, 6, TILE).transpose(2, 0, 1, 3).reshape(RAW1 + RAW2, P, TILE)
    c = {
        "ada1": ada[:RAW1], "ada2": ada[RAW1:], "win": _chunks(np.concatenate([gq, gk, gv, nq, ks, kw, gz, kc, vc], 1)),
        "tok": _rows(np.concatenate([vs, vw], 1), 4), "cmp": cmpw, "wout": _chunks(g["w_out"]), "up": up,
        "down": g["ffn_w_down"].reshape(FC, P, D), "in2": _chunks(np.concatenate([rq, rk, rg, mq, mk, a2, b2], 1)),
        "tok2": tok2, "retw": _chunks(g["ret_w_branch_2"]), "mobw": mob, "out2": _chunks(g["w_out_2"]),
        "pq": _chunks(g["peer_w_q_2"]), "subk": subk, "u": u, "v": v,
    }
    out = {"w_" + k: x for k, x in c.items()}
    cols = lambda x: x.reshape(-1, P).T
    every = lambda x: np.broadcast_to(x.reshape(1, -1), (P, x.size))
    convw = g["gdn_conv_w"].reshape(4, 12, P).transpose(2, 1, 0).reshape(P, 48)
    prm = [cols(g["norm1_w"]), cols(g["norm2_w"]), cols(g["mix_norm_g_2"]), cols(g["ffn_norm_g_2"]), convw,
           cols(g["gdn_out_norm_w"]), cols(g["nsa_q_norm_w"]), cols(g["nsa_k_norm_cmp"]), cols(g["nsa_k_norm_slc"]),
           cols(g["nsa_k_norm_win"]), every(g["gdn_dt_bias"]), every(g["gdn_A_log"]), np.zeros((P, 3), np.float32),
           cols(f["c"][0]), cols(g["ada_b"]), g["cmp_k_pos"].T, g["cmp_v_pos"].T]
    prm = np.concatenate(prm, 1)
    out["prm"] = np.concatenate([prm, np.zeros((P, 256 - prm.shape[1]), np.float32)], 1)
    out["xT"] = f["x"][0].T.reshape(KC, P, SEQ).transpose(1, 0, 2)
    out["wsm"] = np.concatenate([ga, gb, ng], 1).reshape(KC, P, 20).transpose(1, 0, 2)
    out["w2"] = np.stack([g["cmp_k_w2"], g["cmp_v_w2"]], 1)
    taps = np.concatenate([g["ffn_conv_w"], g["ffn_conv_b"][None]], 0)
    out["upc"] = taps.reshape(4, 2, FC, P).transpose(3, 2, 1, 0).reshape(P, 2 * FC, 4)
    gains = np.stack([np.tile(g["moba_q_gain_2"], 2), np.tile(g["moba_k_gain_2"], 2)], 1)
    rest = np.zeros((P, 14), np.float32)
    rest[:, 1] = EPS
    out["prm2"] = np.concatenate([gains, rest], 1)
    out["relb"] = f["rel_bias_2"]
    return out


def kernel(**inputs):
    from concourse import bacc
    from concourse.bass_utils import run_bass_kernel_spmd

    nc = bacc.Bacc("TRN2", target_bir_lowering=False, num_devices=1)
    arrays = {k: np.ascontiguousarray(v) for k, v in {**_layout(inputs), **_constants()}.items()}
    A = {k: nc.dram_tensor("in_" + k, v.shape, mybir.dt.from_np(v.dtype), kind="ExternalInput").ap() for k, v in arrays.items()}
    A["line"] = nc.dram_tensor("bias_lines", (MH, 2 * SEQ), mybir.dt.float32).ap()
    out = nc.dram_tensor("out_x", (1, SEQ, D), mybir.dt.float32, kind="ExternalOutput").ap()
    build_program(nc, A, out)
    r = run_bass_kernel_spmd(nc, [{"in_" + k: v for k, v in arrays.items()}], core_ids=[0])
    return r.results[0]["out_x"]
```

```python
import math
import numpy as np
import concourse.bass as bass
from concourse import mybir
from contextlib import ExitStack

P = 128
SEQ, D = 256, 1024
KC = D // P
TT = SEQ // P
HEAD = 128
EPS = 1e-6
NEG = -1e30
TILE = 1024
RING = 4
LEAD = 2

FF = 2816
FC = FF // P
GH = 4
NH = 4
CMP_BLOCK, CMP_STRIDE = 32, 16
N_CMP = (SEQ - CMP_BLOCK) // CMP_STRIDE + 1
CPAD = 16
LEVELS = 7

RH, RQK, RV = 8, 64, 128
MH, MD = 8, 64
BUCKETS, MAXDIST = 32, 2048
PH, NKEY, TOPK = 8, 128, 16
NPAIR = PH * TOPK
NEXP = NKEY * NKEY

C_GQ, C_GK, C_GV, C_NQ, C_KS, C_KW, C_GZ, C_KC, C_VC = 0, 4, 8, 12, 16, 17, 18, 22, 23
CONV = 12
C_RQ, C_RK, C_RG, C_MQ, C_MK, C_GA, C_GB = 0, 4, 8, 16, 20, 24, 32

SEGMENTS = [("ada1", 16), ("win", 24), ("tok", 2), ("cmp", 8), ("ada2", 32), ("wout", 8), ("up", 2 * FC), ("down", FC),
            ("in2", 40), ("tok2", 12), ("retw", 8), ("mobw", 4), ("out2", 8), ("pq", 16), ("subk", 2),
            ("u", NKEY), ("v", NKEY)]
BASE, _at = {}, 0
for _name, _n in SEGMENTS:
    BASE[_name] = _at
    _at += _n
COUNT = dict(SEGMENTS)
TOTAL = _at
RAW1, RAW2 = COUNT["ada1"], COUNT["cmp"] + COUNT["ada2"]


def is_raw(g):
    return g < RAW1 or 0 <= g - BASE["cmp"] < RAW2


def ada_tile(r):
    return BASE["ada1"] + r if r < COUNT["ada1"] else BASE["ada2"] + r - COUNT["ada1"]


def nth(g):
    raw = min(g + 1, RAW1) + min(max(g + 1 - BASE["cmp"], 0), RAW2)
    return raw if is_raw(g) else g + 1 - raw


def build_program(nc, A, out):
    f32, f32r = mybir.dt.float32, mybir.dt.float32r
    u32 = mybir.dt.uint32
    ALU, ACT = mybir.AluOpType, mybir.ActivationFunctionType
    X = mybir.AxisListType.X
    add, sub, mul = ALU.add, ALU.subtract, ALU.mult

    ctx = ExitStack()
    with ctx:
        sems = {}

        def S(name):
            if name not in sems:
                sems[name] = ctx.enter_context(nc.semaphore(name))
            return sems[name]

        top = [-(-nc.sbuf_base // 32) * 32]

        def span(shape):
            return -(-4 * int(np.prod(shape[1:])) // 32) * 32

        def at(name, shape, dt, offset=None):
            size = span(shape)
            if offset is None:
                offset = top[0]
                top[0] = offset + size
            assert offset + size <= nc.sbuf_usable_end, (name, offset, size)
            return nc.alloc_sbuf_tensor_at(name, list(shape), dt, offset=offset)

        raw = at("raw", [P, RING, TILE], f32)
        whi = at("whi", [P, RING, TILE], f32r)
        wlo = at("wlo", [P, RING, TILE], f32r)
        raw_end = top[0]
        x = at("x", [P, KC, SEQ], f32)
        hhi = at("hhi", [P, KC, SEQ], f32r)
        hlo = at("hlo", [P, KC, SEQ], f32r)
        cst = at("cst", [P, 4 * P], f32)
        ident, ones, tri, iota = (cst[:, i * P:(i + 1) * P] for i in range(4))
        gains = at("gains", [P, 4, KC], f32)
        shifts = at("shifts", [P, 4, KC], f32)
        mod = at("mod", [P, 48], f32)
        epsc = at("epsc", [P, 1], f32)
        PAIR0 = top[0]
        G0 = PAIR0 + 3 * SEQ * 4
        up_at = [G0]

        def big(name, shape, dt=f32, offset=None):
            if offset is None:
                offset = up_at[0]
                up_at[0] += span(shape)
            return at(name, shape, dt, offset)

        tmp = big("tmp", [P, KC, SEQ])
        rs = big("rs", [P, 14, SEQ])
        R1 = up_at[0]
        acc2 = big("acc2", [P, 2, TILE], offset=G0)
        prm = big("prm", [P, 256])
        proj = big("proj", [P, 24, SEQ])
        vtok = big("vtok", [P, TT, 256])
        small = big("small", [P, TT, 20])
        wsm = big("wsm", [P, KC, 20])
        w2 = big("w2", [P, 2, P])
        lvl = big("lvl", [P, LEVELS, P])
        nmask = big("nmask", [P, P])
        cmask = big("cmask", [P, TT, CPAD + 1])
        csl = big("csl", [P, KC])
        hid = big("hid", [P, 2, CPAD])
        kc = big("kc", [P, CPAD])
        sqc = big("sqc", [P, CPAD])
        rsc = big("rsc", [P, CPAD])
        vc = big("vc", [P, P])
        blk = big("blk", [P, 2, CMP_BLOCK, CPAD])
        gsm = big("gsm", [P, 96])
        gcB = big("gcB", [P, 8, P])
        Xs = big("Xs", [P, 8, P])
        wT = big("wT", [P, GH, P])
        St = big("St", [P, GH, P])
        kbT = big("kbT", [P, GH, SEQ])
        R2 = up_at[0]
        DT = big("DT", [P, 8, P])
        AT = big("AT", [P, 8, P])
        QT = big("QT", [P, 8, P])
        BT = big("BT", [P, 8, P])
        Tm = big("Tm", [P, 8, P])
        TTm = big("TTm", [P, 8, P])
        vb = big("vb", [P, 8, P])
        kw = big("kw", [P, 8, P])
        U = big("U", [P, 8, P])
        qd = big("qd", [P, GH, P])
        eg = big("eg", [P, GH, P])
        og = big("og", [P, GH, SEQ])
        ogsq = big("ogsq", [P, 1024])
        acc = big("acc", [P, 2, 2, TILE], offset=R2 + 16 * 1024)
        cv = big("cv", [P, 12, SEQ], offset=R2)
        sq = big("sq", [P, 14 * SEQ], offset=R2)
        sp_ = big("sp_", [P, TT, NH, 512], offset=R2 + 14 * 1024)
        spc = big("spc", [P, TT, NH, CPAD], offset=R2 + 8192)
        nst = big("nst", [P, TT, 48], offset=R2)
        pt = big("pt", [P, 2, 512], offset=R2 + 8704)
        ptc = big("ptc", [P, 2, P], offset=R2 + 12800)
        ahi = big("ahi", [P, FC, SEQ], f32r, offset=R1)
        alo = big("alo", [P, FC, SEQ], f32r, offset=R1 + FC * 1024)
        o_ = R1 + 2 * FC * 1024
        upc = big("upc", [P, 2 * FC, 4], offset=o_)
        uc = big("uc", [P, 4, SEQ], offset=o_ + 1024)
        upp = big("upp", [P, 2, SEQ], offset=o_ + 5120)
        zz = big("zz", [P, 512], f32r, offset=o_ + 7168)
        zf = big("zf", [P, 512], offset=o_ + 9216)
        up_at[0] = R1
        proj2 = big("proj2", [P, 40, SEQ])
        vtok2 = big("vtok2", [P, TT, 1536])
        bias = big("bias", [P, TT, MH, SEQ])
        dec = big("dec", [P, RH, SEQ])
        rot = big("rot", [P, 3 * P + 2 * SEQ])
        relhot = big("relhot", [BUCKETS, 2 * SEQ])
        relb = big("relb", [BUCKETS, MH])
        line = big("line", [MH, 2 * SEQ])
        prm2 = big("prm2", [P, 16])
        ro = big("ro", [P, RH, SEQ])
        ya = big("ya", [P, KC, SEQ])
        mbhi = big("mbhi", [P, 4, SEQ], f32r)
        mblo = big("mblo", [P, 4, SEQ], f32r)
        mst = big("mst", [P, 32])
        vmean = big("vmean", [P, 16])
        RS = 8192 + G0
        pr = big("pr", [P, 2, 384], offset=RS + 2048)
        pt2 = big("pt2", [P, 2, SEQ], offset=RS)
        sp2 = big("sp2", [P, 2, 4, SEQ], offset=RS + 1024 * 6)
        pair = at("pair", [P, 3, SEQ], f32, PAIR0)
        G = at("G", [P, NKEY, SEQ], f32, G0)
        qhi = at("qhi", [P, 16, SEQ], f32r, G0 + 48 * 1024)
        qlo = at("qlo", [P, 16, SEQ], f32r, G0 + 64 * 1024)
        sc = at("sc", [P, TT * PH * 2, NKEY], f32, G0 + 104 * 1024)
        o_ = G0 + 120 * 1024
        scu = at("scu", [P, 4, NKEY], f32, o_)
        scr = at("scr", [P, 4, NKEY], f32, o_ + 2048)
        cand = at("cand", [P, 2, TOPK, TOPK], f32, o_ + 2048)
        cand2 = at("cand2", [P, 2, TOPK * TOPK], f32, o_)
        eq = at("eq", [P, 2, 2, TOPK, TOPK], f32, o_)
        top8 = at("top8", [P, 4, TOPK], f32, o_ + 4096)
        tix = at("tix", [P, 4, TOPK], u32, o_ + 4352)
        tixf = at("tixf", [P, 4, TOPK], f32, o_ + 4608)
        cbu = at("cbu", [P, 2, TOPK], f32, o_ + 4864)
        cix = at("cix", [P, 2, TOPK], u32, o_ + 4992)
        cau = at("cau", [P, 2, 2, TOPK], u32, o_ + 5120)
        cab = at("cab", [P, 2, 2, TOPK], f32, o_ + 5376)
        gden = at("gden", [P, 2, TT * PH], f32, o_ + 5632)
        ctop = at("ctop", [P, TT * PH, TOPK], f32, PAIR0)
        pidx = at("pidx", [P, 2, TT * PH, TOPK], f32, PAIR0 + 1024)
        hh0 = raw_end + KC * SEQ * 4
        e1 = at("e1", [P, 2, 4, P], f32, hh0)
        e2 = at("e2", [P, 2, 4, P], f32, hh0 + 4096)
        mhi = at("mhi", [P, RING, SEQ], f32r, hh0 + 8192)
        dist = at("dist", [P, 4, 4, P], f32, hh0 + 8192)
        mlo = at("mlo", [P, RING, SEQ], f32r, hh0 + 12288)
        y = at("y", [P, TT, D], f32, hh0)

        ps = ctx.enter_context(nc.psum_tensor("ps", [P, 8, 512], f32))

        def bank(b, n=1):
            return ps[:, b:b + n, :].rearrange("p b c -> p (b c)")

        w_loaded = [S(f"w_loaded{s}") for s in range(RING)]
        hi_made, lo_made, tile_used, raw_used = S("hi_made"), S("lo_made"), S("tile_used"), S("raw_used")

        def wait(eng, sem, value):
            if not isinstance(value, int) or value > 0:
                eng.wait_ge(sem, value)

        def tiles(eng, name, body, start=0, stop=None, loop=True):
            n = COUNT[name] if stop is None else stop
            head = start + 4 if start == 0 else start
            tail = n - 4 if (name, n) == ("v", COUNT["v"]) else n
            m = (tail - head) // 4
            if m < 2 or not loop:
                m, head = 0, start
            for j in range(start, head):
                body(0, j)
            if m:
                with eng.Fori(0, m) as i:
                    for s in range(4):
                        body(i, head + s)
            for j in range(head + 4 * m, n):
                body(0, j)

        def pick(t, j):
            if isinstance(j, int):
                return t[:, j]
            return t[:, bass.ds(j, 1)].rearrange("p o t -> p (o t)")

        def col(t, j):
            return t[:, j:j + 1] if isinstance(j, int) else t[:, bass.ds(j, 1)]

        def load(sp, name):
            def body(i, j):
                g = BASE[name] + j
                if g >= RING:
                    sp.wait_ge(raw_used if is_raw(g - RING) else lo_made, 4 * i + nth(g - RING))
                src = A["w_" + name]
                src = src[4 * i + j] if isinstance(i, int) else src[bass.ds(4 * i + j, 1)].rearrange("o p c -> p (o c)")
                sp.dma_start(raw[:, g % RING, :], src).then_inc(w_loaded[g % RING], 16)
            return body

        def split_hi(act, g, i=0):
            if g < TOTAL and not is_raw(g):
                act.wait_ge(w_loaded[g % RING], 16 * i + 16 * (g // RING + 1))
                if nth(g) > RING:
                    act.wait_ge(tile_used, 4 * i + nth(g) - RING)
                act.activation(whi[:, g % RING, :], raw[:, g % RING, :], ACT.Copy).then_inc(hi_made, 1)

        def split_lo(dve, g, i=0):
            if g < TOTAL and not is_raw(g):
                dve.wait_ge(hi_made, 4 * i + nth(g))
                dve.tensor_tensor(wlo[:, g % RING, :], raw[:, g % RING, :], whi[:, g % RING, :].bitcast(f32), sub).then_inc(lo_made, 1)

        def products(pe, g, o, cols, bh, bl, start, stop):
            wh, wl = whi[:, g % RING, cols], wlo[:, g % RING, cols]
            pe.matmul(o, wh, bh, start=start, stop=False, skip_group_check=True)
            pe.matmul(o, wh, bl, start=False, stop=False, skip_group_check=True)
            return pe.matmul(o, wl, bh, start=False, stop=stop, skip_group_check=True)

        def chunk_bank(g):
            return ps[:, 6 + g % 2, 0:SEQ]

        def turned_cmp(m):
            return ps[0:CPAD, 5 + m % 2, 2 * P:3 * P] if m < NH else ps[0:CPAD, m % 2, 0:P]

        def segment_T(pe, name, bh, bl, kept, count0=0, nk=KC, norm=None):
            def body(i, j):
                g, per = BASE[name] + j, KC // nk
                pe.wait_ge(lo_made, 4 * i + nth(g))
                for u in range(per):
                    if per * j + u >= 2:
                        pe.wait_ge(S(kept), per * 4 * i + (count0 + per * j + u - 1))
                    for k in range(nk):
                        if norm is not None and isinstance(i, int) and j == 0:
                            pe.wait_ge(S("h_lo"), KC * norm + k + 1)
                        last = products(pe, g, chunk_bank(g * per + u), slice((u * nk + k) * P, (u * nk + k + 1) * P),
                                        bh[:, k, :], bl[:, k, :], k == 0, k == nk - 1)
                last.then_inc(tile_used, 1)
            return body

        block = ctx.enter_context(nc.Block())
        @block.sync
        def _(sp):
            sp.dma_start(cst[:, :], A["c_cst"]).then_inc(S("prm_in"), 16)
            sp.dma_start(prm[:, :], A["prm"]).then_inc(S("prm_in"), 16)
            sp.dma_start(x[:, :, :], A["xT"]).then_inc(S("x_in"), 16)
            for name, _ in SEGMENTS:
                tiles(sp, name, load(sp, name))
            sp.wait_ge(S("y_made"), TT)
            for t in range(TT):
                sp.dma_start(out[0, t * P:(t + 1) * P, :], y[:, t, :]).then_inc(S("stored"), 16)
            sp.wait_ge(S("stored"), 16 * TT)

        @block.gpsimd
        def _(pool):
            pool.dma_start(lvl[:, :, :], A["c_lvl"]).then_inc(S("mix1_in"), 16)
            pool.dma_start(nmask[:, :], A["c_nmask"]).then_inc(S("mix1_in"), 16)
            pool.dma_start(cmask[:, :, :], A["c_cmask"]).then_inc(S("mix1_in"), 16)
            pool.dma_start(wsm[:, :, :], A["wsm"]).then_inc(S("mix1_in"), 16)
            pool.dma_start(w2[:, :, :], A["w2"]).then_inc(S("mix1_in"), 16)
            pool.wait_ge(S("x_new"), KC)
            pool.dma_start(upc[:, :, :], A["upc"]).then_inc(S("up_in"), 16)
            pool.wait_ge(S("x_new"), 2 * KC)
            pool.dma_start(prm2[:, :], A["prm2"]).then_inc(S("prm2_in"), 16)
            for dst, src in ((rot[:, :], "c_rot"), (dec[:, :, :], "c_dec"), (relhot[:, :], "c_relhot"), (relb[:, :], "relb")):
                pool.dma_start(dst, A[src]).then_inc(S("mix2_in"), 16)
            pool.wait_ge(S("line_made"), 2)
            pool.dma_start(A["line"], line[:, :]).then_inc(S("line_out"), 16)
            pool.wait_ge(S("line_out"), 16)
            for h in range(MH):
                for t in range(TT):
                    pool.dma_start(bias[:, t, h, 0:(t + 1) * P],
                                   bass.AP(tensor=A["line"].tensor, offset=h * 2 * SEQ + (1 - t) * P,
                                           ap=[[1, P], [1, (t + 1) * P]])).then_inc(S("bias_in"), 16)

        @block.tensor
        def _(pe):
            def norm_sum(k, c):
                pe.wait_ge(S("norm_squared"), KC * k + c + 1)
                last = pe.matmul(ps[:, 4, 0:SEQ], ones, tmp[:, c, :], start=c == 0, stop=c == KC - 1, skip_group_check=True)
                if c == KC - 1:
                    last.then_inc(S("norm_summed"), 1)

            def norm(k):
                for c in range(KC):
                    norm_sum(k, c)

            def new_x(name, k, count0):
                seg = segment_T(pe, name, hhi, hlo, "x_new", count0=count0)

                def body(i, j):
                    seg(i, j)
                    if j >= 2:
                        norm_sum(k, j - 2)
                tiles(pe, name, body)
                for c in range(KC - 2, KC):
                    norm_sum(k, c)

            pe.wait_ge(S("prm_in"), 32)
            norm(0)
            def mod_sum(n):
                pe.wait_ge(raw_used, nth(ada_tile(KC * n + KC - 1)))
                for m in range(KC):
                    w = slice(m * P, (m + 1) * P)
                    if n < 2:
                        o = ps[:, 1, KC * n + m:KC * n + m + 1]
                        pe.matmul(o, acc[:, n, 0, w], ones[:, 0:1], start=True, stop=False)
                        last = pe.matmul(o, acc[:, n, 1, w], ones[:, 0:1], start=False, stop=True)
                    else:
                        o = ps[:, 7, KC * (n - 2) + m:KC * (n - 2) + m + 1]
                        last = pe.matmul(o, acc2[:, n % 2, w], ones[:, 0:1], start=True, stop=True)
                last.then_inc(S("mod_summed"), 1)
            mod_sum(0)
            mod_sum(1)

            tiles(pe, "win", segment_T(pe, "win", hhi, hlo, "win_kept", norm=0))

            def tok(i, j):
                slot = (BASE["tok"] + j) % RING
                pe.wait_ge(lo_made, nth(BASE["tok"] + j))
                for t in range(TT):
                    for kk in range(4):
                        k, w = 4 * j + kk, slice(kk * 256, kk * 256 + 256)
                        s = slice(t * P, (t + 1) * P)
                        pe.matmul(ps[:, 4 + t, 0:256], hhi[:, k, s], whi[:, slot, w], start=k == 0, stop=False)
                        pe.matmul(ps[:, 4 + t, 0:256], hlo[:, k, s], whi[:, slot, w], start=False, stop=False)
                        last = pe.matmul(ps[:, 4 + t, 0:256], hhi[:, k, s], wlo[:, slot, w], start=False, stop=k == KC - 1)
                last.then_inc(tile_used, 1)
            tiles(pe, "tok", tok)
            pe.wait_ge(S("mix1_in"), 5 * 16)
            pe.wait_ge(S("h_made"), 1)
            for t in range(TT):
                for k in range(KC):
                    last = pe.matmul(ps[:, 3, 32 * t:32 * t + 20], tmp[:, k, t * P:(t + 1) * P], wsm[:, k, :], start=k == 0, stop=k == KC - 1)
            last.then_inc(S("small_made"), 1)
            pe.wait_ge(S("blk_made"), 1)

            def cmp(i, j):
                g = BASE["cmp"] + j
                pe.wait_ge(w_loaded[g % RING], 16 * (g // RING + 1))
                kv = j // 4
                for k in range(8):
                    m = (j % 4) * 8 + k
                    last = pe.matmul(ps[:, 7, kv * CPAD:(kv + 1) * CPAD], raw[:, g % RING, k * P:(k + 1) * P], blk[:, kv, m, :], start=m == 0, stop=m == 31)
                last.then_inc(raw_used, 1)
                if j == 1:
                    pe.wait_ge(S("heads_squared"), 2)
                    pe.wait_ge(S("vtok_made"), TT)
                    pe.wait_ge(S("small_kept"), 1)
                    for b in range(7):
                        last = pe.matmul(ps[:, b, :], ones, sq[:, b * 512:(b + 1) * 512], start=True, stop=True)
                    last.then_inc(S("heads_summed"), 1)
            tiles(pe, "cmp", cmp)
            pe.wait_ge(S("hid_made"), 1)
            pe.matmul(ps[:, 7, 64:64 + CPAD], w2[:, 0, :], hid[:, 0, :], start=True, stop=True)
            pe.matmul(ps[0:CPAD, 7, P:2 * P], hid[:, 1, :], w2[:, 1, :], start=True, stop=True).then_inc(S("cmp_made"), 1)
            pe.wait_ge(S("heads_root"), 1)

            pe.wait_ge(S("decay_made"), 1)
            for p in range(8):
                t, h = p // 4, p % 4
                pe.matmul(ps[:, p // 4, h * P:(h + 1) * P], gsm[:, p:p + 1].to_broadcast([P, P]), tri, start=True, stop=True)
            for t in range(TT):
                pe.matmul(ps[:, 4, 4 * t:4 * t + 4], tri, gsm[:, 4 * t:4 * t + 4], start=True, stop=True)
            for p in range(8):
                last = pe.matmul(ps[:, 2 + p // 4, (p % 4) * P:(p % 4 + 1) * P], gsm[:, 8 + p:9 + p].to_broadcast([P, P]), ident, start=True, stop=True)
            last.then_inc(S("sums_made"), 1)
            pe.wait_ge(S("cmp_squared"), 1)
            pe.wait_ge(S("vc_made"), 1)
            pe.matmul(ps[:, 7, 0:CPAD], ones, sqc[:, :], start=True, stop=True).then_inc(S("cmp_summed"), 1)
            pe.wait_ge(S("kbT_made"), 1)
            pe.wait_ge(S("cmp_root"), 1)

            def tt(p):
                return slice((p // 4) * P, (p // 4 + 1) * P)
            for p in range(8):
                h, b, c = p % 4, p // 4, slice((p % 4) * P, (p % 4 + 1) * P)
                pe.matmul(ps[:, b, c], proj[:, C_GK + h, tt(p)], kbT[:, h, tt(p)], start=True, stop=True)
                pe.matmul(ps[:, 2 + b, c], proj[:, C_GK + h, tt(p)], proj[:, C_GQ + h, tt(p)], start=True, stop=True)
            for p in range(8):
                h, b, c = p % 4, p // 4, slice((p % 4) * P, (p % 4 + 1) * P)
                pe.transpose(ps[:, 4 + b, c], proj[:, C_GK + h, tt(p)], ident)
                last = pe.transpose(ps[:, 6 + b, c], proj[:, C_GV + h, tt(p)], ident)
            last.then_inc(S("kk_made"), 1)
            pe.wait_ge(S("kv_scaled"), 1)
            for l in range(LEVELS):
                if l in (2, 5):
                    mod_sum(2 + l // 5)
                for b in range(2):
                    pe.wait_ge(S("lvl_masked"), 2 * l + b + 1)
                    if l:
                        pe.wait_ge(S("inv_updated"), 2 * (l - 1) + b + 1)
                    for p in range(4 * b, 4 * b + 4):
                        last = pe.matmul(ps[:, b, (p % 4) * P:(p % 4 + 1) * P], BT[:, p, :], Tm[:, p, :], start=True, stop=True)
                    last.then_inc(S("inv_x"), 1)
                for b in range(2):
                    pe.wait_ge(S("inv_xs"), 2 * l + b + 1)
                    for p in range(4 * b, 4 * b + 4):
                        c = slice((p % 4) * P, (p % 4 + 1) * P)
                        pe.matmul(ps[:, 2 + b, c], TTm[:, p, :], Xs[:, p, :], start=True, stop=True)
                        last = pe.matmul(ps[:, 4 + b, c], Xs[:, p, :], TTm[:, p, :], start=True, stop=True)
                    last.then_inc(S("inv_y"), 1)
            pe.wait_ge(S("inv_updated"), 2 * LEVELS)
            for p in range(8):
                c = slice((p % 4) * P, (p % 4 + 1) * P)
                pe.matmul(ps[:, p // 4, c], TTm[:, p, :], vb[:, p, :], start=True, stop=True)
            for h in range(GH):
                last = pe.matmul(ps[:, 2, h * P:(h + 1) * P], kw[:, 4 + h, :], TTm[:, 4 + h, :], start=True, stop=True)
            last.then_inc(S("uw_made"), 1)
            pe.wait_ge(S("uw_kept"), 1)
            for h in range(GH):
                last = pe.matmul(ps[:, 3, h * P:(h + 1) * P], kw[:, h, :], U[:, h, :], start=True, stop=True)
            last.then_inc(S("state_made"), 1)
            pe.wait_ge(S("state_kept"), 1)
            for h in range(GH):
                last = pe.matmul(ps[:, 4, h * P:(h + 1) * P], wT[:, h, :], St[:, h, :], start=True, stop=True)
            last.then_inc(S("ws_made"), 1)
            for h in range(GH):
                pe.matmul(ps[:, 5, h * P:(h + 1) * P], U[:, h, :], QT[:, h, :], start=True, stop=True)
            pe.wait_ge(S("vnew_made"), 1)
            for h in range(GH):
                c = slice(h * P, (h + 1) * P)
                pe.matmul(ps[:, 6, c], St[:, h, :], qd[:, h, :], start=True, stop=False)
                last = pe.matmul(ps[:, 6, c], U[:, 4 + h, :], QT[:, 4 + h, :], start=False, stop=True)
            last.then_inc(S("og_made"), 1)
            pe.wait_ge(S("og_squared"), 1)
            for b in range(2):
                last = pe.matmul(ps[:, b, :], ones, ogsq[:, b * 512:(b + 1) * 512], start=True, stop=True)
            last.then_inc(S("og_summed"), 1)
            mod_sum(4)
            mod_sum(5)

            def nsa_scores(t):
                W = (t + 1) * P
                pe.wait_ge(S("og_lo"), 1)
                if t:
                    pe.wait_ge(S("nsa_max"), t)
                for h in range(NH):
                    q = proj[:, C_NQ + h, t * P:(t + 1) * P]
                    pe.matmul(ps[:, h, 0:W], q, proj[:, C_KS, 0:W], start=True, stop=True)
                    pe.matmul(ps[:, h, 256:256 + W], q, proj[:, C_KW, 0:W], start=True, stop=True)
                for h in range(NH):
                    last = pe.matmul(ps[:, 4, h * CPAD:(h + 1) * CPAD], proj[:, C_NQ + h, t * P:(t + 1) * P], kc[:, :], start=True, stop=True)
                last.then_inc(S("nsa_s"), 1)

            def nsa_turn(t, h):
                m, n = NH * t + h, 0
                pe.wait_ge(S("nsa_p"), m + 1)
                if m >= 2:
                    pe.wait_ge(S("nsa_pt"), m - 1)
                for kk in range(2):
                    for u in range(t + 1):
                        pe.transpose(ps[:, 5 + m % 2, n * P:(n + 1) * P], sp_[:, t, h, kk * 256 + u * P:kk * 256 + (u + 1) * P], ident)
                        n += 1
                pe.transpose(turned_cmp(m), spc[:, t, h, :], ident).then_inc(S("nsa_tr"), 1)

            nsa_scores(0)
            nsa_scores(1)
            for t in range(TT):
                nsa_turn(t, 0)
                if t:
                    pe.wait_ge(S("mix_lo"), t)
                for h in range(NH):
                    m, n = NH * t + h, 0
                    if h + 1 < NH:
                        nsa_turn(t, h + 1)
                    pe.wait_ge(S("nsa_pt"), m + 1)
                    o = ps[:, 7, h * P:(h + 1) * P]
                    for kk in range(2):
                        for u in range(t + 1):
                            pe.matmul(o, vtok[:, u, kk * P:(kk + 1) * P], pt[:, m % 2, n * P:(n + 1) * P], start=n == 0, stop=False)
                            n += 1
                    last = pe.matmul(o, vc[0:CPAD, :], ptc[0:CPAD, m % 2, :], start=False, stop=True)
                last.then_inc(S("nsa_o"), 1)

            pe.wait_ge(S("mix_lo"), TT)
            new_x("wout", 1, 0)
            tiles(pe, "up", segment_T(pe, "up", hhi, hlo, "up_kept", norm=1))
            pe.wait_ge(S("zeros_made"), 1)
            for b in range(4):
                pe.matmul(ps[:, b, :], zz[:, 0:P], zz[:, :], start=True, stop=False, skip_group_check=True)
            pe.wait_ge(S("act_lo"), FC)

            def down(i, j):
                g = BASE["down"] + j
                pe.wait_ge(lo_made, 4 * i + nth(g))
                for c in range(KC):
                    last = products(pe, g, ps[:, c // 2, (c % 2) * SEQ:(c % 2 + 1) * SEQ], slice(c * P, (c + 1) * P),
                                    pick(ahi, 4 * i + j), pick(alo, 4 * i + j), False, False)
                last.then_inc(tile_used, 1)
            tiles(pe, "down", down)

            norm(2)
            pe.wait_ge(S("mix2_in"), 4 * 16)
            pe.matmul(ps[0:MH, 5, :], relb[:, :], relhot[:, :], start=True, stop=True).then_inc(S("line_psum"), 1)
            tiles(pe, "in2", segment_T(pe, "in2", hhi, hlo, "in2_kept", norm=2))

            pe.wait_ge(S("in2_kept"), 40)
            for c in range(8):
                last = pe.matmul(ps[:, 4 + c // 2, (c % 2) * SEQ:(c % 2 + 1) * SEQ], rot[:, 0:P], proj2[:, C_RQ + c, :], start=True, stop=True)
            last.then_inc(S("rot_made"), 1)

            def tok2(i, j):
                g, n = BASE["tok2"] + j, j // 4
                pe.wait_ge(lo_made, nth(g))
                if j == 8:
                    pe.wait_ge(S("m_squared"), 1)
                    for b in range(4):
                        last = pe.matmul(ps[:, 4 + b, :], rot[:, P + 2 * SEQ:2 * P + 2 * SEQ], tmp[:, 2 * b:2 * b + 2, :].rearrange("p c t -> p (c t)"), start=True, stop=True)
                    last.then_inc(S("m_summed"), 1)
                    pe.wait_ge(S("tok2_kept"), 2)
                for t in range(TT):
                    for kk in range(2):
                        k, w, s = 2 * (j % 4) + kk, slice(kk * 512, kk * 512 + 512), slice(t * P, (t + 1) * P)
                        o = ps[:, 2 * (n % 2) + t, :]
                        pe.matmul(o, hhi[:, k, s], whi[:, g % RING, w], start=k == 0, stop=False)
                        pe.matmul(o, hlo[:, k, s], whi[:, g % RING, w], start=False, stop=False)
                        last = pe.matmul(o, hhi[:, k, s], wlo[:, g % RING, w], start=False, stop=k == KC - 1)
                last.then_inc(tile_used, 1)
            tiles(pe, "tok2", tok2, loop=False)
            pe.wait_ge(S("tok2_kept"), 6)
            pe.wait_ge(S("mk_normed"), 1)
            pe.wait_ge(S("rotated"), 1)
            pe.wait_ge(S("v_centred"), 1)

            def ret_s(h):
                r = slice(64 * (h % 2), 64 * (h % 2) + 64)
                if h >= 2:
                    pe.wait_ge(S("ret_p"), h - 1)
                pe.matmul(ps[:, h % 2, 0:SEQ], proj2[r, C_RK + h // 2, 0:P], proj2[r, C_RQ + h // 2, :], start=True, stop=True)
                pe.matmul(ps[:, h % 2, SEQ:SEQ + P], proj2[r, C_RK + h // 2, P:SEQ], proj2[r, C_RQ + h // 2, P:SEQ], start=True, stop=True).then_inc(S("ret_s"), 1)

            def ret_o(h):
                pe.wait_ge(S("ret_p"), h + 1)
                if h >= 2:
                    pe.wait_ge(S("ro_kept"), h - 1)
                c = slice(h * RV, (h + 1) * RV)
                pe.matmul(ps[:, 2 + h % 2, 0:P], vtok2[:, 0, c], pr[:, h % 2, 0:P], start=True, stop=True)
                pe.matmul(ps[:, 2 + h % 2, P:SEQ], vtok2[:, 0, c], pr[:, h % 2, P:SEQ], start=True, stop=False)
                pe.matmul(ps[:, 2 + h % 2, P:SEQ], vtok2[:, 1, c], pr[:, h % 2, SEQ:SEQ + P], start=False, stop=True).then_inc(S("ret_o"), 1)
            ret_s(0)
            for h in range(RH):
                if h + 1 < RH:
                    ret_s(h + 1)
                ret_o(h)
            pe.wait_ge(S("bias_in"), 16 * MH * TT)

            def m_scores(n):
                t, hg = n // 2, n % 2
                W = (t + 1) * P
                if n == 0:
                    pe.wait_ge(S("ret_p"), RH)
                if n == 1:
                    pe.wait_ge(S("ro_var"), 1)
                if n >= 2:
                    pe.wait_ge(S("m_exp"), 4 * (n - 1))
                for h in range(4):
                    hh = 4 * hg + h
                    r = slice(64 * (hh % 2), 64 * (hh % 2) + 64)
                    o = ps[:, 2 * (n % 2) + h % 2, (h // 2) * SEQ:(h // 2) * SEQ + W]
                    pe.matmul(o, proj2[r, C_MQ + hh // 2, t * P:(t + 1) * P], proj2[r, C_MK + hh // 2, 0:W], start=True, stop=False)
                    last = pe.matmul(o, rot[:, 2 * P + 2 * SEQ:3 * P + 2 * SEQ], bias[:, t, hh, 0:W], start=False, stop=True)
                last.then_inc(S("m_s"), 1)

            def m_turn(n, h):
                m = 4 * n + h
                if m >= 2:
                    pe.wait_ge(S("m_pt"), m - 1)
                for u in range(n // 2 + 1):
                    last = pe.transpose(ps[:, 4 + m % 2, u * P:(u + 1) * P], sp2[:, n % 2, h, u * P:(u + 1) * P], ident)
                last.then_inc(S("m_tr"), 1)

            m_scores(0)
            pe.wait_ge(S("ro_squared"), 1)
            for b in range(4):
                last = pe.matmul(ps[:, 2 + b, :], ones, tmp[:, 2 * b:2 * b + 2, :].rearrange("p c t -> p (c t)"), start=True, stop=True)
            last.then_inc(S("ro_summed"), 1)
            for n in range(4):
                t, hg = n // 2, n % 2
                if n < 3:
                    m_scores(n + 1)
                pe.wait_ge(S("m_p"), n + 1)
                if n >= 2:
                    pe.wait_ge(S("m_lo"), n - 1)
                m_turn(n, 0)
                for h in range(4):
                    m, hh = 4 * n + h, 4 * hg + h
                    if h < 3:
                        m_turn(n, h + 1)
                    pe.wait_ge(S("m_pt"), m + 1)
                    r = 64 * (hh % 2)
                    for u in range(t + 1):
                        last = pe.matmul(ps[r:r + 64, 6 + n % 2, (h // 2) * P:(h // 2 + 1) * P], vtok2[:, u, 1024 + hh * MD:1024 + (hh + 1) * MD],
                                         pt2[:, m % 2, u * P:(u + 1) * P], start=u == 0, stop=u == t)
                last.then_inc(S("m_o"), 1)
            pe.wait_ge(S("m_lo"), 4)
            tiles(pe, "retw", segment_T(pe, "retw", hhi, hlo, "ya_kept"))
            pe.wait_ge(S("ya_kept"), KC)
            tiles(pe, "mobw", segment_T(pe, "mobw", mbhi, mblo, "yb_kept", nk=4))
            pe.wait_ge(S("merged_lo"), KC)
            new_x("out2", 3, 2 * KC)

            tiles(pe, "pq", segment_T(pe, "pq", hhi, hlo, "q_lo", norm=3))
            pe.wait_ge(S("q_lo"), 16)

            def subk(i, j):
                g = BASE["subk"] + j
                pe.wait_ge(lo_made, nth(g))
                for t in range(TT):
                    for c in range(8):
                        s, w = slice(t * P, (t + 1) * P), slice(c * P, (c + 1) * P)
                        o = ps[:, 4 * j + 2 * t + c // 4, (c % 4) * P:(c % 4 + 1) * P]
                        pe.matmul(o, qhi[:, 8 * j + c, s], whi[:, g % RING, w], start=True, stop=False)
                        pe.matmul(o, qlo[:, 8 * j + c, s], whi[:, g % RING, w], start=False, stop=False)
                        last = pe.matmul(o, qhi[:, 8 * j + c, s], wlo[:, g % RING, w], start=False, stop=True)
                last.then_inc(tile_used, 1)
            tiles(pe, "subk", subk, loop=False)
            pe.wait_ge(S("scores_kept"), 2 * TT)
            pre = segment_T(pe, "u", hhi, hlo, "g_made")
            tiles(pe, "u", pre, 0, 102)
            pe.wait_ge(S("gates_made"), 1)
            for n in range(3):
                for t in range(TT):
                    s = ctop[:, t * PH:(t + 1) * PH, :] if n == 2 else pidx[:, n, t * PH:(t + 1) * PH, :]
                    last = pe.transpose(ps[:, 3 + n, t * P:(t + 1) * P], s.rearrange("p h k -> p (h k)"), ident)
            last.then_inc(S("pairs_turned"), 1)
            tiles(pe, "u", pre, 102, 128)

            def outer(i, q):
                pe.wait_ge(S("e1_made"), 2 * i + (q + 1))
                pe.wait_ge(S("e2_made"), 2 * i + (q + 1))
                wait(pe, S("outer_multiplied"), 2 * i + (q - 1))
                for a in range(4):
                    last = pe.matmul(ps[:, 4 + q % 2, a * P:(a + 1) * P], e1[:, q % 2, a, :], e2[:, q % 2, a, :], start=True, stop=True)
                last.then_inc(S("outer_made"), 1)
            outer(0, 0)
            outer(0, 1)
            with pe.Fori(0, SEQ // 8 - 1) as i:
                outer(i, 2)
                outer(i, 3)
            for t in range(TT):
                for c in range(KC):
                    pe.matmul(ps[:, 2 * t + c // 4, (c % 4) * P:(c % 4 + 1) * P], x[:, c, t * P:(t + 1) * P], ident, start=c % 4 == 0, stop=False, skip_group_check=True)

            def vals(i, j):
                g = BASE["v"] + j
                pe.wait_ge(lo_made, 4 * i + nth(g))
                pe.wait_ge(S("mlo_made"), 4 * i + (j + 1))
                for t in range(TT):
                    for n in range(2):
                        o, s, w = ps[:, 2 * t + n, :], slice(t * P, (t + 1) * P), slice(n * 512, n * 512 + 512)
                        stop = isinstance(i, int) and j == NKEY - 1
                        pe.matmul(o, mhi[:, g % RING, s], whi[:, g % RING, w], start=False, stop=False, skip_group_check=True)
                        pe.matmul(o, mhi[:, g % RING, s], wlo[:, g % RING, w], start=False, stop=False, skip_group_check=True)
                        last = pe.matmul(o, mlo[:, g % RING, s], whi[:, g % RING, w], start=False, stop=stop, skip_group_check=True)
                last.then_inc(tile_used, 1)
            tiles(pe, "v", vals)

        @block.scalar
        def _(act):
            steps = [0]

            def link(ins):
                steps[0] += 1
                ins.then_inc(S("act_step"), 1)
                act.wait_ge(S("act_step"), steps[0])

            def hi_only(name):
                return lambda i, j: split_hi(act, BASE[name] + j + LEAD, i)

            def norm_square(k, c):
                if k:
                    act.wait_ge(S("x_new"), KC * (k - 1) + c + 1)
                act.activation(tmp[:, c, :], x[:, c, :], ACT.Square).then_inc(S("norm_squared"), 1)

            def norm_squares(k):
                for c in range(KC):
                    norm_square(k, c)

            def new_x(name, k):
                def body(i, j):
                    split_hi(act, BASE[name] + j + LEAD)
                    if j:
                        norm_square(k, j - 1)
                tiles(act, name, body)
                norm_square(k, KC - 1)

            def norm_root(k):
                act.wait_ge(S("norm_summed"), k + 1)
                link(act.activation(rs[:, 0, :], ps[:, 4, 0:SEQ], ACT.Ln, bias=epsc[:, :], scale=1.0 / D))
                act.activation(rs[:, 0, :], rs[:, 0, :], ACT.Exp, scale=-0.5).then_inc(S("norm_root"), 1)

            def norm_out(k):
                for c in range(KC):
                    act.wait_ge(S("norm_scaled"), KC * k + c + 1)
                    act.activation(hhi[:, c, :], tmp[:, c, :], ACT.Identity, bias=shifts[:, k, c:c + 1]).then_inc(S("h_hi"), 1)

            act.wait_ge(S("prm_in"), 32)
            act.activation(csl[:, :], prm[:, 96:104], ACT.Silu).then_inc(S("c_silu"), 1)
            act.wait_ge(S("x_in"), 16)
            norm_squares(0)
            act.wait_ge(S("eps_made"), 1)
            norm_root(0)
            for g in range(LEAD):
                split_hi(act, RAW1 + g)
            norm_out(0)

            def win(i, j):
                g = BASE["win"] + j
                split_hi(act, g + LEAD, i)
                act.wait_ge(tile_used, 4 * i + nth(g))
                act.activation(pick(proj, 4 * i + j), chunk_bank(g), ACT.Copy).then_inc(S("win_kept"), 1)
            tiles(act, "win", win)
            act.wait_ge(S("h_lo"), KC)
            for c in range(KC):
                last = act.activation(tmp[:, c, :], tmp[:, c, :], ACT.Identity, bias=shifts[:, 0, c:c + 1])
                if c % 4 == 3:
                    split_hi(act, BASE["tok"] + c // 4 + LEAD)
            last.then_inc(S("h_made"), 1)
            act.wait_ge(tile_used, nth(BASE["tok"] + 1))
            for t in range(TT):
                act.activation(vtok[:, t, :], ps[:, 4 + t, 0:256], ACT.Copy).then_inc(S("vtok_made"), 1)
            act.wait_ge(S("small_made"), 1)
            act.activation(small[:, :, :], ps[:, 3, 0:64].rearrange("p (t c) -> p t c", t=2)[:, :, 0:20], ACT.Copy).then_inc(S("small_kept"), 1)
            act.wait_ge(S("conv_tap"), 4 * CONV)
            act.activation(proj[:, 0:CONV, :], cv[:, :, :], ACT.Silu).then_inc(S("conv_silu"), 1)
            act.activation(proj[:, C_GZ:C_GZ + 4, :], proj[:, C_GZ:C_GZ + 4, :], ACT.Silu).then_inc(S("conv_silu"), 1)
            act.wait_ge(S("conv_silu"), 2)
            act.activation(sq[:, 0:8 * SEQ], proj[:, 0:8, :].rearrange("p c t -> p (c t)"), ACT.Square).then_inc(S("heads_squared"), 1)
            act.activation(sq[:, 8 * SEQ:14 * SEQ], proj[:, C_NQ:C_NQ + 6, :].rearrange("p c t -> p (c t)"), ACT.Square).then_inc(S("heads_squared"), 1)
            act.wait_ge(S("z_made"), 1)
            link(act.activation(gsm[:, 16:24], gsm[:, 16:24], ACT.Exp, scale=-1.0))
            link(act.activation(gsm[:, 16:24], gsm[:, 16:24], ACT.Ln, bias=1.0))
            act.activation(gsm[:, 24:28], prm[:, 89:93], ACT.Exp)
            act.activation(small[:, :, 4:20], small[:, :, 4:20], ACT.Exp, scale=-1.0).then_inc(S("gates_exp"), 1)
            act.wait_ge(S("heads_summed"), 1)
            act.activation(rs[:, 0:8, :].rearrange("p a b -> p (a b)"), bank(0, 4), ACT.Ln, bias=epsc[:, :])
            link(act.activation(rs[:, 8:14, :].rearrange("p a b -> p (a b)"), bank(4, 3), ACT.Ln, bias=epsc[:, :], scale=1.0 / HEAD))
            act.activation(rs[:, :, :], rs[:, :, :], ACT.Exp, scale=-0.5).then_inc(S("heads_root"), 1)
            act.wait_ge(raw_used, nth(BASE["cmp"] + 7))
            act.activation(hid[:, :, :], ps[:, 7, 0:2 * CPAD].rearrange("p (a b) -> p a b", a=2), ACT.Silu).then_inc(S("hid_made"), 1)
            act.wait_ge(S("cmp_made"), 1)
            link(act.activation(kc[:, :], ps[:, 7, 64:64 + CPAD], ACT.Copy))
            act.activation(sqc[:, :], kc[:, :], ACT.Square).then_inc(S("cmp_squared"), 1)
            act.activation(vc[0:CPAD, :], ps[0:CPAD, 7, P:2 * P], ACT.Copy).then_inc(S("vc_made"), 1)
            act.wait_ge(S("cmp_summed"), 1)
            link(act.activation(rsc[:, :], ps[:, 7, 0:CPAD], ACT.Ln, bias=epsc[:, :], scale=1.0 / HEAD))
            act.activation(rsc[:, :], rsc[:, :], ACT.Exp, scale=-0.5).then_inc(S("cmp_root"), 1)
            act.wait_ge(S("diff_made"), 1)
            act.activation(DT[:, :, :], DT[:, :, :], ACT.Exp).then_inc(S("DT_exp"), 1)
            act.wait_ge(S("sums_kept"), 1)
            act.activation(gsm[:, 40:48], gsm[:, 32:40], ACT.Exp)
            for h in range(GH):
                act.activation(gsm[:, 48 + h:49 + h], gsm[:, 32 + h:33 + h], ACT.Exp, bias=gcB[:, h, P - 1:P], scale=-1.0)
            act.activation(eg[:, :, :], gcB[:, 4:8, :], ACT.Exp).then_inc(S("eg_made"), 1)
            act.wait_ge(S("kk_made"), 1)
            act.activation(vb[:, :, :].rearrange("p a b -> p (a b)"), bank(6, 2), ACT.Copy).then_inc(S("vt_kept"), 1)
            for l in range(LEVELS):
                for b in range(2):
                    act.wait_ge(S("inv_x"), 2 * l + b + 1)
                    if l:
                        act.wait_ge(S("inv_y"), 2 * (l - 1) + b + 1)
                    act.activation(Xs[:, 4 * b:4 * b + 4, :].rearrange("p a b -> p (a b)"), bank(b), ACT.Copy).then_inc(S("inv_xs"), 1)
            act.wait_ge(S("uw_made"), 1)
            act.activation(wT[:, :, :].rearrange("p a b -> p (a b)"), bank(2), ACT.Copy)
            act.activation(U[:, :, :].rearrange("p a b -> p (a b)"), bank(0, 2), ACT.Copy).then_inc(S("uw_kept"), 1)
            act.wait_ge(S("state_made"), 1)
            act.activation(St[:, :, :].rearrange("p a b -> p (a b)"), bank(3), ACT.Copy).then_inc(S("state_kept"), 1)
            act.wait_ge(S("og_made"), 1)
            link(act.activation(og[:, :, 0:P], ps[:, 5, :].rearrange("p (h t) -> p h t", h=GH), ACT.Copy))
            link(act.activation(og[:, :, P:SEQ], ps[:, 6, :].rearrange("p (h t) -> p h t", h=GH), ACT.Copy))
            act.activation(ogsq[:, :], og[:, :, :].rearrange("p h t -> p (h t)"), ACT.Square).then_inc(S("og_squared"), 1)
            act.wait_ge(S("og_summed"), 1)
            link(act.activation(rs[:, 0:4, :].rearrange("p a b -> p (a b)"), bank(0, 2), ACT.Ln, bias=epsc[:, :], scale=1.0 / HEAD))
            act.activation(rs[:, 0:4, :], rs[:, 0:4, :], ACT.Exp, scale=-0.5).then_inc(S("og_root"), 1)
            for g in range(LEAD):
                split_hi(act, BASE["wout"] + g)
            act.wait_ge(S("og_done"), 1)
            act.activation(hhi[:, 0:4, :], og[:, :, :], ACT.Copy).then_inc(S("og_hi"), 1)
            def nsa_exps(t):
                W = (t + 1) * P
                act.wait_ge(S("nsa_max"), t + 1)
                for h in range(NH):
                    for kk in range(2):
                        s = sp_[:, t, h, kk * 256:kk * 256 + W]
                        act.activation(s, s, ACT.Exp, bias=nst[:, t, 2 * h + kk:2 * h + kk + 1], accum_out=nst[:, t, 16 + 2 * h + kk:17 + 2 * h + kk])
                    act.activation(spc[:, t, h, :], spc[:, t, h, :], ACT.Exp, bias=nst[:, t, 8 + h:9 + h], accum_out=nst[:, t, 24 + h:25 + h]).then_inc(S("nsa_exp"), 1)
            nsa_exps(0)
            for t in range(TT):
                W = (t + 1) * P
                for h in range(NH):
                    m = NH * t + h
                    act.wait_ge(S("nsa_tr"), m + 1)
                    act.activation(pt[:, m % 2, 0:2 * W], ps[:, 5 + m % 2, 0:2 * W], ACT.Copy)
                    act.activation(ptc[0:CPAD, m % 2, :], turned_cmp(m), ACT.Copy).then_inc(S("nsa_pt"), 1)
                if t == 0:
                    nsa_exps(1)
                act.wait_ge(S("nsa_o"), t + 1)
                act.activation(hhi[:, 4:8, t * P:(t + 1) * P], ps[:, 7, :].rearrange("p (h q) -> p h q", h=NH), ACT.Copy).then_inc(S("mix_hi"), 1)
            act.wait_ge(S("mix_lo"), TT)
            new_x("wout", 1)
            norm_root(1)
            norm_out(1)

            def up(i, j):
                g, m = BASE["up"] + j, j // 2
                split_hi(act, g + LEAD, i)
                act.wait_ge(tile_used, 4 * i + nth(g))
                wait(act, S("up_used"), 2 * i + (m - 1))
                w = pick(upc, 4 * i + j)
                act.activation(uc[:, j % 4, :], chunk_bank(g), ACT.Identity, bias=w[:, 3:4], scale=w[:, 2:3]).then_inc(S("up_scaled"), 1)
                if j % 2:
                    act.wait_ge(S("up_kept"), 4 * i + j)
                    act.activation(uc[:, j % 4 - 1, :], uc[:, j % 4 - 1, :], ACT.Silu).then_inc(S("up_silu"), 1)
                    if j > 1:
                        act_hi(i, m - 1)

            def act_hi(i, m):
                act.wait_ge(S("up_used"), 2 * i + (m + 1))
                act.activation(pick(ahi, 2 * i + m), upp[:, m % 2, :], ACT.Copy).then_inc(S("act_hi"), 1)

            act.wait_ge(S("up_in"), 16)
            act.wait_ge(S("zf_made"), 1)
            act.activation(zz[:, :], zf[:, :], ACT.Copy).then_inc(S("zeros_made"), 1)
            tiles(act, "up", up)
            act_hi(0, FC - 1)
            tiles(act, "down", hi_only("down"))
            norm_squares(2)
            norm_root(2)
            norm_out(2)

            act.wait_ge(S("line_psum"), 1)
            act.activation(line[:, :], ps[0:MH, 5, :], ACT.Copy).then_inc(S("line_made"), 1)

            def in2(i, j):
                g = BASE["in2"] + j
                split_hi(act, g + LEAD, i)
                act.wait_ge(tile_used, 4 * i + nth(g))
                act.activation(pick(proj2, 4 * i + j), chunk_bank(g), ACT.Copy).then_inc(S("in2_kept"), 1)
            tiles(act, "in2", in2)

            def tok2(i, j):
                split_hi(act, BASE["tok2"] + j + LEAD)
                if j == 0:
                    act.activation(proj2[:, C_RG:C_RG + 8, :], proj2[:, C_RG:C_RG + 8, :], ACT.Silu).then_inc(S("rg_silu"), 1)
                if j in (2, 4):
                    c = C_GA + 4 * (j - 2)
                    act.activation(proj2[:, c:c + 8, :], proj2[:, c:c + 8, :], ACT.Sigmoid).then_inc(S("ab_sig"), 1)
                if j == 6:
                    act.wait_ge(S("rotated"), 1)
                    act.activation(tmp[:, :, :], proj2[:, C_MQ:C_MQ + 8, :], ACT.Square).then_inc(S("m_squared"), 1)
                if j % 4 == 3:
                    n = j // 4
                    act.wait_ge(tile_used, nth(BASE["tok2"] + j))
                    for t in range(TT):
                        act.activation(vtok2[:, t, n * 512:(n + 1) * 512], ps[:, 2 * (n % 2) + t, :], ACT.Copy).then_inc(S("tok2_kept"), 1)
                if j == 9:
                    act.wait_ge(S("m_summed"), 1)
                    link(act.activation(rs[:, 0:8, :].rearrange("p a b -> p (a b)"), bank(4, 4), ACT.Ln, bias=epsc[:, :], scale=1.0 / MD))
                    act.activation(rs[:, 0:8, :], rs[:, 0:8, :], ACT.Exp, scale=-0.5).then_inc(S("m_root"), 1)
            tiles(act, "tok2", tok2, loop=False)
            for h in range(RH):
                act.wait_ge(S("ret_o"), h + 1)
                act.activation(ro[:, h, :], ps[:, 2 + h % 2, 0:SEQ], ACT.Copy).then_inc(S("ro_kept"), 1)
            act.wait_ge(S("ro_kept"), RH)
            act.activation(tmp[:, :, :], ro[:, :, :], ACT.Square).then_inc(S("ro_squared"), 1)

            def m_exps(n):
                W = (n // 2 + 1) * P
                act.wait_ge(S("m_max"), n + 1)
                if n >= 2:
                    act.wait_ge(S("m_tr"), 4 * (n - 1))
                for h in range(4):
                    s = 16 * (n % 2) + h
                    act.activation(sp2[:, n % 2, h, 0:W], ps[:, 2 * (n % 2) + h % 2, (h // 2) * SEQ:(h // 2) * SEQ + W], ACT.Exp, bias=mst[:, s:s + 1], accum_out=mst[:, s + 4:s + 5]).then_inc(S("m_exp"), 1)
            m_exps(0)
            act.wait_ge(S("ro_summed"), 1)
            act.activation(ya[:, :, :].rearrange("p a b -> p (a b)"), bank(2, 4), ACT.Ln, bias=epsc[:, :], scale=1.0 / RV).then_inc(S("ro_var"), 1)
            act.wait_ge(S("ro_var"), 1)
            act.activation(ya[:, :, :], ya[:, :, :], ACT.Exp, scale=-0.5).then_inc(S("ro_root"), 1)
            for n in range(4):
                t, hg = n // 2, n % 2
                W = (t + 1) * P
                for h in range(4):
                    m = 4 * n + h
                    act.wait_ge(S("m_tr"), m + 1)
                    act.activation(pt2[:, m % 2, 0:W], ps[:, 4 + m % 2, 0:W], ACT.Copy).then_inc(S("m_pt"), 1)
                    if h == 1 and n < 3:
                        m_exps(n + 1)
                if n == 1:
                    act.wait_ge(S("ro_done"), 1)
                    act.activation(hhi[:, :, :], ro[:, :, :], ACT.Copy).then_inc(S("ro_hi"), 1)
                act.wait_ge(S("m_o"), n + 1)
                act.activation(mbhi[:, 2 * hg:2 * hg + 2, t * P:(t + 1) * P], ps[:, 6 + n % 2, 0:2 * P].rearrange("p (c q) -> p c q", c=2), ACT.Copy).then_inc(S("m_hi"), 1)
            tiles(act, "retw", hi_only("retw"))
            def mobw(i, j):
                split_hi(act, BASE["mobw"] + j + LEAD)
                for c in (2 * j, 2 * j + 1):
                    act.wait_ge(S("merged"), c + 1)
                    act.activation(hhi[:, c, :], ya[:, c, :], ACT.Copy).then_inc(S("merged_hi"), 1)
            act.wait_ge(tile_used, nth(BASE["mobw"] - 1))
            tiles(act, "mobw", mobw)
            new_x("out2", 3)
            norm_root(3)
            norm_out(3)

            def pq(i, j):
                g = BASE["pq"] + j
                split_hi(act, g + LEAD, i)
                act.wait_ge(tile_used, 4 * i + nth(g))
                act.activation(pick(qhi, 4 * i + j), chunk_bank(g), ACT.Copy).then_inc(S("q_hi"), 1)
            tiles(act, "pq", pq)

            def subk(i, j):
                split_hi(act, BASE["subk"] + j + LEAD)
                act.wait_ge(tile_used, nth(BASE["subk"] + j))
                for t in range(TT):
                    act.activation(sc[:, t * 16 + 8 * j:t * 16 + 8 * j + 8, :].rearrange("p a b -> p (a b)"), bank(4 * j + 2 * t, 2), ACT.Copy).then_inc(S("scores_kept"), 1)
            tiles(act, "subk", subk, loop=False)

            def exps(i, j):
                g = BASE["u"] + j
                split_hi(act, g + LEAD, i)
                act.wait_ge(tile_used, 4 * i + nth(g))
                act.activation(pick(G, 4 * i + j), chunk_bank(g), ACT.Gelu).then_inc(S("g_made"), 1)
            tiles(act, "u", exps, 0, 100)
            act.wait_ge(S("gate_shifted"), 1)
            act.activation(ctop[:, :, :], ctop[:, :, :], ACT.Exp).then_inc(S("gate_exp"), 1)
            tiles(act, "u", exps, 100, 104)
            act.wait_ge(S("routed"), 1)
            tiles(act, "u", exps, 104, 128)
            def distances(i, q):
                for a in range(4):
                    tok = 4 * q + a if isinstance(i, int) else 16 * i + (4 * q + a)
                    act.activation(dist[:, q % 4, a, :], iota, ACT.Abs, bias=col(pair[:, 0, :], tok), scale=-1.0).then_inc(S("dist_made"), 1)

            def first_rows(i, q):
                if q + 1 < SEQ // 4:
                    distances(i, q + 1)
                act.wait_ge(S("dist_made"), 16 * i + 4 * (q + 1))
                wait(act, S("outer_made"), 4 * i + (q - 1))
                act.activation(e1[:, q % 2, :, :], dist[:, q % 4, :, :], ACT.Relu, bias=1.0, scale=-1.0).then_inc(S("e1_made"), 1)
            act.wait_ge(tile_used, nth(BASE["v"] - 1))
            distances(0, 0)
            for q in range(4):
                first_rows(0, q)
            with act.Fori(0, SEQ // 16 - 2) as i:
                for q in range(4, 8):
                    first_rows(i, q)
            for q in range(SEQ // 4 - 4, SEQ // 4):
                first_rows(0, q)
            act.wait_ge(S("outer_multiplied"), SEQ // 4)

            def m_hi(i, j):
                if j < NKEY:
                    act.activation(mhi[:, (BASE["v"] + j) % RING, :], pick(G, 4 * i + j), ACT.Copy).then_inc(S("mhi_made"), 1)
            for j in range(LEAD):
                m_hi(0, j)

            def vals(i, j):
                split_hi(act, BASE["v"] + j + LEAD, i)
                m_hi(i, j + LEAD)
            tiles(act, "v", vals)
            act.wait_ge(tile_used, nth(TOTAL - 1))
            for t in range(TT):
                act.activation(y[:, t, :], bank(2 * t, 2), ACT.Copy).then_inc(S("y_made"), 1)

        @block.vector
        def _(dve):
            steps = [0]

            def link(ins):
                steps[0] += 1
                ins.then_inc(S("dve_step"), 1)
                dve.wait_ge(S("dve_step"), steps[0])

            def lo_only(name):
                return lambda i, j: split_lo(dve, BASE[name] + j + LEAD, i)

            def over(t, n):
                return t.rearrange("p (o t) -> p o t", o=1).to_broadcast([P, n, t.shape[-1]])

            def flat(t):
                return t.rearrange("p a b -> p (a b)")

            def norm(k):
                dve.wait_ge(S("norm_root"), k + 1)

                def lower(c):
                    dve.wait_ge(S("h_hi"), KC * k + c + 1)
                    dve.scalar_tensor_tensor(hlo[:, c, :], tmp[:, c, :], shifts[:, k, c:c + 1], hhi[:, c, :].bitcast(f32), add, sub).then_inc(S("h_lo"), 1)
                for c in range(KC):
                    dve.scalar_tensor_tensor(tmp[:, c, :], x[:, c, :], gains[:, k, c:c + 1], rs[:, 0, :], mul, mul).then_inc(S("norm_scaled"), 1)
                    if c >= 2:
                        lower(c - 2)
                lower(KC - 2)
                lower(KC - 1)

            dve.memset(shifts[:, :, :], 0.0)
            dve.memset(blk[:, :, :, :], 0.0)
            dve.memset(epsc[:, :], EPS).then_inc(S("eps_made"), 1)
            dve.wait_ge(S("c_silu"), 1)
            def ada(g0, count):
                for r in range(g0, g0 + count):
                    n, k, g = r // KC, r % KC, ada_tile(r)
                    dve.wait_ge(w_loaded[g % RING], 16 * (g // RING + 1))
                    ways = 2 if n < 2 else 1
                    o = acc[:, n, k % 2, :] if n < 2 else acc2[:, n % 2, :]
                    if k < ways:
                        if n >= 4 and k == 0:
                            dve.wait_ge(S("mod_summed"), n - 1)
                        dve.tensor_scalar(o, raw[:, g % RING, :], csl[:, k:k + 1], None, mul).then_inc(raw_used, 1)
                    else:
                        dve.wait_ge(raw_used, nth(g) - ways)
                        dve.scalar_tensor_tensor(o, raw[:, g % RING, :], csl[:, k:k + 1], o, mul, add).then_inc(raw_used, 1)
            ada(0, RAW1)
            def factors(k, o, source):
                link(dve.tensor_tensor(mod[:, o], source, prm[:, 104 + o.start:104 + o.stop], add))
                dve.scalar_tensor_tensor(gains[:, k, :], mod[:, 24 * k + 8:24 * k + 16], 1.0, prm[:, 8 * k:8 * k + 8], add, mul)
                dve.tensor_copy(shifts[:, k, :], mod[:, 24 * k:24 * k + 8])
                dve.tensor_copy(gains[:, 2 + k, :], prm[:, 16 + 8 * k:24 + 8 * k])
            dve.wait_ge(S("mod_summed"), 2)
            factors(0, slice(0, 16), ps[:, 1, 0:16])
            link(dve.memset(gsm[:, :], 0.0))
            for g in range(LEAD):
                split_lo(dve, RAW1 + g)
            norm(0)

            def conv(i, j):
                dve.wait_ge(S("win_kept"), 4 * i + (j + 1))
                src, o = pick(proj, 4 * i + j), pick(cv, 4 * i + j)
                w = pick(prm[:, 32:80].rearrange("p (n t) -> p n t", t=4), 4 * i + j)
                dve.tensor_scalar(o, src, w[:, 3:4], None, mul).then_inc(S("conv_tap"), 1)
                for tap in range(1, 4):
                    dve.wait_ge(S("conv_tap"), 16 * i + (4 * j + tap))
                    dve.scalar_tensor_tensor(o[:, tap:SEQ], src[:, 0:SEQ - tap], w[:, 3 - tap:4 - tap], o[:, tap:SEQ], mul, add).then_inc(S("conv_tap"), 1)

            def win(i, j):
                split_lo(dve, BASE["win"] + j + LEAD, i)
                if j:
                    conv(i, j - 1)
            tiles(dve, "win", win, 0, CONV)
            conv(0, CONV - 1)
            tiles(dve, "win", lo_only("win"), CONV)
            tiles(dve, "tok", lo_only("tok"))
            dve.wait_ge(S("win_kept"), 24)
            for kv in range(2):
                src = proj[:, C_KC + kv, :]
                span = bass.AP(tensor=src.tensor, offset=src.offset, ap=[src.ap[0], [1, CMP_BLOCK], [CMP_STRIDE, N_CMP]])
                pos = prm[:, 152 + 32 * kv:184 + 32 * kv].rearrange("p (l o) -> p l o", o=1).to_broadcast([P, CMP_BLOCK, N_CMP])
                last = dve.tensor_tensor(blk[:, kv, :, 0:N_CMP], span, pos, add)
            last.then_inc(S("blk_made"), 1)
            dve.wait_ge(S("small_kept"), 1)
            for t in range(TT):
                last = dve.tensor_tensor(gsm[:, 4 * t:4 * t + 4], small[:, t, 0:4], prm[:, 85:89], add)
            link(last)
            dve.tensor_scalar(gsm[:, 56:64], gsm[:, 0:8], 0.0, None, ALU.max)
            link(dve.tensor_scalar(gsm[:, 64:72], gsm[:, 0:8], -1.0, None, mul))
            dve.tensor_tensor(gsm[:, 16:24], gsm[:, 0:8], gsm[:, 64:72], ALU.max).then_inc(S("z_made"), 1)
            dve.wait_ge(S("gates_exp"), 1)
            link(dve.tensor_scalar(small[:, :, 4:20], small[:, :, 4:20], 1.0, None, add))
            link(dve.reciprocal(small[:, :, 4:20], small[:, :, 4:20]))
            link(dve.tensor_tensor(gsm[:, 56:64], gsm[:, 56:64], gsm[:, 16:24], add))
            for t in range(TT):
                dve.scalar_tensor_tensor(gsm[:, 4 * t:4 * t + 4], gsm[:, 56 + 4 * t:60 + 4 * t], -1.0, gsm[:, 24:28], mul, mul)
                last = dve.tensor_copy(gsm[:, 8 + 4 * t:12 + 4 * t], small[:, t, 4:8])
            last.then_inc(S("decay_made"), 1)
            dve.wait_ge(S("heads_root"), 1)
            dve.wait_ge(S("conv_silu"), 2)
            root = float(HEAD) ** -0.5
            dve.scalar_tensor_tensor(flat(proj[:, 0:4, :]), flat(proj[:, 0:4, :]), root, flat(rs[:, 0:4, :]), mul, mul)
            dve.tensor_tensor(flat(proj[:, 4:8, :]), flat(proj[:, 4:8, :]), flat(rs[:, 4:8, :]), mul)
            link(dve.scalar_tensor_tensor(flat(proj[:, C_NQ:C_NQ + 4, :]), flat(proj[:, C_NQ:C_NQ + 4, :]), prm[:, 81:82], flat(rs[:, 8:12, :]), mul, mul))
            link(dve.tensor_scalar(flat(proj[:, C_NQ:C_NQ + 4, :]), flat(proj[:, C_NQ:C_NQ + 4, :]), root, None, mul))
            dve.scalar_tensor_tensor(proj[:, C_KS, :], proj[:, C_KS, :], prm[:, 83:84], rs[:, 12, :], mul, mul)
            dve.scalar_tensor_tensor(proj[:, C_KW, :], proj[:, C_KW, :], prm[:, 84:85], rs[:, 13, :], mul, mul)
            dve.wait_ge(raw_used, nth(BASE["cmp"] + 7))
            ada(RAW1, 3)
            dve.wait_ge(S("sums_made"), 1)
            dve.tensor_copy(flat(gcB[:, :, :]), bank(0, 2))
            dve.tensor_copy(gsm[:, 32:40], ps[:, 4, 0:8]).then_inc(S("sums_kept"), 1)
            for t in range(TT):
                last = dve.tensor_tensor(kbT[:, :, t * P:(t + 1) * P], ps[:, 2 + t, :].rearrange("p (h c) -> p h c", h=GH), proj[:, 4:8, t * P:(t + 1) * P], mul)
            last.then_inc(S("kbT_made"), 1)
            dve.wait_ge(S("sums_kept"), 1)
            for p in range(8):
                last = dve.tensor_scalar(DT[:, p, :], gcB[:, p, :], gsm[:, 32 + p:33 + p], 0.0, sub, ALU.min)
            last.then_inc(S("diff_made"), 1)
            for t in (Tm, TTm):
                last = dve.tensor_copy(t[:, :, :], over(ident, 8))
            dve.wait_ge(S("cmp_root"), 1)
            dve.scalar_tensor_tensor(kc[:, :], kc[:, :], prm[:, 82:83], rsc[:, :], mul, mul)
            dve.wait_ge(S("DT_exp"), 1)
            link(dve.tensor_tensor(DT[:, :, :], DT[:, :, :], over(tri, 8), mul))
            dve.wait_ge(S("kk_made"), 1)
            dve.tensor_tensor(flat(QT[:, :, :]), flat(DT[:, :, :]), bank(2, 2), mul)
            link(dve.tensor_tensor(flat(AT[:, :, :]), flat(DT[:, :, :]), bank(0, 2), mul))

            def masked(l):
                for b in range(2):
                    if l:
                        dve.wait_ge(S("inv_x"), 2 * (l - 1) + b + 1)
                    dve.tensor_tensor(BT[:, 4 * b:4 * b + 4, :], AT[:, 4 * b:4 * b + 4, :], over(lvl[:, l, :], 4), mul).then_inc(S("lvl_masked"), 1)
            masked(0)
            dve.wait_ge(S("eg_made"), 1)
            link(dve.tensor_tensor(gsm[:, 52:56], gsm[:, 12:16], gsm[:, 44:48], mul))
            dve.tensor_tensor(qd[:, :, :], proj[:, 0:4, P:SEQ], eg[:, :, :], mul)
            dve.wait_ge(S("vt_kept"), 1)
            for p in range(8):
                h = p % 4
                dve.tensor_scalar(vb[:, p, :], vb[:, p, :], gsm[:, 8 + p:9 + p], None, mul)
                f = 52 + h if p >= 4 else 48 + h
                last = dve.tensor_scalar(kw[:, p, :], ps[:, 4 + p // 4, h * P:(h + 1) * P], gsm[:, f:f + 1], None, mul)
            last.then_inc(S("kv_scaled"), 1)
            for l in range(LEVELS):
                if l + 1 < LEVELS:
                    masked(l + 1)
                for b in range(2):
                    ada(RAW1 + 3 + 3 * l + 2 * b, 2 - b)
                    dve.wait_ge(S("inv_y"), 2 * l + b + 1)
                    o = slice(4 * b, 4 * b + 4)
                    dve.tensor_tensor(flat(Tm[:, o, :]), flat(Tm[:, o, :]), bank(2 + b), sub)
                    dve.tensor_tensor(flat(TTm[:, o, :]), flat(TTm[:, o, :]), bank(4 + b), sub).then_inc(S("inv_updated"), 1)
            ada(RAW1 + 24, 2)
            dve.wait_ge(S("uw_kept"), 1)
            dve.wait_ge(S("ws_made"), 1)
            dve.tensor_tensor(flat(U[:, 4:8, :]), flat(U[:, 4:8, :]), bank(4), sub).then_inc(S("vnew_made"), 1)
            ada(RAW1 + 26, 6)
            dve.wait_ge(S("og_root"), 1)
            link(dve.scalar_tensor_tensor(flat(og[:, :, :]), flat(og[:, :, :]), prm[:, 80:81], flat(rs[:, 0:4, :]), mul, mul))
            dve.tensor_tensor(og[:, :, :], og[:, :, :], proj[:, C_GZ:C_GZ + 4, :], mul).then_inc(S("og_done"), 1)
            dve.wait_ge(S("mod_summed"), 6)
            factors(1, slice(16, 48), ps[:, 7, 0:32])
            for g in range(LEAD):
                split_lo(dve, BASE["wout"] + g)
            dve.wait_ge(S("og_hi"), 1)
            dve.tensor_tensor(hlo[:, 0:4, :], og[:, :, :], hhi[:, 0:4, :].bitcast(f32), sub).then_inc(S("og_lo"), 1)

            def nsa_masked(t):
                W = (t + 1) * P
                dve.wait_ge(S("nsa_s"), t + 1)
                s = sp_[:, t, :, :].rearrange("p h (b k) -> p (h b) k", b=2)
                sums = ps[:, 0:NH, :].rearrange("p h (b k) -> p (h b) k", b=2)
                if t:
                    dve.tensor_copy(s[:, :, 0:P], sums[:, :, 0:P])
                dve.tensor_tensor(s[:, :, t * P:W], sums[:, :, t * P:W], over(nmask[:, :], 2 * NH), add)
                link(dve.tensor_tensor(spc[:, t, :, :], ps[:, 4, 0:NH * CPAD].rearrange("p (h c) -> p h c", h=NH), over(cmask[:, t, 0:CPAD], NH), add))
                dve.tensor_reduce(nst[:, t, 0:8], s[:, :, 0:W], X, ALU.max, negate=True)
                dve.tensor_reduce(nst[:, t, 8:12], spc[:, t, :, :], X, ALU.max, negate=True).then_inc(S("nsa_max"), 1)

            def nsa_weighed(t):
                W, n = (t + 1) * P, nst[:, t, :]
                dve.wait_ge(S("nsa_exp"), NH * (t + 1))
                link(dve.reciprocal(n[:, 32:44], n[:, 16:28]))
                g = small[:, t, 8:20].rearrange("p (h b) -> p h b", b=3)
                dve.tensor_tensor(n[:, 0:8].rearrange("p (h b) -> p h b", b=2), n[:, 32:40].rearrange("p (h b) -> p h b", b=2), g[:, :, 1:3], mul)
                link(dve.scalar_tensor_tensor(n[:, 8:12], n[:, 40:44], cmask[:, t, CPAD:CPAD + 1], g[:, :, 0], mul, mul))
                for h in range(NH):
                    for kk in range(2):
                        s = sp_[:, t, h, kk * 256:kk * 256 + W]
                        dve.tensor_scalar(s, s, n[:, 2 * h + kk:2 * h + kk + 1], None, mul)
                    dve.tensor_scalar(spc[:, t, h, :], spc[:, t, h, :], n[:, 8 + h:9 + h], None, mul).then_inc(S("nsa_p"), 1)
            nsa_masked(0)
            nsa_weighed(0)
            nsa_masked(1)
            nsa_weighed(1)
            for t in range(TT):
                dve.wait_ge(S("mix_hi"), t + 1)
                dve.tensor_tensor(hlo[:, 4:8, t * P:(t + 1) * P], ps[:, 7, :].rearrange("p (h q) -> p h q", h=NH), hhi[:, 4:8, t * P:(t + 1) * P].bitcast(f32), sub).then_inc(S("mix_lo"), 1)

            def wout(i, j):
                g = BASE["wout"] + j
                split_lo(dve, g + LEAD)
                dve.wait_ge(tile_used, nth(g))
                dve.scalar_tensor_tensor(x[:, j, :], chunk_bank(g), mod[:, 16 + j:17 + j], x[:, j, :], mul, add).then_inc(S("x_new"), 1)
            tiles(dve, "wout", wout)
            dve.memset(zf[:, :], 0.0).then_inc(S("zf_made"), 1)
            norm(1)

            def up(i, j):
                g, m, o = BASE["up"] + j, j // 2, uc[:, j % 4, :]
                split_lo(dve, g + LEAD, i)
                dve.wait_ge(S("up_scaled"), 4 * i + (j + 1))
                w = pick(upc, 4 * i + j)
                b = chunk_bank(g)
                dve.scalar_tensor_tensor(o[:, 1:SEQ], b[:, 0:SEQ - 1], w[:, 1:2], o[:, 1:SEQ], mul, add).then_inc(S("up_tap"), 1)
                dve.wait_ge(S("up_tap"), 4 * i + (j + 1))
                dve.scalar_tensor_tensor(o[:, 2:SEQ], b[:, 0:SEQ - 2], w[:, 0:1], o[:, 2:SEQ], mul, add).then_inc(S("up_kept"), 1)
                if j % 2:
                    dve.wait_ge(S("up_silu"), 2 * i + (m + 1))
                    dve.wait_ge(S("up_kept"), 4 * i + (j + 1))
                    dve.tensor_tensor(upp[:, m % 2, :], uc[:, j % 4 - 1, :], o, mul).then_inc(S("up_used"), 1)
                    if j > 1:
                        act_lo(i, m - 1)

            def act_lo(i, m):
                dve.wait_ge(S("act_hi"), 2 * i + (m + 1))
                dve.tensor_tensor(pick(alo, 2 * i + m), upp[:, m % 2, :], pick(ahi, 2 * i + m).bitcast(f32), sub).then_inc(S("act_lo"), 1)
            tiles(dve, "up", up)
            act_lo(0, FC - 1)
            tiles(dve, "down", lo_only("down"))
            dve.wait_ge(tile_used, nth(BASE["down"] + FC - 1))
            for c in range(KC):
                dve.scalar_tensor_tensor(x[:, c, :], ps[:, c // 2, (c % 2) * SEQ:(c % 2 + 1) * SEQ], mod[:, 40 + c:41 + c], x[:, c, :], mul, add).then_inc(S("x_new"), 1)
            dve.wait_ge(S("x_new"), 2 * KC)
            norm(2)

            dve.wait_ge(S("line_made"), 1)
            dve.memset(line[:, SEQ:2 * SEQ], NEG).then_inc(S("line_made"), 1)
            tiles(dve, "in2", lo_only("in2"))

            def tok2(i, j):
                split_lo(dve, BASE["tok2"] + j + LEAD)
                if j == 1:
                    dve.wait_ge(S("rot_made"), 1)
                    dve.tensor_tensor(proj2[:, 0:8, :], proj2[:, 0:8, :], over(rot[:, P:P + SEQ], 8), mul)
                    link(dve.tensor_tensor(tmp[:, :, :], ps[:, 4:8, :].rearrange("p b (c t) -> p (b c) t", c=2), over(rot[:, P + SEQ:P + 2 * SEQ], 8), mul))
                    dve.tensor_tensor(flat(proj2[:, 0:8, :]), flat(proj2[:, 0:8, :]), flat(tmp[:, :, :]), add).then_inc(S("rotated"), 1)
                if j == 9:
                    dve.wait_ge(S("tok2_kept"), 4)
                    rows = [vtok2[:, t, 0:1024].rearrange("p (h d) -> p h d", h=RH) for t in range(TT)]
                    for t in range(TT):
                        last = dve.tensor_reduce(vmean[:, 8 * t:8 * t + 8], rows[t], X, add)
                    link(last)
                    link(dve.tensor_scalar(vmean[:, :], vmean[:, :], 1.0 / RV, None, mul))
                    for t in range(TT):
                        last = dve.tensor_tensor(rows[t], rows[t], vmean[:, 8 * t:8 * t + 8].rearrange("p (h o) -> p h o", o=1).to_broadcast([P, RH, RV]), sub)
                    last.then_inc(S("v_centred"), 1)
            tiles(dve, "tok2", tok2, loop=False)
            link(dve.tensor_scalar(prm2[:, 2:3], prm2[:, 0:1], float(MD) ** -0.5, None, mul))
            dve.wait_ge(S("m_root"), 1)
            dve.scalar_tensor_tensor(flat(proj2[:, C_MQ:C_MQ + 4, :]), flat(proj2[:, C_MQ:C_MQ + 4, :]), prm2[:, 2:3], flat(rs[:, 0:4, :]), mul, mul)
            dve.scalar_tensor_tensor(flat(proj2[:, C_MK:C_MK + 4, :]), flat(proj2[:, C_MK:C_MK + 4, :]), prm2[:, 1:2], flat(rs[:, 4:8, :]), mul, mul).then_inc(S("mk_normed"), 1)
            dve.wait_ge(S("mk_normed"), 1)
            for h in range(RH):
                dve.wait_ge(S("ret_s"), h + 1)
                if h >= 2:
                    dve.wait_ge(S("ret_o"), h - 1)
                dve.tensor_tensor(pr[:, h % 2, 0:SEQ], ps[:, h % 2, 0:SEQ], dec[:, h, :], mul)
                dve.tensor_tensor(pr[:, h % 2, SEQ:SEQ + P], ps[:, h % 2, SEQ:SEQ + P], dec[:, h, 0:P], mul).then_inc(S("ret_p"), 1)

            def m_max(n):
                W = (n // 2 + 1) * P
                dve.wait_ge(S("m_s"), n + 1)
                for b in range(2):
                    last = dve.tensor_reduce(mst[:, 16 * (n % 2) + b:16 * (n % 2) + 4:2], ps[:, 2 * (n % 2) + b, :].rearrange("p (h k) -> p h k", h=2)[:, :, 0:W], X, ALU.max, negate=True)
                last.then_inc(S("m_max"), 1)

            def m_lower(n):
                dve.wait_ge(S("m_hi"), n + 1)
                o = (slice(2 * (n % 2), 2 * (n % 2) + 2), slice((n // 2) * P, (n // 2 + 1) * P))
                dve.tensor_tensor(mblo[:, o[0], o[1]], ps[:, 6 + n % 2, 0:2 * P].rearrange("p (c q) -> p c q", c=2), mbhi[:, o[0], o[1]].bitcast(f32), sub).then_inc(S("m_lo"), 1)
            m_max(0)
            for n in range(4):
                W, s = (n // 2 + 1) * P, 16 * (n % 2)
                dve.wait_ge(S("m_exp"), 4 * (n + 1))
                link(dve.reciprocal(mst[:, s + 8:s + 12], mst[:, s + 4:s + 8]))
                for h in range(4):
                    last = dve.tensor_scalar(sp2[:, n % 2, h, 0:W], sp2[:, n % 2, h, 0:W], mst[:, s + 8 + h:s + 9 + h], None, mul)
                last.then_inc(S("m_p"), 1)
                if n < 3:
                    m_max(n + 1)
                if n == 0:
                    dve.wait_ge(S("ro_root"), 1)
                    dve.wait_ge(S("rg_silu"), 1)
                    link(dve.tensor_tensor(flat(ro[:, :, :]), flat(ro[:, :, :]), flat(ya[:, :, :]), mul))
                    dve.tensor_tensor(flat(ro[:, :, :]), flat(ro[:, :, :]), flat(proj2[:, C_RG:C_RG + 8, :]), mul).then_inc(S("ro_done"), 1)
                if n:
                    m_lower(n - 1)
                if n == 2:
                    dve.wait_ge(S("ro_hi"), 1)
                    dve.tensor_tensor(hlo[:, :, :], ro[:, :, :], hhi[:, :, :].bitcast(f32), sub).then_inc(S("ro_lo"), 1)
            m_lower(3)

            dve.wait_ge(S("ab_sig"), 2)

            def retw(i, j):
                g = BASE["retw"] + j
                split_lo(dve, g + LEAD)
                dve.wait_ge(tile_used, nth(g))
                dve.tensor_tensor(ya[:, j, :], chunk_bank(g), proj2[:, C_GA + j, :], mul).then_inc(S("ya_kept"), 1)
            tiles(dve, "retw", retw)

            def merge(c):
                dve.wait_ge(S("yb_kept"), c + 1)
                dve.tensor_tensor(ya[:, c, :], ya[:, c, :], proj2[:, C_GB + c, :], add).then_inc(S("merged"), 1)

            def merge_lo(c):
                dve.wait_ge(S("merged_hi"), c + 1)
                dve.tensor_tensor(hlo[:, c, :], ya[:, c, :], hhi[:, c, :].bitcast(f32), sub).then_inc(S("merged_lo"), 1)

            def mobw(i, j):
                g = BASE["mobw"] + j
                split_lo(dve, g + LEAD)
                dve.wait_ge(tile_used, nth(g))
                for c in (2 * j, 2 * j + 1):
                    dve.tensor_tensor(proj2[:, C_GB + c, :], chunk_bank(c), proj2[:, C_GB + c, :], mul).then_inc(S("yb_kept"), 1)
                for c in (2 * j, 2 * j + 1):
                    merge(c)
                    if c >= 2:
                        merge_lo(c - 2)
            dve.wait_ge(S("ya_kept"), KC)
            tiles(dve, "mobw", mobw)
            merge_lo(KC - 2)
            merge_lo(KC - 1)

            def out2(i, j):
                g = BASE["out2"] + j
                split_lo(dve, g + LEAD)
                dve.wait_ge(tile_used, nth(g))
                dve.tensor_tensor(x[:, j, :], chunk_bank(g), x[:, j, :], add).then_inc(S("x_new"), 1)
            tiles(dve, "out2", out2)
            dve.wait_ge(S("x_new"), 3 * KC)
            norm(3)

            def pq(i, j):
                g = BASE["pq"] + j
                split_lo(dve, g + LEAD, i)
                dve.wait_ge(S("q_hi"), 4 * i + (j + 1))
                dve.tensor_tensor(pick(qlo, 4 * i + j), chunk_bank(g), pick(qhi, 4 * i + j).bitcast(f32), sub).then_inc(S("q_lo"), 1)
            tiles(dve, "pq", pq)
            tiles(dve, "subk", lo_only("subk"), loop=False)
            u_lo = lo_only("u")
            for j in range(4):
                u_lo(0, j)
            dve.wait_ge(S("scores_kept"), 2 * TT)

            def route(u):
                tile = [4]

                def step():
                    if tile[0] < 16:
                        u_lo(3 * u, tile[0])
                        tile[0] += 1
                    dve.drain()

                def top16(n, best, place, values, rest):
                    for m in range(n):
                        dve.max(best[:, m, 0:8], values(m))
                    step()
                    for m in range(n):
                        dve.match_replace(rest(m), in_to_replace=best[:, m, 0:8], in_values=values(m), imm_value=-3e38)
                        dve.max_index(place[:, m, 0:8], best[:, m, 0:8], values(m))
                    step()
                    for m in range(n):
                        dve.max(best[:, m, 8:16], rest(m))
                    step()
                    for m in range(n):
                        dve.max_index(place[:, m, 8:16], best[:, m, 8:16], rest(m))
                    step()

                dve.drain()
                dve.tensor_copy(scu[:, :, :], sc[:, bass.ds(4 * u, 4), :])
                step()
                top16(4, top8, tix, lambda m: scu[:, m, :], lambda m: scr[:, m, :])
                wide = [P, TOPK, TOPK]

                def along(t):
                    return t.rearrange("p (o e) -> p o e", o=1).to_broadcast(wide)

                def down_(t):
                    return t.rearrange("p (k o) -> p k o", o=1).to_broadcast(wide)
                dve.tensor_copy(tixf[:, :, :], tix[:, :, :])
                for m in range(2):
                    dve.tensor_tensor(cand[:, m, :, :], down_(top8[:, 2 * m, :]), along(top8[:, 2 * m + 1, :]), add)
                step()
                top16(2, cbu, cix, lambda m: cand[:, m, :, :].rearrange("p a b -> p (a b)"), lambda m: cand2[:, m, :])
                dve.tensor_copy(ctop[:, bass.ds(2 * u, 2), :], cbu[:, :, :])
                dve.tensor_scalar(cau[:, :, 0, :], cix[:, :, :], 4, None, ALU.logical_shift_right)
                dve.tensor_scalar(cau[:, :, 1, :], cix[:, :, :], TOPK - 1, None, ALU.bitwise_and)
                step()
                dve.tensor_copy(cab[:, :, :, :], cau[:, :, :, :])
                step()
                for m in range(4):
                    dve.tensor_tensor(eq[:, m % 2, m // 2, :, :], down_(cab[:, m // 2, m % 2, :]), along(iota[:, 0:TOPK]), ALU.is_equal)
                step()
                for m in range(4):
                    dve.tensor_tensor(eq[:, m % 2, m // 2, :, :], eq[:, m % 2, m // 2, :, :], along(tixf[:, m, :]), mul)
                step()
                for c in range(2):
                    dve.tensor_reduce(pidx[:, c, bass.ds(2 * u, 2), :], eq[:, c, :, :, :], X, add)
                assert tile[0] == 16

            with dve.Fori(0, TT * PH // 2) as u:
                route(u)
            dve.drain()
            link(dve.tensor_copy(gden[:, 0, :], ctop[:, :, 0]))
            wide = [P, TT * PH, TOPK]
            dve.tensor_tensor(ctop[:, :, :], ctop[:, :, :], gden[:, 0, :].rearrange("p (u o) -> p u o", o=1).to_broadcast(wide), sub).then_inc(S("gate_shifted"), 1)
            dve.wait_ge(S("gate_exp"), 1)
            link(dve.tensor_reduce(gden[:, 0, :], ctop[:, :, :], X, add))
            link(dve.reciprocal(gden[:, 1, :], gden[:, 0, :]))
            dve.tensor_tensor(ctop[:, :, :], ctop[:, :, :], gden[:, 1, :].rearrange("p (u o) -> p u o", o=1).to_broadcast(wide), mul).then_inc(S("gates_made"), 1)
            tiles(dve, "u", u_lo, 100, 102)
            dve.wait_ge(S("pairs_turned"), 1)
            dve.tensor_copy(pair[:, :, :], ps[:, 3:6, 0:SEQ]).then_inc(S("routed"), 1)
            tiles(dve, "u", u_lo, 102, 128)
            dve.wait_ge(S("routed"), 1)

            def rows(i, q):
                for a in range(4):
                    tok = 4 * q + a if isinstance(i, int) else 8 * i + (4 * q + a)
                    second, gate = col(pair[:, 1, :], tok), col(pair[:, 2, :], tok)
                    last = dve.tensor_scalar(e2[:, q % 2, a, :], iota, second, gate, ALU.is_equal, mul)
                last.then_inc(S("e2_made"), 1)

            def weigh(i, q):
                dve.wait_ge(S("outer_made"), 2 * i + (q + 1))
                toks = G[:, :, 4 * q:4 * q + 4] if isinstance(i, int) else G[:, :, bass.ds(8 * i + 4 * q, 4)]
                toks = toks.rearrange("p j t -> p t j")
                dve.tensor_tensor(toks, ps[:, 4 + q % 2, :].rearrange("p (t j) -> p t j", t=4), toks, mul).then_inc(S("outer_multiplied"), 1)
            dve.wait_ge(tile_used, nth(BASE["v"] - 1))
            rows(0, 0)
            dve.wait_ge(S("g_made"), NKEY)
            rows(0, 1)
            weigh(0, 0)
            with dve.Fori(0, SEQ // 8 - 1) as i:
                rows(i, 2)
                weigh(i, 1)
                rows(i, 3)
                weigh(i, 2)
            weigh(0, SEQ // 4 - 1)

            def m_lo(i, j):
                if j < NKEY:
                    dve.wait_ge(S("mhi_made"), 4 * i + (j + 1))
                    s = (BASE["v"] + j) % RING
                    dve.tensor_tensor(mlo[:, s, :], pick(G, 4 * i + j), mhi[:, s, :].bitcast(f32), sub).then_inc(S("mlo_made"), 1)
            dve.wait_ge(S("outer_multiplied"), SEQ // 4)
            for j in range(LEAD):
                m_lo(0, j)

            def vals(i, j):
                split_lo(dve, BASE["v"] + j + LEAD, i)
                m_lo(i, j + LEAD)
            tiles(dve, "v", vals)


_PARAMS = ["xT", "prm", "wsm", "w2", "upc", "prm2", "relb"]
_CONSTS = ["c_cst", "c_lvl", "c_nmask", "c_cmask", "c_rot", "c_dec", "c_relhot"]


def _constants():
    f = np.float32
    n = np.arange(P)
    cst = np.concatenate([np.eye(P), np.ones((P, P)), n[:, None] <= n[None, :], np.broadcast_to(n, (P, P))], 1).astype(f)
    lvl = np.zeros((P, LEVELS, P), f)
    for l in range(LEVELS):
        b = 1 << l
        same = (n[:, None] // (2 * b)) == (n[None, :] // (2 * b))
        lvl[:, l, :] = same & (n[:, None] % (2 * b) < b) & (n[None, :] % (2 * b) >= b)
    nmask = np.where(n[None, :] <= n[:, None], 0, NEG).astype(f)
    cmask = np.zeros((P, TT, CPAD + 1), f)
    for t in range(TT):
        q = t * P + n
        ends = np.arange(CPAD) * CMP_STRIDE + CMP_BLOCK - 1
        seen = (ends[None, :] <= q[:, None]) & (np.arange(CPAD) < N_CMP)[None, :]
        cmask[:, t, :CPAD] = np.where(seen, 0, NEG)
        cmask[:, t, CPAD] = seen.any(1)
    half = RQK // 2
    inv = f(10000.0) ** (-np.arange(half, dtype=f) / half)
    ang = np.arange(SEQ, dtype=f)[None, :] * inv.astype(f)[:, None]
    cos, sin = np.tile(np.cos(ang), (4, 1)), np.tile(np.sin(ang), (4, 1))
    perm = np.zeros((P, P), f)
    for m in range(P):
        if m % RQK < half:
            perm[m + half, m] = -1
        else:
            perm[m - half, m] = 1
    halves = (n[:, None] // MD == n[None, :] // MD)
    rot = np.concatenate([perm, cos, sin, halves, np.eye(P)[::-1]], 1).astype(f)
    log_g = np.log1p(-np.exp2(-5.0 - np.arange(RH)))
    d = np.arange(SEQ)[None, :] - n[:, None]
    dec = np.where(d[:, None, :] >= 0, np.exp(np.maximum(d, 0)[:, None, :] * log_g[None, :, None]), 0) * RQK ** -0.5
    dist = np.maximum(SEQ - 1 - np.arange(2 * SEQ), 0)
    exact = BUCKETS // 2
    large = exact + (np.log(np.maximum(dist, 1).astype(f) / exact) / f(math.log(MAXDIST / exact)) * (BUCKETS - exact)).astype(np.int32)
    bucket = np.where(dist < exact, dist, np.minimum(large, BUCKETS - 1))
    relhot = (np.arange(BUCKETS)[:, None] == bucket[None, :]).astype(f)
    return dict(c_cst=cst, c_lvl=lvl, c_nmask=nmask, c_cmask=cmask, c_rot=rot, c_dec=dec.astype(f), c_relhot=relhot)


def _chunks(w, nk=KC):
    n = w.shape[1] // P
    return w.reshape(nk, P, n, P).transpose(2, 1, 0, 3).reshape(n, P, nk * P)


def _rows(w, kk):
    return w.reshape(-1, kk, P, w.shape[1]).transpose(0, 2, 1, 3).reshape(-1, P, kk * w.shape[1])


def _layout(a):
    f = {k: np.asarray(v) for k, v in a.items()}
    g = {k: v[0] for k, v in f.items()}
    w = g["w_in"]
    cuts = np.cumsum([0, 512, 512, 512, 512, 4, 4, 512, 128, 128, 128, 128, 128, 128, 12])
    gq, gk, gv, gz, ga, gb, nq, kc, vc, ks, vs, kw, vw, ng = (w[:, s:e] for s, e in zip(cuts[:-1], cuts[1:]))
    w2 = g["w_in_2"]
    cut2 = np.cumsum([0, 512, 512, 1024, 1024, 512, 512, 512, 1024, 1024])
    rq, rk, rv, rg, mq, mk, mv, a2, b2 = (w2[:, s:e] for s, e in zip(cut2[:-1], cut2[1:]))
    up = _chunks(g["ffn_w_up"]).reshape(2, FC, P, TILE).transpose(1, 0, 2, 3).reshape(2 * FC, P, TILE)
    mob = _chunks(g["moba_w_branch_2"], 4).reshape(4, 2, P, 512).transpose(0, 2, 1, 3).reshape(4, P, TILE)
    tok2 = _rows(np.concatenate([rv, mv], 1), 1).reshape(4, 2, P, 3, 512).transpose(3, 0, 2, 1, 4).reshape(12, P, TILE)
    cmpw = np.stack([g["cmp_k_w1"], g["cmp_v_w1"]]).reshape(2, 4, 8, P, P).transpose(0, 1, 3, 2, 4).reshape(8, P, TILE)
    subk = g["peer_sub_keys_2"].reshape(2, 8, NKEY, P).transpose(0, 3, 1, 2).reshape(2, P, TILE)
    u = g["peer_u_2"].reshape(NKEY, NKEY, KC, P).transpose(1, 3, 2, 0).reshape(NKEY, P, TILE)
    v = g["peer_v_2"].reshape(NKEY, NKEY, D).transpose(1, 0, 2)
    ada = g["ada_w"].reshape(KC, P, 6, TILE).transpose(2, 0, 1, 3).reshape(6 * KC, P, TILE)
    c = {
        "ada1": ada[:RAW1], "ada2": ada[RAW1:], "win": _chunks(np.concatenate([gq, gk, gv, nq, ks, kw, gz, kc, vc], 1)),
        "tok": _rows(np.concatenate([vs, vw], 1), 4), "cmp": cmpw, "wout": _chunks(g["w_out"]), "up": up,
        "down": g["ffn_w_down"].reshape(FC, P, D), "in2": _chunks(np.concatenate([rq, rk, rg, mq, mk, a2, b2], 1)),
        "tok2": tok2, "retw": _chunks(g["ret_w_branch_2"]), "mobw": mob, "out2": _chunks(g["w_out_2"]),
        "pq": _chunks(g["peer_w_q_2"]), "subk": subk, "u": u, "v": v,
    }
    out = {"w_" + k: x for k, x in c.items()}
    cols = lambda x: x.reshape(-1, P).T
    every = lambda x: np.broadcast_to(x.reshape(1, -1), (P, x.size))
    convw = g["gdn_conv_w"].reshape(4, 12, P).transpose(2, 1, 0).reshape(P, 48)
    prm = [cols(g["norm1_w"]), cols(g["norm2_w"]), cols(g["mix_norm_g_2"]), cols(g["ffn_norm_g_2"]), convw,
           cols(g["gdn_out_norm_w"]), cols(g["nsa_q_norm_w"]), cols(g["nsa_k_norm_cmp"]), cols(g["nsa_k_norm_slc"]),
           cols(g["nsa_k_norm_win"]), every(g["gdn_dt_bias"]), every(g["gdn_A_log"]), np.zeros((P, 3), np.float32),
           cols(f["c"][0]), cols(g["ada_b"]), g["cmp_k_pos"].T, g["cmp_v_pos"].T]
    prm = np.concatenate(prm, 1)
    out["prm"] = np.concatenate([prm, np.zeros((P, 256 - prm.shape[1]), np.float32)], 1)
    out["xT"] = f["x"][0].T.reshape(KC, P, SEQ).transpose(1, 0, 2)
    out["wsm"] = np.concatenate([ga, gb, ng], 1).reshape(KC, P, 20).transpose(1, 0, 2)
    out["w2"] = np.stack([g["cmp_k_w2"], g["cmp_v_w2"]], 1)
    taps = np.concatenate([g["ffn_conv_w"], g["ffn_conv_b"][None]], 0)
    out["upc"] = taps.reshape(4, 2, FC, P).transpose(3, 2, 1, 0).reshape(P, 2 * FC, 4)
    gains = np.stack([np.tile(g["moba_q_gain_2"], 2), np.tile(g["moba_k_gain_2"], 2)], 1)
    out["prm2"] = np.concatenate([gains, np.zeros((P, 14), np.float32)], 1)
    out["relb"] = f["rel_bias_2"]
    return out


def kernel(**inputs):
    from concourse import bacc
    from concourse.bass_utils import run_bass_kernel_spmd

    nc = bacc.Bacc("TRN2", target_bir_lowering=False, num_devices=1)
    arrays = {k: np.ascontiguousarray(v) for k, v in {**_layout(inputs), **_constants()}.items()}
    A = {k: nc.dram_tensor("in_" + k, v.shape, mybir.dt.from_np(v.dtype), kind="ExternalInput").ap() for k, v in arrays.items()}
    A["line"] = nc.dram_tensor("bias_lines", (MH, 2 * SEQ), mybir.dt.float32).ap()
    out = nc.dram_tensor("out_x", (1, SEQ, D), mybir.dt.float32, kind="ExternalOutput").ap()
    build_program(nc, A, out)
    r = run_bass_kernel_spmd(nc, [{"in_" + k: v for k, v in arrays.items()}], core_ids=[0])
    return r.results[0]["out_x"]
```
